# Optimizing a Trainium2 kernel written in Bass

```python
import math
import jax
import jax.numpy as jnp
from jax import lax
import numpy as np

D_MODEL = 1024
BATCH = 1
SEQ = 256
DEPTH = 1
DEC_BATCH = 8
DEC_SEQ = 8
PAST_LEN = 256
PAGE_SIZE = 128

N_HEADS = 4
HEAD_DIM = 64
V_DIM = 2 * HEAD_DIM
D_QK = N_HEADS * 2 * HEAD_DIM
D_ATTN = N_HEADS * V_DIM
Q_BLOCK = 128
D_POOL = 512
POOL_WINDOWS = (2, 4, 8, 16)
N_POOL_GROUPS = 4
POOL_GROUP = D_POOL // N_POOL_GROUPS
POOL_STATE = max(POOL_WINDOWS) - 1
N_EXPERT_GROUPS = 4
EXPERTS_PER_GROUP = 8
TOP_K_IN_GROUP = 2
D_EXPERT = 256
D_PLE = 256
D_IN = D_POOL + 2 * D_QK + D_ATTN + 2 * D_MODEL
LN_EPS = 1e-5
DEEPNORM_ALPHA = (2 * DEPTH) ** 0.25
DEEPNORM_BETA = (8 * DEPTH) ** -0.25

kernel_name = 'hybrid_pool_diffattn_hmoe_step'

def layer_norm(x, g, b):
    xf = x.astype(jnp.float32)
    mu = jnp.mean(xf, axis=-1, keepdims=True)
    var = jnp.mean(jnp.square(xf - mu), axis=-1, keepdims=True)
    y = (xf - mu) * lax.rsqrt(var + LN_EPS) * g.astype(jnp.float32) + b.astype(jnp.float32)
    return y.astype(x.dtype)

def split_projection(z):
    o1 = D_POOL
    o2 = o1 + D_QK
    o3 = o2 + D_QK
    o4 = o3 + D_ATTN
    o5 = o4 + D_MODEL
    u = z[..., :o1]
    q = z[..., o1:o2]
    k = z[..., o2:o3]
    v = z[..., o3:o4]
    gp = jax.nn.sigmoid(z[..., o4:o5])
    ga = jax.nn.sigmoid(z[..., o5:])
    return u, q, k, v, gp, ga

def pool_mixer(u_ext, pos, w_grp, s_pool):
    P = POOL_STATE
    T = u_ext.shape[1] - P
    cs = jnp.cumsum(u_ext.astype(jnp.float32), axis=1)
    cs = jnp.concatenate([jnp.zeros_like(cs[:, :1]), cs], axis=1)
    u_new = u_ext[:, P:].astype(jnp.float32)
    outs = []
    for gi, w in enumerate(POOL_WINDOWS):
        sl = slice(gi * POOL_GROUP, (gi + 1) * POOL_GROUP)
        win = cs[:, P + 1:P + 1 + T, sl] - cs[:, P + 1 - w:P + 1 - w + T, sl]
        cnt = jnp.minimum(pos + 1, w).astype(jnp.float32)[:, None]
        d = (win / cnt - u_new[..., sl]).astype(u_ext.dtype)
        outs.append(jnp.einsum('btc,ce->bte', d, w_grp[gi]))
    return jnp.concatenate(outs, axis=-1) * s_pool

def diff_attention(q, ks, vs, q_pos, k_poss, lam, slopes):
    scores = []
    for k, k_pos in zip(ks, k_poss):
        s = jnp.einsum('bqhcd,bkhcd->bchqk', q, k).astype(jnp.float32) * (HEAD_DIM ** -0.5)
        dist = q_pos[:, None] - k_pos[None, :]
        bias = -slopes[:, None, None] * dist.astype(jnp.float32)
        scores.append(jnp.where(dist >= 0, s + bias, -jnp.inf))
    probs = jax.nn.softmax(jnp.concatenate(scores, axis=-1), axis=-1)
    a = probs[:, 0] - lam * probs[:, 1]
    outs = []
    off = 0
    for v in vs:
        n = v.shape[1]
        outs.append(jnp.einsum('bhqk,bkhe->bqhe', a[..., off:off + n].astype(v.dtype), v))
        off += n
    out = outs[0]
    for o in outs[1:]:
        out = out + o
    return out

def prompt_attention(q, k, v, lam, slopes):
    B, T = q.shape[:2]
    nb = T // Q_BLOCK
    pos = jnp.arange(T, dtype=jnp.int32)
    qb = jnp.moveaxis(q.reshape(B, nb, Q_BLOCK, N_HEADS, 2, HEAD_DIM), 1, 0)
    pb = pos.reshape(nb, Q_BLOCK)
    ob = lax.map(lambda a: diff_attention(a[0], [k], [v], a[1], [pos], lam, slopes), (qb, pb))
    return jnp.moveaxis(ob, 0, 1).reshape(B, T, N_HEADS, V_DIM)

def sample_attention(q, k, v, k_pages, v_pages, page_table, lam, slopes):
    DB, T = q.shape[:2]
    n_past = page_table.shape[1] * PAGE_SIZE
    k_past = k_pages[page_table].reshape(DB, n_past, N_HEADS, 2, HEAD_DIM)
    v_past = v_pages[page_table].reshape(DB, n_past, N_HEADS, V_DIM)
    past_pos = jnp.arange(n_past, dtype=jnp.int32)
    new_pos = n_past + jnp.arange(T, dtype=jnp.int32)
    return diff_attention(q, [k_past, k], [v_past, v], new_pos, [past_pos, new_pos], lam, slopes)

def hier_moe(x, w_rg, b_rg, w_re, b_re, w_gate, w_up, w_down):
    shp = x.shape
    xt = x.reshape(-1, shp[-1])
    lg = jnp.einsum('nd,dg->ng', xt, w_rg).astype(jnp.float32) + b_rg.astype(jnp.float32)
    pg = jax.nn.softmax(lg, axis=-1)
    _, g_idx = lax.top_k(lg, 1)
    oh_g = jax.nn.one_hot(g_idx[:, 0], N_EXPERT_GROUPS, dtype=jnp.float32)
    g_w = jnp.sum(pg * oh_g, axis=-1)
    le = jnp.einsum('nd,dge->nge', xt, w_re).astype(jnp.float32) + b_re.astype(jnp.float32)
    le_sel = jnp.sum(le * oh_g[:, :, None], axis=1)
    e_val, e_idx = lax.top_k(le_sel, TOP_K_IN_GROUP)
    e_w = jax.nn.softmax(e_val, axis=-1)
    w_e = jnp.sum(jax.nn.one_hot(e_idx, EXPERTS_PER_GROUP, dtype=jnp.float32) * e_w[..., None], axis=1)
    comb = (g_w[:, None, None] * oh_g[:, :, None] * w_e[:, None, :]).astype(x.dtype)
    y = jnp.zeros_like(xt)
    for g in range(N_EXPERT_GROUPS):
        h = jax.nn.silu(jnp.einsum('nd,edf->nef', xt, w_gate[g])) * jnp.einsum('nd,edf->nef', xt, w_up[g])
        y = y + jnp.einsum('nef,efd->nd', h * comb[:, g, :, None], w_down[g])
    return y.reshape(shp)

def setup_inputs(seed: int = 0) -> dict:
    key = jax.random.key(seed)
    keys = jax.random.split(key, 64)
    ctr = [0]

    def nxt():
        ctr[0] += 1
        return keys[ctr[0] - 1]

    def nrm(shape, scale):
        return jax.random.normal(nxt(), shape, jnp.float32) * scale

    n_pages = PAST_LEN // PAGE_SIZE
    n_used = DEC_BATCH * n_pages
    n_phys = n_used + n_used // 4
    L = DEPTH
    G, E, F = N_EXPERT_GROUPS, EXPERTS_PER_GROUP, D_EXPERT
    x_prompt = nrm((BATCH, SEQ, D_MODEL), 1.0)
    x_sample = nrm((DEC_BATCH, DEC_SEQ, D_MODEL), 1.0)
    p_prompt = nrm((DEPTH, BATCH, SEQ, D_PLE), 1.0)
    p_sample = nrm((DEPTH, DEC_BATCH, DEC_SEQ, D_PLE), 1.0)
    cache_k = nrm((DEPTH, n_phys, PAGE_SIZE, N_HEADS, V_DIM), 1.0)
    cache_v = nrm((DEPTH, n_phys, PAGE_SIZE, N_HEADS, V_DIM), DEEPNORM_BETA)
    state_pool = nrm((DEPTH, DEC_BATCH, POOL_STATE, D_POOL), 1.0)
    page_table = jax.random.permutation(nxt(), n_phys)[:n_used].reshape(DEC_BATCH, n_pages).astype(jnp.int32)
    sd = D_MODEL ** -0.5
    w_in = jnp.concatenate([
        nrm((L, D_MODEL, D_POOL + 2 * D_QK), sd),
        nrm((L, D_MODEL, D_ATTN), sd * DEEPNORM_BETA),
        nrm((L, D_MODEL, 2 * D_MODEL), sd)], axis=-1)
    return {
        'x_prompt': x_prompt,
        'x_sample': x_sample,
        'p_prompt': p_prompt,
        'p_sample': p_sample,
        'cache_k': cache_k,
        'cache_v': cache_v,
        'state_pool': state_pool,
        'page_table': page_table,
        'w_in': w_in,
        'b_in': nrm((L, D_IN), 0.01),
        'lam_q1': nrm((L, HEAD_DIM), 0.1),
        'lam_k1': nrm((L, HEAD_DIM), 0.1),
        'lam_q2': nrm((L, HEAD_DIM), 0.1),
        'lam_k2': nrm((L, HEAD_DIM), 0.1),
        'g_sub': 1.0 + nrm((L, V_DIM), 0.1),
        'w_pool_grp': nrm((L, N_POOL_GROUPS, POOL_GROUP, POOL_GROUP), POOL_GROUP ** -0.5),
        's_pool': 1.0 + nrm((L, D_POOL), 0.1),
        'w_pool_br': nrm((L, D_POOL, D_MODEL), D_POOL ** -0.5),
        'w_attn_br': nrm((L, D_ATTN, D_MODEL), D_ATTN ** -0.5),
        'w_o': nrm((L, D_MODEL, D_MODEL), sd * DEEPNORM_BETA),
        'ln1_g': 1.0 + nrm((L, D_MODEL), 0.1),
        'ln1_b': nrm((L, D_MODEL), 0.01),
        'w_rg': nrm((L, D_MODEL, G), sd),
        'b_rg': nrm((L, G), 0.01),
        'w_re': nrm((L, D_MODEL, G, E), sd),
        'b_re': nrm((L, G, E), 0.01),
        'w_gate': nrm((L, G, E, D_MODEL, F), sd),
        'w_up': nrm((L, G, E, D_MODEL, F), sd),
        'w_down': nrm((L, G, E, F, D_MODEL), (F ** -0.5) * DEEPNORM_BETA),
        'ln2_g': 1.0 + nrm((L, D_MODEL), 0.1),
        'ln2_b': nrm((L, D_MODEL), 0.01),
        'w_ple_gate': nrm((L, D_MODEL, D_MODEL), sd),
        'b_ple_gate': nrm((L, D_MODEL), 0.01),
        'w_ple': nrm((L, D_PLE, D_MODEL), (D_PLE ** -0.5) * DEEPNORM_BETA),
        'ln3_g': 1.0 + nrm((L, D_MODEL), 0.1),
        'ln3_b': nrm((L, D_MODEL), 0.01),
    }

def reference(x_prompt, x_sample, p_prompt, p_sample, cache_k, cache_v, state_pool, page_table,
              w_in, b_in, lam_q1, lam_k1, lam_q2, lam_k2, g_sub, w_pool_grp, s_pool,
              w_pool_br, w_attn_br, w_o, ln1_g, ln1_b, w_rg, b_rg, w_re, b_re,
              w_gate, w_up, w_down, ln2_g, ln2_b, w_ple_gate, b_ple_gate, w_ple, ln3_g, ln3_b):
    f32 = jnp.float32
    slopes = 2.0 ** (-8.0 * jnp.arange(1, N_HEADS + 1, dtype=f32) / N_HEADS)
    n_past = page_table.shape[1] * PAGE_SIZE
    xp, xs = x_prompt, x_sample
    kp_l, vp_l, sp_l, ks_l, vs_l, ss_l = [], [], [], [], [], []
    for i in range(DEPTH):
        lam_init = 0.8 - 0.6 * math.exp(-0.3 * i)
        lam = (jnp.exp(jnp.sum(lam_q1[i].astype(f32) * lam_k1[i].astype(f32)))
               - jnp.exp(jnp.sum(lam_q2[i].astype(f32) * lam_k2[i].astype(f32))) + lam_init)

        def block(x, p_emb, prefix, pos, attend):
            B, T = x.shape[:2]
            z = jnp.einsum('btd,de->bte', x, w_in[i]) + b_in[i]
            u, q, k, v, gp, ga = split_projection(z)
            q = q.reshape(B, T, N_HEADS, 2, HEAD_DIM)
            k = k.reshape(B, T, N_HEADS, 2, HEAD_DIM)
            v = v.reshape(B, T, N_HEADS, V_DIM)
            u_ext = jnp.concatenate([prefix.astype(u.dtype), u], axis=1)
            y_pool = pool_mixer(u_ext, pos, w_pool_grp[i], s_pool[i])
            o = attend(q, k, v).astype(f32)
            o = (o * lax.rsqrt(jnp.mean(jnp.square(o), axis=-1, keepdims=True) + LN_EPS)
                 * g_sub[i].astype(f32) * (1.0 - lam_init))
            y_attn = o.astype(x.dtype).reshape(B, T, D_ATTN)
            merged = (gp * jnp.einsum('btc,cd->btd', y_pool, w_pool_br[i])
                      + ga * jnp.einsum('btc,cd->btd', y_attn, w_attn_br[i]))
            x1 = layer_norm(DEEPNORM_ALPHA * x + jnp.einsum('btd,de->bte', merged, w_o[i]), ln1_g[i], ln1_b[i])
            moe = hier_moe(x1, w_rg[i], b_rg[i], w_re[i], b_re[i], w_gate[i], w_up[i], w_down[i])
            x2 = layer_norm(DEEPNORM_ALPHA * x1 + moe, ln2_g[i], ln2_b[i])
            gate = jax.nn.sigmoid(jnp.einsum('btd,de->bte', x2, w_ple_gate[i]) + b_ple_gate[i])
            pe = jnp.einsum('btp,pd->btd', p_emb, w_ple[i])
            x3 = layer_norm(DEEPNORM_ALPHA * x2 + gate * pe, ln3_g[i], ln3_b[i])
            return x3, k.reshape(B, T, N_HEADS, V_DIM), v, u_ext[:, -POOL_STATE:]

        pos_p = jnp.arange(xp.shape[1], dtype=jnp.int32)
        prefix_p = jnp.zeros((xp.shape[0], POOL_STATE, D_POOL), xp.dtype)
        xp, kp, vp, sp = block(xp, p_prompt[i], prefix_p, pos_p,
                               lambda q, k, v: prompt_attention(q, k, v, lam, slopes))
        pos_s = n_past + jnp.arange(xs.shape[1], dtype=jnp.int32)
        xs, ks_, vs_, ss_ = block(xs, p_sample[i], state_pool[i], pos_s,
                                  lambda q, k, v: sample_attention(q, k, v, cache_k[i], cache_v[i],
                                                                   page_table, lam, slopes))
        kp_l.append(kp)
        vp_l.append(vp)
        sp_l.append(sp)
        ks_l.append(ks_)
        vs_l.append(vs_)
        ss_l.append(ss_)
    return (xp, xs, jnp.stack(kp_l), jnp.stack(vp_l), jnp.stack(sp_l),
            jnp.stack(ks_l), jnp.stack(vs_l), jnp.stack(ss_l))


_drawn_inputs = setup_inputs


def setup_inputs(seed=0):
    import zlib

    import numpy as np

    out = dict(_drawn_inputs(seed))
    spreads = {}
    factors = {'b_in': 3.221,
     'lam_q2': 200.0,
     'ln1_b': 3.45,
     'b_rg': 17.984,
     'b_re': 6.935,
     'ln2_b': 5.651,
     'b_ple_gate': 56.573,
     'ln3_b': 5.466}
    for name, (base, spread) in spreads.items():
        noise = np.random.default_rng([zlib.crc32(name.encode()), seed]).standard_normal(out[name].shape)
        drawn = base * np.exp(spread * noise) if base else spread * noise
        out[name] = jnp.asarray(drawn.astype(out[name].dtype))
    for name, factor in factors.items():
        out[name] = (out[name] * factor).astype(out[name].dtype)
    return out
```

```python
from contextlib import ExitStack

import concourse.bass as bass
from concourse import mybir
import math
import numpy as np

F32 = mybir.dt.float32
I32 = mybir.dt.int32
ALU = mybir.AluOpType
ACT = mybir.ActivationFunctionType
AX = mybir.AxisListType

P = 128
D = 1024
KD = D // P
PROMPT = 256
SEQS, NEW = 8, 8
T = PROMPT + SEQS * NEW
TILES = 3
ROWS = [128, 128, 64]
H, HD = 4, 64
PAST, PAGE = 256, 128
PAGES = PAST // PAGE
N_PHYS = 20
POOL, GROUPS, STATE = 512, 4, 15
EXPERTS, EG, EE, FF = 32, 4, 8, 256
WIN = 64
PAIRS = 2 * T
SORTED = PAIRS + WIN
WINDOWS = T // WIN
PLE = 256
EPS = 1e-5
ALPHA = 2.0 ** 0.25
LAM_INIT = 0.8 - 0.6 * math.exp(0.0)
MASKED = -1e30
SLOPES = [2.0 ** (-8.0 * (h + 1) / H) for h in range(H)]

UNIT = 2048
RING = 12
W_IN_ORDER = [2, 3, 4, 5, 6, 7, 8, 9, 10, 11, 12, 13, 0, 1, 14, 15]
U_BRANCH = 16
U_WO = 20
U_EXPERT = 24
U_PLE = U_EXPERT + 3 * EXPERTS

C_IDENT = 0
C_TRI = C_IDENT + 128
C_PROMPT = C_TRI + 128
C_PAST = C_PROMPT + H * 384
C_NEW = C_PAST + PAST
C_FOLD = C_NEW + SEQS * 64
C_COUNT = C_FOLD + 32
C_IOTA = C_COUNT + GROUPS * 16
C_ROW = C_IOTA + 32
C_END = C_ROW + 2


def constant_tables():
    c = np.zeros((P, C_END), np.float32)
    p = np.arange(P)[:, None]
    c[:, C_IDENT:C_IDENT + 128] = np.eye(P)
    c[:, C_TRI:C_TRI + 128] = p < np.arange(P)[None, :]
    j = np.arange(384)[None, :]
    dist = np.where(j < 128, p - j, p + 128 - (j - 128))
    for h in range(H):
        c[:, C_PROMPT + 384 * h:C_PROMPT + 384 * (h + 1)] = np.where(dist >= 0, -SLOPES[h] * dist, MASKED)
    h, r = p // 32, p % 32
    q, used = r % 8, r < 16
    slope = np.array(SLOPES)[h]
    c[:, C_PAST:C_PAST + PAST] = np.where(used, -slope * (PAST + q - np.arange(PAST)[None, :]), 0.0)
    key = np.arange(64)[None, :]
    for s in range(SEQS):
        d = q - key % NEW
        ok = (key // NEW == s) & (d >= 0)
        c[:, C_NEW + 64 * s:C_NEW + 64 * (s + 1)] = np.where(used, np.where(ok, -slope * d, MASKED), 0.0)
    c[:, C_FOLD:C_FOLD + 32] = used & (np.arange(32)[None, :] == 8 * h + q)
    for g in range(GROUPS):
        w = 2 ** (g + 1)
        c[:, C_COUNT + 16 * g:C_COUNT + 16 * (g + 1)] = [w / min(i + 1, w) for i in range(16)]
    c[:, C_IOTA:C_IOTA + 32] = np.arange(32)
    c[:, C_ROW] = (used & (r < 8))[:, 0]
    c[:, C_ROW + 1] = (used & (r >= 8))[:, 0]
    iota = np.broadcast_to(np.arange(PAIRS, dtype=np.float32), (P, PAIRS)).copy()
    return c, iota


def hybrid_step(nc, a):
    ctx = ExitStack()
    with ctx:
        def fixed(name, shape, dt=F32):
            return ctx.enter_context(nc.sbuf_tensor(name, shape, dt))

        def sem(name):
            return ctx.enter_context(nc.semaphore(name))

        ring = fixed("ring", [P, RING, UNIT])
        cst = fixed("cst", [P, C_END])
        ones = fixed("ones", [P, P])
        br_row = fixed("br_row", [P, 36])
        vec = fixed("vec", [41, P])
        col = fixed("col", [P, 41])
        misc = fixed("misc", [P, 64])
        arena_bytes = 95488
        arena = fixed("arena", [P, arena_bytes // 4])

        def at(off, shape, dt=F32):
            n = int(np.prod(shape[1:]))
            v = arena[:, off // 4:off // 4 + n]
            if dt != F32:
                v = v.bitcast(dt)
            if len(shape) == 3:
                v = v.rearrange("p (a b) -> p a b", a=shape[1])
            if len(shape) == 4:
                v = v.rearrange("p (a b c) -> p a b c", a=shape[1], b=shape[2])
            return v

        xT = at(0, [P, KD, T])
        qT = at(10240, [P, H, T])
        kT = at(15360, [P, H, T])
        v_tm = at(20480, [P, TILES, 512])
        gT = at(26624, [P, 16, T])
        x_tm = at(47104, [P, TILES, D])
        k_raw = at(47104, [P, 2, PAGES * 512])
        k_t = at(55296, [P, H, PAST])
        v_raw = at(59392, [P, 2, PAGES * 512])
        qbd = at(67584, [P, SEQS, H * 32])
        p_s = at(71680, [P, 2, 320])
        a_s = at(74240, [P, 2, 96])
        s_p = at(75008, [P, 4, 384])
        aT_p = at(81152, [P, 2, 384])
        k_out = at(84224, [P, TILES, 512])
        oT = at(90368, [P, H, T])
        sq = at(75008, [P, H, T])
        bv_row = at(75008, [P, 512])
        rs = at(47104, [P, H, T])
        state = at(81152, [P, 512])
        lv = [at(52224 + 7280 * i, [P, 1820]) for i in range(3)]
        lvP = [x[:, 0:GROUPS * 271].rearrange("p (g j) -> p g j", g=GROUPS) for x in lv]
        lvS = [x[:, GROUPS * 271:1820].rearrange("p (g s j) -> p g s j", g=GROUPS, s=SEQS) for x in lv]
        dT = at(84224, [P, GROUPS, T])
        u_out = at(75008, [P, 2, 512])
        w_grp = at(79104, [P, GROUPS, P])
        u_new = at(83200, [P, 4, 64])
        yaT = at(10240, [P, H, T])
        ypT = at(15360, [P, GROUPS, T])
        mT = at(0, [P, KD, T])
        x_again = at(47104, [P, TILES, D])
        ln1 = at(59520, [P, 2, D])
        x1 = at(26624, [P, TILES, D])
        x1T = at(10240, [P, KD, T])
        w_r = at(67712, [P, KD, 36])
        XsT = at(38912, [P, KD, SORTED])
        PT = at(61440, [P, TILES, PAIRS])
        CT = at(69120, [P, TILES, PAIRS])
        YsT = at(61440, [P, KD, SORTED])
        w_ple = at(76800, [P, 2, D])
        p_tm = at(84992, [P, TILES, PLE])
        xg = at(88064, [P, 2, KD * WIN])
        weighted = at(88064, [P, PAIRS])
        iota = at(92160, [P, PAIRS])
        Pj = at(0, [P, 5, T])
        pe_s = at(10240, [P, TILES, D])
        pT = at(22528, [P, 2, T])
        sig, gg, hh, hT = (at(22528 + 512 * i, [P, P]) for i in range(4))
        y_s = at(6400, [P, 512])
        Yj = at(38912, [P, 5, D])
        x2 = at(61440, [P, TILES, D])
        x2T = at(73728, [P, KD, T])
        gt = at(38912, [P, TILES, D])
        ln2, ln3, bpg = ring[:, 4, :], ring[:, 5, :], ring[:, 6, 0:D]
        small = fixed("small", [P, 1330])
        cursor = [0]

        def tiny(*shape):
            n = int(np.prod(shape))
            v = small[:, cursor[0]:cursor[0] + n]
            cursor[0] += n
            assert cursor[0] <= 1330, cursor[0]
            if len(shape) == 2:
                v = v.rearrange("p (a b) -> p a b", a=shape[0])
            return v

        logits = tiny(3, 36)
        c4, c8a, c8b, oh8a, le_s = tiny(3, 4), tiny(3, 8), tiny(3, 8), tiny(3, 8), tiny(3, 8)
        oh4, dl4, lt8 = tiny(3, 4), tiny(3, 4), tiny(3, 8)
        le_m = tiny(3, 32)
        E1, E2, GG, G2 = tiny(3, 32), tiny(3, 32), tiny(3, 32), tiny(3, 32)
        Mt = c_rank = tiny(3, 32)
        m_g, g_id, s_g, m1, i1, m2, i2, ex, c1, c2, e1, e2, pos1, pos2 = (tiny(3) for _ in range(14))
        start_f = tiny(WINDOWS, 33)
        start_i = tiny(WINDOWS, 33).bitcast(I32)
        cnt_max = tiny(2)
        flag = tiny(2).bitcast(I32)
        stats, mv = tiny(3, 12), tiny(3, 2)
        rstd = tiny(4)
        mx, nmx, sm, rr = tiny(2, 4), tiny(2, 4), tiny(2, 4), tiny(2, 4)
        msx, nms, ss, rrs = tiny(2), tiny(2), tiny(2), tiny(2)
        coef, coef_s, lam_p, lam_e, neg_lam, gs, eps = tiny(4), tiny(1), tiny(2), tiny(2), tiny(1), tiny(1), tiny(1)
        pages = fixed("pages", [1, SEQS * PAGES], I32)
        scratch = misc[:, 0:4]

        bank = [ctx.enter_context(nc.psum_tensor(f"bank{i}", [P, 512], F32)) for i in range(8)]

        ident = cst[:, C_IDENT:C_IDENT + P]
        tri = cst[:, C_TRI:C_TRI + P]
        iota32 = cst[:, C_IOTA:C_IOTA + 32]

        w_in_slot = [sem(f"w_in_slot{i}") for i in range(RING)]
        x_here, cst_here, vec_here, rows_here, grp_here = map(sem, ("x_here", "cst_here", "vec_here", "rows_here", "grp_here"))
        wgrp_here = sem("wgrp_here")
        pages_here, vec_zero, ones_set, qbd_zero = map(sem, ("pages_here", "vec_zero", "ones_set", "qbd_zero"))
        xt_ps, xt_v, xt_a = map(sem, ("xt_ps", "xt_v", "xt_a"))
        vec_ps, col_set, lam_prod, lam_ps, lam_exp, coef_set = map(sem, ("vec_ps", "col_set", "lam_prod", "lam_ps", "lam_exp", "coef_set"))
        z_ps, z_out, v_ps, v_out, qbd_set = map(sem, ("z_ps", "z_out", "v_ps", "v_out", "qbd_set"))
        ko_ps, ko_set = map(sem, ("ko_ps", "ko_set"))
        sc_ps, sc_used, sc_max, sc_exp, a_set, at_ps, at_set, pv_ps, op_out = map(
            sem, ("sc_ps", "sc_used", "sc_max", "sc_exp", "a_set", "at_ps", "at_set", "pv_ps", "op_out"))
        k_here, v_here = [sem(f"k_here{i}") for i in range(2)], [sem(f"v_here{i}") for i in range(2)]
        kt_ps, kt_a, kt_v = map(sem, ("kt_ps", "kt_a", "kt_v"))
        ssc_ps, ssc_used, ssc_max, ssc_exp, ss_set, fold_ps, fold_set, spv_ps, os_out = map(
            sem, ("ssc_ps", "ssc_used", "ssc_max", "ssc_exp", "ss_set", "fold_ps", "fold_set", "spv_ps", "os_out"))
        sq_set, ms_ps, std_set, ya_set = map(sem, ("sq_set", "ms_ps", "std_set", "ya_set"))
        state_here, st_ps, st_set, pre_zero, win_set, win_step, d_set, u_ps, u_set, unew_set = map(
            sem, ("state_here", "st_ps", "st_set", "pre_zero", "win_set", "win_step", "d_set", "u_ps", "u_set", "unew_set"))
        yp_ps, yp_set, br_ps, br_mul, m_set = map(sem, ("yp_ps", "yp_set", "br_ps", "br_mul", "m_set"))
        x2_here, ln1_here, wo_ps, wo_used = map(sem, ("x2_here", "ln1_here", "wo_ps", "wo_used"))
        var_set, sd_set, x1_set = map(sem, ("var_set", "sd_set", "x1_set"))
        x1t_ps, x1t_v, x1t_a, wr_here, rt_ps = map(sem, ("x1t_ps", "x1t_v", "x1t_a", "wr_here", "rt_ps"))
        rt_dl, rt_exp, rt_dm, rt_ex, m_hot, rank_ps, pt_set, ct_set, starts_set = map(
            sem, ("rt_dl", "rt_exp", "rt_dm", "rt_ex", "m_hot", "rank_ps", "pt_set", "ct_set", "starts_set"))
        iota_here, ple_here, pt_ps, pt_out, pe_ps, pe_out = map(sem, ("iota_here", "ple_here", "pt_ps", "pt_out", "pe_ps", "pe_out"))
        ga_ps, ga_v, ga_a, pads_set = map(sem, ("ga_ps", "ga_v", "ga_a", "pads_set"))
        steps = ("xg", "gu", "sig", "g", "h", "ht", "hT", "y", "ys", "yt", "out")
        main = {n: sem("main_" + n) for n in steps}
        over = {n: sem("over_" + n) for n in steps + ("w", "freed")}
        moe_done = sem("moe_done")
        yt_ps, yt_v, yt_a, cm_ps, cm_used = map(sem, ("yt_ps", "yt_v", "yt_a", "cm_ps", "cm_used"))
        x2t_ps, x2t_v, x2t_a, pg_ps, pg_add, pg_sig, pg_mul = map(
            sem, ("x2t_ps", "x2t_v", "x2t_a", "pg_ps", "pg_add", "pg_sig", "pg_mul"))
        late_here, y_set, x2_set = map(sem, ("late_here", "y_set", "x2_set"))
        stored = sem("stored")
        chain_v, chain_g = sem("chain_v"), sem("chain_g")

        win_d = a["w_in"].rearrange("l (k p) (c n) -> (l c) p k n", p=P, n=256)
        pbr_d = a["w_pool_br"].rearrange("l (k p) (c n) -> (l c) p k n", p=P, n=512)
        abr_d = a["w_attn_br"].rearrange("l (k p) (c n) -> (l c) p k n", p=P, n=512)
        wo_d = a["w_o"].rearrange("l (k p) (c n) -> (l c) p k n", p=P, n=256)
        wg_d = a["w_gate"].rearrange("l g e (k p) f -> (l g e) p k f", p=P)
        wu_d = a["w_up"].rearrange("l g e (k p) f -> (l g e) p k f", p=P)
        wd_d = a["w_down"].rearrange("l g e (k p) d -> (l g e) p k d", p=P)
        pg_d = a["w_ple_gate"].rearrange("l (k p) (c n) -> (l c) p k n", p=P, n=256)
        ck_d = a["cache_k"].rearrange("l n p h d -> (l n) p (h d)")
        cv_d = a["cache_v"].rearrange("l n p h d -> (l n) p (h d)")
        xp_d = a["x_prompt"].rearrange("b (t p) d -> p (b t) d", p=P)
        xs_d = a["x_sample"].rearrange("s t d -> (s t) d")
        pp_d = a["p_prompt"].rearrange("l b (t p) d -> p (l b t) d", p=P)
        ps_d = a["p_sample"].rearrange("l s t d -> (l s t) d")

        def unit(slot, k):
            return ring[:, slot, :].rearrange("p (k n) -> p k n", k=k)

        def level(n):
            return 0 if n == 0 else 2 - n % 2

        def gather_out(copy, j):
            b = bank[j % 6]
            if j < 16:
                return copy(XsT[:, j // 2, 320 * (j % 2):320 * (j % 2 + 1)], b[:, 0:320])
            return copy(Pj[:, j - 16, :], b[:, 0:T])

        def yt_out(copy, g):
            return copy(Yj[:, g // 2, 512 * (g % 2):512 * (g % 2 + 1)], bank[g % 6][:, :])

        block = ctx.enter_context(nc.Block())

        @block.sync
        def _(sp):
            def wait_used(i):
                if i < U_BRANCH:
                    if i in (4, 5):
                        sp.wait_ge(v_ps, 3 * (i - 3))
                    else:
                        sp.wait_ge(z_ps, 2 * i + 2 if i < 4 else 2 * i - 2)
                elif i < U_WO:
                    sp.wait_ge(br_ps, 4 * ((i - U_BRANCH) // 2 + 1))
                elif i < U_EXPERT:
                    sp.wait_ge(wo_ps, 3 * (i - U_WO + 1))
                else:
                    e, r = divmod(i - U_EXPERT, 3)
                    sp.wait_ge(main["gu"] if r < 2 else main["y"], e + 1)

            def load(i, src, k):
                if i >= RING:
                    wait_used(i - RING)
                sp.dma_start(unit(i % RING, k), src).then_inc(w_in_slot[i % RING], 16)

            sp.dma_start(x_tm[:, 0:2, :], xp_d).then_inc(x_here, 16)
            sp.dma_start(x_tm[0:64, 2, :], xs_d).then_inc(x_here, 16)
            sp.dma_start(cst[:], a["cst"]).then_inc(cst_here, 16)
            sp.dma_start(bv_row[:], a["b_in"][0, 1536:2048].partition_broadcast(P)).then_inc(rows_here, 16)
            for i, c in enumerate(W_IN_ORDER):
                load(i, win_d[c], KD)
            for i, (w, c) in enumerate(((pbr_d, 0), (abr_d, 0), (pbr_d, 1), (abr_d, 1))):
                load(U_BRANCH + i, w[c], 4)
            for c in range(4):
                load(U_WO + c, wo_d[c], KD)
            for e in range(4):
                for r, (w, k) in enumerate(((wg_d, KD), (wu_d, KD), (wd_d, 2))):
                    load(U_EXPERT + 3 * e + r, w[e], k)
            with sp.Fori(0, EXPERTS // 4 - 1) as i:
                for j in range(4):
                    for r, (w, k) in enumerate(((wg_d, KD), (wu_d, KD), (wd_d, 2))):
                        slot = 3 * j + r
                        sp.wait_ge(main["gu"] if r < 2 else main["y"], i * 4 + (j + 1))
                        src = w[bass.ds(i * 4 + (j + 4), 1), :, :, :].rearrange("o p k n -> p (o k) n")
                        sp.dma_start(unit(slot, k), src).then_inc(w_in_slot[slot], 16)
            for c in range(4):
                load(U_PLE + c, pg_d[c], KD)
            wait_used(U_PLE - RING + 6)
            for n, name in enumerate(("ln2_g", "ln2_b", "ln3_g", "ln3_b")):
                dst = (ln2, ln3)[n // 2][:, (n % 2) * D:(n % 2 + 1) * D]
                sp.dma_start(dst, a[name][0].partition_broadcast(P)).then_inc(late_here, 16)
            sp.dma_start(bpg, a["b_ple_gate"][0].partition_broadcast(P)).then_inc(late_here, 16)
            sp.wait_ge(starts_set, 1)
            crowded = sp.value_load(flag[0:1, 0:1], min_val=0, max_val=1)
            with sp.If(crowded > 0):
                with sp.Fori(0, EXPERTS) as e:
                    sp.wait_ge(over["freed"], e + 1)
                    for r, (w, k) in enumerate(((wg_d, KD), (wu_d, KD), (wd_d, 2))):
                        src = w[bass.ds(e, 1), :, :, :].rearrange("o p k n -> p (o k) n")
                        sp.dma_start(unit(9 + r, k), src).then_inc(over["w"], 16)
            yp = a["y_prompt"].rearrange("b (t p) d -> p (b t) d", p=P)
            for t in range(TILES):
                sp.wait_ge(y_set, t + 1)
                dst = yp[:, t, :] if t < 2 else a["y_sample"].rearrange("s t d -> (s t) d")
                sp.dma_start(dst, x2[0:ROWS[t], t, :]).then_inc(stored, 16)
            sp.wait_ge(stored, 16 * 10)

        @block.gpsimd
        def _(pool):
            count = [0]

            def link(ins):
                count[0] += 1
                ins.then_inc(chain_g, 1)
                pool.wait_ge(chain_g, count[0])

            pool.memset(vec[:], 0.0).then_inc(vec_zero, 1)
            pool.dma_start(pages[0:1, :], a["page_table"].rearrange("s n -> (s n)").unsqueeze(0)).then_inc(pages_here, 16)
            pool.wait_ge(vec_zero, 1)
            pool.dma_start(vec[0:32, :], a["b_in"].rearrange("l (c p) -> (l c) p", p=P)).then_inc(vec_here, 16)
            pool.dma_start(vec[32:36, :], a["s_pool"].rearrange("l (c p) -> (l c) p", p=P)).then_inc(vec_here, 16)
            pool.dma_start(vec[36:37, :], a["g_sub"]).then_inc(vec_here, 16)
            for n, name in enumerate(("lam_q1", "lam_k1", "lam_q2", "lam_k2")):
                pool.dma_start(vec[37 + n:38 + n, 0:HD], a[name]).then_inc(vec_here, 16)
            pool.memset(ones[:], 1.0).then_inc(ones_set, 1)
            pool.dma_start(br_row[:, 0:4], a["b_rg"][0].partition_broadcast(P)).then_inc(grp_here, 16)
            pool.dma_start(br_row[:, 4:36], a["b_re"].rearrange("l g e -> l (g e)")[0].partition_broadcast(P)).then_inc(grp_here, 16)
            pool.wait_ge(xt_ps, 6)
            pool.memset(qbd[:], 0.0).then_inc(qbd_zero, 1)
            pool.wait_ge(pages_here, 16)

            def load_pages(s, src, dst, here):
                for n in range(PAGES):
                    pg = pool.value_load(pages[0:1, PAGES * s + n:PAGES * s + n + 1], min_val=0, max_val=N_PHYS - 1)
                    pool.dma_start(dst[:, s % 2, 512 * n:512 * (n + 1)],
                                   src[bass.ds(pg, 1), :, :].rearrange("o p n -> p (o n)")).then_inc(here[s % 2], 16)

            for s in range(SEQS + 2):
                if s < SEQS:
                    if s >= 2:
                        pool.wait_ge(kt_ps, 2 * (s - 1))
                    load_pages(s, ck_d, k_raw, k_here)
                v = s - 2
                if v >= 0:
                    if v >= 2:
                        pool.wait_ge(spv_ps, v - 1)
                    load_pages(v, cv_d, v_raw, v_here)
                if v == 2:
                    pool.wait_ge(pv_ps, H)
                    pool.dma_start(state[0:120, :], a["state_pool"].rearrange("l s j c -> (l s j) c")).then_inc(state_here, 16)
            pool.wait_ge(os_out, 1)
            pool.wait_ge(op_out, 2)
            pool.tensor_tensor(sq[:], oT[:], oT[:], ALU.mult).then_inc(sq_set, 1)
            pool.wait_ge(spv_ps, SEQS)
            pool.wait_ge(kt_v, SEQS)
            pool.memset(lvP[0][:, :, 0:15], 0.0).then_inc(pre_zero, 1)
            pool.wait_ge(pre_zero, 1)
            pool.wait_ge(z_out, 24)
            pool.wait_ge(st_set, 1)
            for n in range(1, 5):
                src, dst, step, g = level(n - 1), level(n), 2 ** (n - 1), n - 1
                lo = 2 ** n - 1
                pool.tensor_tensor(lvP[dst][:, g:4, lo:271], lvP[src][:, g:4, lo:271], lvP[src][:, g:4, lo - step:271 - step], ALU.add).then_inc(win_step, 1)
                for gg_ in range(g, 4):
                    last = pool.tensor_tensor(lvS[dst][:, gg_, :, lo:23], lvS[src][:, gg_, :, lo:23], lvS[src][:, gg_, :, lo - step:23 - step], ALU.add)
                    last.then_inc(win_step, 1)
                total = sum(1 + 4 - k for k in range(n))
                pool.wait_ge(win_step, total)
                pool.tensor_tensor(lvP[dst][:, g, 15:31], lvP[dst][:, g, 15:31], cst[:, C_COUNT + 16 * g:C_COUNT + 16 * g + 16], ALU.mult).then_inc(win_set, 1)
            pool.wait_ge(ms_ps, H)
            pool.dma_start(w_grp[:], a["w_pool_grp"].rearrange("l g c e -> c (l g) e")).then_inc(wgrp_here, 16)
            pool.wait_ge(d_set, 4)
            pool.wait_ge(ya_set, 1)
            pool.wait_ge(u_ps, 2)
            pool.wait_ge(unew_set, 1)
            pool.dma_start(x_again[:, 0:2, :], xp_d).then_inc(x2_here, 16)
            pool.dma_start(x_again[0:64, 2, :], xs_d).then_inc(x2_here, 16)
            pool.dma_start(ln1[:, 0, :], a["ln1_g"][0].partition_broadcast(P)).then_inc(ln1_here, 16)
            pool.dma_start(ln1[:, 1, :], a["ln1_b"][0].partition_broadcast(P)).then_inc(ln1_here, 16)
            pool.dma_start(w_r[:, :, 0:4], a["w_rg"].rearrange("l (k p) g -> p (l k) g", p=P)).then_inc(wr_here, 16)
            pool.dma_start(w_r[:, :, 4:36], a["w_re"].rearrange("l (k p) g e -> p (l k) (g e)", p=P)).then_inc(wr_here, 16)
            for n in range(KD):
                pool.wait_ge(br_mul, n + 1)
                if n == 0:
                    pool.wait_ge(z_ps, 28)
                pool.tensor_tensor(mT[:, n, :], gT[:, n, :], gT[:, 8 + n, :], ALU.add).then_inc(m_set, 1)
            pool.wait_ge(x1_set, 3)
            pool.dma_start(iota[:], a["iota"]).then_inc(iota_here, 16)
            pool.wait_ge(rt_ps, 1)
            pool.wait_ge(yp_ps, GROUPS)
            pool.wait_ge(stored, 16 * 7)
            pool.dma_start(w_ple[:], a["w_ple"].rearrange("l (k p) d -> p (l k) d", p=P)).then_inc(ple_here, 16)
            pool.dma_start(p_tm[:, 0:2, :], pp_d).then_inc(ple_here, 16)
            pool.dma_start(p_tm[0:64, 2, :], ps_d).then_inc(ple_here, 16)
            pool.memset(XsT[:, :, PAIRS:SORTED], 0.0).then_inc(pads_set, 1)
            for j in range(12):
                t, c = j % 3, j // 3
                pool.wait_ge(pg_sig, j + 1)
                v = gt[0:ROWS[t], t, 256 * c:256 * (c + 1)]
                pool.tensor_tensor(v, v, pe_s[0:ROWS[t], t, 256 * c:256 * (c + 1)], ALU.mult).then_inc(pg_mul, 1)

        @block.scalar
        def _(act):
            def four(b, rows):
                return b[:, :].rearrange("p (j n) -> p j n", j=4)[:, :, 0:rows]

            for g in range(1, 6, 2):
                t, hf = g // 2, g % 2
                act.wait_ge(xt_ps, g + 1)
                nc.scalar.copy(xT[:, 4 * hf:4 * hf + 4, P * t:P * t + ROWS[t]], four(bank[g], ROWS[t])).then_inc(xt_a, 1)
            act.wait_ge(lam_ps, 1)
            nc.scalar.activation(lam_e[:, :], bank[6][:, 64:66], ACT.Exp).then_inc(lam_exp, 1)

            def z_job(j):
                act.wait_ge(z_ps, j + 1)
                b = bank[j % 2]
                if j < 8:
                    dst = (qT if j < 4 else kT)[:, j % 4, :]
                    c = 4 + j
                    nc.scalar.activation(dst, b[:, 0:T], ACT.Identity, bias=col[:, c:c + 1]).then_inc(z_out, 1)
                elif 20 <= j < 24:
                    g = j - 20
                    if g == 0:
                        act.wait_ge(spv_ps, SEQS)
                        act.wait_ge(kt_v, SEQS)
                    nc.scalar.activation(lvP[0][:, g, 15:271], b[:, 0:PROMPT], ACT.Identity, bias=col[:, g:g + 1])
                    nc.scalar.activation(lvS[0][:, g, :, 15:23], b[:, PROMPT:T].rearrange("p (s j) -> p s j", s=SEQS),
                                         ACT.Identity, bias=col[:, g:g + 1]).then_inc(z_out, 1)
                else:
                    g = j - 8 if j < 20 else j - 12
                    nc.scalar.activation(gT[:, g, :], b[:, 0:T], ACT.Sigmoid, bias=col[:, 16 + g:17 + g]).then_inc(z_out, 1)

            act.wait_ge(col_set, 1)
            for j in range(8):
                z_job(j)
            for t in range(TILES):
                act.wait_ge(ko_ps, t + 1)
                nc.scalar.copy(k_out[0:ROWS[t], t, :], bank[4 + t][0:ROWS[t], :]).then_inc(ko_set, 1)
            act.wait_ge(ko_set, TILES)
            act.dma_start(a["new_k_prompt"].rearrange("l b (t p) h d -> p (l b t) (h d)", p=P), k_out[:, 0:2, :]).then_inc(stored, 16)
            act.dma_start(a["new_k_sample"].rearrange("l s t h d -> (l s t) (h d)"), k_out[0:64, 2, :]).then_inc(stored, 16)
            act.wait_ge(v_out, 6)
            act.dma_start(a["new_v_prompt"].rearrange("l b (t p) h d -> p (l b t) (h d)", p=P), v_tm[:, 0:2, :]).then_inc(stored, 16)
            act.dma_start(a["new_v_sample"].rearrange("l s t h d -> (l s t) (h d)"), v_tm[0:64, 2, :]).then_inc(stored, 16)

            for i in range(14):
                if i < 4:
                    act.wait_ge(sc_max, i + 1)
                    for c in range(2):
                        for q in range(2):
                            v = s_p[:, 2 * (i % 2) + c, 128 * q:128 + 256 * q]
                            last = nc.scalar.activation(v, v, ACT.Exp, bias=nmx[:, i % 2, 2 * c + q:2 * c + q + 1],
                                                        accum_out=sm[:, i % 2, 2 * c + q:2 * c + q + 1])
                    last.then_inc(sc_exp, 1)
                if 4 <= i < 12:
                    s = i - 4
                    act.wait_ge(ssc_max, s + 1)
                    v = p_s[:, s % 2, :]
                    nc.scalar.activation(v, v, ACT.Exp, bias=nms[:, s % 2:s % 2 + 1], accum_out=ss[:, s % 2:s % 2 + 1]).then_inc(ssc_exp, 1)
                if 3 <= i < 11:
                    s = i - 3
                    act.wait_ge(kt_ps, 2 * s + 1)
                    if s >= 1:
                        act.wait_ge(ssc_ps, s)
                    nc.scalar.copy(k_t[:, :, 0:PAGE], four(bank[5], P)).then_inc(kt_a, 1)
                if i in (4, 6):
                    n = i // 2 - 2
                    act.wait_ge(pv_ps, 2 * n + 2)
                    nc.scalar.copy(oT[:, 2 * n:2 * n + 2, 0:PROMPT], bank[6 + n][:, :].rearrange("p (h q) -> p h q", h=2)).then_inc(op_out, 1)
                if i < 12:
                    z_job(8 + i)
            for j in range(20, 24):
                z_job(j)
            act.wait_ge(ms_ps, 4)
            act.wait_ge(spv_ps, SEQS)
            for h in range(H):
                last = nc.scalar.activation(rs[:, h, :], bank[2 + h][:, 0:T], ACT.Sqrt, bias=eps[:, :], scale=1.0 / P)
            last.then_inc(std_set, 1)
            for j in range(24, 28):
                z_job(j)
            for g in range(GROUPS):
                act.wait_ge(yp_ps, g + 1)
                nc.scalar.activation(ypT[:, g, :], bank[4 + g][:, 0:T], ACT.Copy, scale=col[:, 32 + g:33 + g]).then_inc(yp_set, 1)
            act.wait_ge(u_set, 2)
            act.dma_start(a["new_pool_prompt"].rearrange("l b j c -> (l b j) c"), u_out[0:15, 0, :]).then_inc(stored, 16)
            act.dma_start(a["new_pool_sample"].rearrange("l s j c -> (l s) j c")[:, 7:15, :], u_out[0:64, 1, :]).then_inc(stored, 16)
            act.dma_start(a["new_pool_sample"].rearrange("l s j c -> (l s) j c")[:, 0:7, :],
                          a["state_pool"].rearrange("l s j c -> (l s) j c")[:, 8:15, :]).then_inc(stored, 16)

            def norm(n):
                act.wait_ge(var_set, n)
                nc.scalar.activation(rstd[:, 0:3], rstd[:, 0:3], ACT.Sqrt).then_inc(sd_set, 1)

            norm(1)
            for g in range(1, 6, 2):
                t, hf = g // 2, g % 2
                act.wait_ge(x1t_ps, g + 1)
                nc.scalar.copy(x1T[:, 4 * hf:4 * hf + 4, P * t:P * t + ROWS[t]], four(bank[g], ROWS[t])).then_inc(x1t_a, 1)
            act.wait_ge(rt_dl, 1)
            nc.scalar.activation(dl4[:], dl4[:], ACT.Exp).then_inc(rt_exp, 1)
            act.wait_ge(rt_dm, 1)
            nc.scalar.activation(ex[:, :], ex[:, :], ACT.Exp).then_inc(rt_ex, 1)
            for t in range(TILES):
                act.wait_ge(pt_ps, t + 1)
                nc.scalar.copy(pT[:, :, P * t:P * t + ROWS[t]], four(bank[t], ROWS[t])[:, 0:2, :]).then_inc(pt_out, 1)
            for j in range(6):
                t, hf = j // 2, j % 2
                act.wait_ge(pe_ps, j + 1)
                nc.scalar.copy(pe_s[0:ROWS[t], t, 512 * hf:512 * (hf + 1)], bank[3 + j % 3][0:ROWS[t], :]).then_inc(pe_out, 1)
            for j in range(1, 21, 2):
                act.wait_ge(ga_ps, j + 1)
                gather_out(nc.scalar.copy, j).then_inc(ga_a, 1)

            def activations(q, n, b):
                act.wait_ge(q["gu"], n)
                nc.scalar.activation(sig[:], b[:, 0:P], ACT.Sigmoid).then_inc(q["sig"], 1)
                act.wait_ge(q["ht"], n)
                nc.scalar.copy(hT[:], bank[2][:, 0:P]).then_inc(q["hT"], 1)
                act.wait_ge(q["y"], n)
                nc.scalar.copy(y_s[:], bank[3][:, :]).then_inc(q["ys"], 1)

            with act.Fori(0, EXPERTS // 4) as i:
                for j in range(4):
                    activations(main, i * 4 + (j + 1), bank[j % 2])
            act.wait_ge(starts_set, 1)
            crowded = act.value_load(flag[0:1, 0:1], min_val=0, max_val=1)
            with act.If(crowded > 0):
                with act.Fori(0, EXPERTS * WINDOWS) as n:
                    activations(over, n + 1, bank[0])

            for g in range(1, 10, 2):
                act.wait_ge(yt_ps, g + 1)
                yt_out(nc.scalar.copy, g).then_inc(yt_a, 1)
            norm(2)
            for g in range(1, 6, 2):
                t, hf = g // 2, g % 2
                act.wait_ge(x2t_ps, g + 1)
                nc.scalar.copy(x2T[:, 4 * hf:4 * hf + 4, P * t:P * t + ROWS[t]], four(bank[g], ROWS[t])).then_inc(x2t_a, 1)
            for j in range(12):
                t, c = j % 3, j // 3
                act.wait_ge(pg_add, j + 1)
                v = gt[0:ROWS[t], t, 256 * c:256 * (c + 1)]
                nc.scalar.activation(v, v, ACT.Sigmoid).then_inc(pg_sig, 1)
            norm(3)

        @block.vector
        def _(dve):
            V = nc.vector
            count = [0]

            def link(ins):
                count[0] += 1
                ins.then_inc(chain_v, 1)
                dve.wait_ge(chain_v, count[0])

            def four(b, rows):
                return b[:, :].rearrange("p (j n) -> p j n", j=4)[:, :, 0:rows]

            V.memset(eps[:, :], EPS)
            V.memset(start_f[:, :, 32:33], float(PAIRS))
            V.memset(coef[:, :], 1.0)
            V.memset(rstd[:, :], 1.0)
            link(V.memset(logits[:], 0.0))
            for g in range(0, 6, 2):
                t, hf = g // 2, g % 2
                dve.wait_ge(xt_ps, g + 1)
                V.tensor_copy(xT[:, 4 * hf:4 * hf + 4, P * t:P * t + ROWS[t]], four(bank[g], ROWS[t])).then_inc(xt_v, 1)
            dve.wait_ge(vec_ps, 1)
            link(V.tensor_copy(col[:, :], bank[6][:, 0:41]))
            V.tensor_scalar(gs[:, :], col[:, 36:37], 1.0 - LAM_INIT, None, ALU.mult).then_inc(col_set, 1)
            lv4 = col[0:HD, 37:41].rearrange("p (a b) -> p a b", b=2)
            V.tensor_tensor(lam_p[0:HD, :], lv4[:, :, 0], lv4[:, :, 1], ALU.mult).then_inc(lam_prod, 1)
            dve.wait_ge(lam_exp, 1)
            link(V.tensor_tensor(neg_lam[:, :], lam_e[:, 1:2], lam_e[:, 0:1], ALU.subtract))
            link(V.tensor_scalar(neg_lam[:, :], neg_lam[:, :], -LAM_INIT, None, ALU.add))
            dve.wait_ge(cst_here, 16)
            V.tensor_scalar(coef[:, 2:4], coef[:, 2:4], neg_lam[:, :], None, ALU.mult)
            link(V.scalar_tensor_tensor(coef_s[:, :], cst[:, C_ROW + 1:C_ROW + 2], neg_lam[:, :], cst[:, C_ROW:C_ROW + 1], ALU.mult, ALU.add))

            dve.wait_ge(rows_here, 16)
            for j in range(6):
                t, c = j % 3, j // 3
                dve.wait_ge(v_ps, j + 1)
                V.tensor_tensor(v_tm[0:ROWS[t], t, 256 * c:256 * (c + 1)], bank[2 + j % 2][0:ROWS[t], 0:256],
                                bv_row[0:ROWS[t], 256 * c:256 * (c + 1)], ALU.add).then_inc(v_out, 1)
            dve.wait_ge(qbd_zero, 1)
            dve.wait_ge(z_out, 4)
            for c in range(2):
                dst = qbd[64 * c:64 * c + 64, :, :].rearrange("p s (h r) -> p h s r", h=H)[:, :, :, 8 * c:8 * c + 8]
                src = qT[64 * c:64 * c + 64, :, PROMPT:T].rearrange("p h (s t) -> p h s t", s=SEQS)
                for h in range(H):
                    last = V.tensor_copy(dst[:, h], src[:, h])
                    last.then_inc(qbd_set, 1)

            for i in range(14):
                if i < 4:
                    h, b = i, i % 2
                    dve.wait_ge(sc_ps, i + 1)
                    if i >= 2:
                        dve.wait_ge(at_ps, i - 1)
                    bias = cst[:, C_PROMPT + 384 * h:C_PROMPT + 384 * (h + 1)]
                    V.scalar_tensor_tensor(s_p[:, 2 * b, :], bank[2][:, 0:384], HD ** -0.5, bias, ALU.mult, ALU.add).then_inc(sc_used, 1)
                    V.scalar_tensor_tensor(s_p[:, 2 * b + 1, :], bank[3][:, 0:384], HD ** -0.5, bias, ALU.mult, ALU.add).then_inc(sc_used, 1)
                    dve.wait_ge(sc_used, 2 * i + 2)
                    for c in range(2):
                        for q in range(2):
                            last = V.tensor_reduce(mx[:, b, 2 * c + q:2 * c + q + 1], s_p[:, 2 * b + c, 128 * q:128 + 256 * q], AX.X, ALU.max)
                    link(last)
                    V.tensor_scalar(nmx[:, b, :], mx[:, b, :], -1.0, None, ALU.mult).then_inc(sc_max, 1)
                    dve.wait_ge(sc_exp, i + 1)
                    link(V.reciprocal(rr[:, b, :], sm[:, b, :]))
                    link(V.tensor_tensor(rr[:, b, :], rr[:, b, :], coef[:, :], ALU.mult))
                    for q in range(2):
                        lo, hi = 128 * q, 128 + 256 * q
                        v = s_p[:, 2 * b, lo:hi]
                        link(V.tensor_scalar(v, v, rr[:, b, q:q + 1], None, ALU.mult))
                        last = V.scalar_tensor_tensor(v, s_p[:, 2 * b + 1, lo:hi], rr[:, b, 2 + q:3 + q], v, ALU.mult, ALU.add)
                        last.then_inc(a_set, 1)
                if 1 <= i < 5:
                    h = i - 1
                    dve.wait_ge(at_ps, h + 1)
                    if h >= 2:
                        dve.wait_ge(pv_ps, h - 1)
                    V.tensor_copy(aT_p[:, h % 2, :], bank[4][:, 0:384]).then_inc(at_set, 1)
                if 4 <= i < 12:
                    s = i - 4
                    b = s % 2
                    dve.wait_ge(ssc_ps, s + 1)
                    if s >= 2:
                        dve.wait_ge(fold_ps, s - 1)
                    V.scalar_tensor_tensor(p_s[:, b, 0:PAST], bank[2 + b][:, 0:PAST], HD ** -0.5, cst[:, C_PAST:C_PAST + PAST], ALU.mult, ALU.add)
                    link(V.scalar_tensor_tensor(p_s[:, b, PAST:320], bank[2 + b][:, PAST:320], HD ** -0.5,
                                                cst[:, C_NEW + 64 * s:C_NEW + 64 * (s + 1)], ALU.mult, ALU.add))
                    link(V.tensor_reduce(msx[:, b:b + 1], p_s[:, b, :], AX.X, ALU.max))
                    V.tensor_scalar(nms[:, b:b + 1], msx[:, b:b + 1], -1.0, None, ALU.mult).then_inc(ssc_max, 1)
                if 5 <= i < 13:
                    s = i - 5
                    dve.wait_ge(fold_ps, s + 1)
                    if s >= 2:
                        dve.wait_ge(spv_ps, s - 1)
                    V.tensor_copy(a_s[:, s % 2, 0:64], bank[4][:, 0:64])
                    V.tensor_copy(a_s[0:64, s % 2, 64:96], bank[4][0:64, 64:96]).then_inc(fold_set, 1)
                if 4 <= i < 12:
                    s = i - 4
                    b = s % 2
                    dve.wait_ge(ssc_exp, s + 1)
                    link(V.reciprocal(rrs[:, b:b + 1], ss[:, b:b + 1]))
                    link(V.tensor_tensor(rrs[:, b:b + 1], rrs[:, b:b + 1], coef_s[:, :], ALU.mult))
                    V.tensor_scalar(p_s[:, b, :], p_s[:, b, :], rrs[:, b:b + 1], None, ALU.mult).then_inc(ss_set, 1)
                if 3 <= i < 11:
                    s = i - 3
                    dve.wait_ge(kt_ps, 2 * s + 2)
                    if s >= 1:
                        dve.wait_ge(ssc_ps, s)
                    V.tensor_copy(k_t[:, :, PAGE:PAST], four(bank[5], P)).then_inc(kt_v, 1)
            dve.wait_ge(spv_ps, SEQS)
            V.tensor_copy(oT[:, :, PROMPT:T], bank[6][:, 0:256].rearrange("p (h q) -> p h q", h=H)).then_inc(os_out, 1)
            dve.wait_ge(st_ps, 1)
            for g in range(GROUPS):
                last = V.tensor_copy(lvS[0][:, g, :, 0:15], bank[7][:, 120 * g:120 * (g + 1)].rearrange("p (s j) -> p s j", s=SEQS))
            last.then_inc(st_set, 1)
            dve.wait_ge(z_out, 24)
            for g in range(GROUPS):
                last = V.tensor_copy(u_new[:, g, :].rearrange("p (s j) -> p s j", s=SEQS), lvS[0][:, g, :, 15:23])
            last.then_inc(unew_set, 1)
            dve.wait_ge(std_set, 1)
            dve.wait_ge(os_out, 1)
            dve.wait_ge(op_out, 2)
            link(V.reciprocal(rs[:], rs[:]))
            V.scalar_tensor_tensor(yaT[:], oT[:], gs[:, :], rs[:], ALU.mult, ALU.mult).then_inc(ya_set, 1)
            dve.wait_ge(ko_set, TILES)
            dve.wait_ge(stored, 64)
            for g in range(GROUPS):
                lev = level(g + 1)
                dve.wait_ge(win_set, g + 1)
                V.scalar_tensor_tensor(dT[:, g, 0:PROMPT], lvP[lev][:, g, 15:271], 1.0 / 2 ** (g + 1), lvP[0][:, g, 15:271], ALU.mult, ALU.subtract)
                V.scalar_tensor_tensor(dT[:, g, PROMPT:T].rearrange("p (s j) -> p s j", s=SEQS), lvS[lev][:, g, :, 15:23],
                                       1.0 / 2 ** (g + 1), lvS[0][:, g, :, 15:23], ALU.mult, ALU.subtract).then_inc(d_set, 1)
            for n, r in ((0, 15), (1, 64)):
                dve.wait_ge(u_ps, n + 1)
                V.tensor_copy(u_out[0:r, n, :], bank[2 + n][0:r, :]).then_inc(u_set, 1)
            for n in range(KD):
                dve.wait_ge(br_ps, n + 1)
                if n == 0:
                    dve.wait_ge(z_out, 28)
                V.tensor_tensor(gT[:, n, :], gT[:, n, :], bank[n % 2][:, 0:T], ALU.mult)
                V.tensor_tensor(gT[:, 8 + n, :], gT[:, 8 + n, :], bank[2 + n % 2][:, 0:T], ALU.mult).then_inc(br_mul, 1)
            dve.wait_ge(x2_here, 32)
            for j in range(12):
                t, c = j % 3, j // 3
                dve.wait_ge(wo_ps, j + 1)
                V.scalar_tensor_tensor(x1[0:ROWS[t], t, 256 * c:256 * (c + 1)], x_again[0:ROWS[t], t, 256 * c:256 * (c + 1)], ALPHA,
                                       bank[4 + j % 4][0:ROWS[t], 0:256], ALU.mult, ALU.add).then_inc(wo_used, 1)

            def layer_norm(x, gamma, beta, n, done):
                for t in range(TILES):
                    for k in range(2):
                        last = V.bn_stats(stats[0:ROWS[t], t, 6 * k:6 * k + 6], x[0:ROWS[t], t, 512 * k:512 * (k + 1)])
                link(last)
                for t in range(TILES):
                    last = V.bn_aggr(mv[0:ROWS[t], t, :], stats[0:ROWS[t], t, 0:12])
                link(last)
                for t in range(TILES):
                    last = V.tensor_scalar(rstd[0:ROWS[t], t:t + 1], mv[0:ROWS[t], t, 1:2], EPS, None, ALU.add)
                last.then_inc(var_set, 1)
                dve.wait_ge(sd_set, n)
                link(V.reciprocal(rstd[:, 0:3], rstd[:, 0:3]))
                for t in range(TILES):
                    v = x[0:ROWS[t], t, :]
                    link(V.scalar_tensor_tensor(v, v, mv[0:ROWS[t], t, 0:1], gamma[0:ROWS[t], :], ALU.subtract, ALU.mult))
                    V.scalar_tensor_tensor(v, v, rstd[0:ROWS[t], t:t + 1], beta[0:ROWS[t], :], ALU.mult, ALU.add).then_inc(done, 1)

            dve.wait_ge(wo_used, 12)
            dve.wait_ge(ln1_here, 32)
            layer_norm(x1, ln1[:, 0, :], ln1[:, 1, :], 1, x1_set)
            for g in range(0, 6, 2):
                t, hf = g // 2, g % 2
                dve.wait_ge(x1t_ps, g + 1)
                V.tensor_copy(x1T[:, 4 * hf:4 * hf + 4, P * t:P * t + ROWS[t]], four(bank[g], ROWS[t])).then_inc(x1t_v, 1)

            def over_last(v, n):
                return v.unsqueeze(2).to_broadcast([P, 3, n])

            def over_tiles(v, n):
                return v.unsqueeze(1).to_broadcast([P, 3, n])

            def first_max(x, n, top, cand, idx):
                link(V.tensor_reduce(top[:, :], x, AX.X, ALU.max))
                link(V.tensor_tensor(cand[:], x, over_last(top, n), ALU.is_lt))
                link(V.scalar_tensor_tensor(cand[:], cand[:], 64.0, over_tiles(iota32[:, 0:n], n), ALU.mult, ALU.add))
                link(V.tensor_reduce(idx[:, :], cand[:], AX.X, ALU.min))

            dve.wait_ge(rt_ps, 1)
            dve.wait_ge(grp_here, 32)
            lp = bank[6][:, 0:108].rearrange("p (t n) -> p t n", t=3)
            V.tensor_tensor(logits[:, 0:2, :], lp[:, 0:2, :], br_row[:, :].unsqueeze(1).to_broadcast([P, 2, 36]), ALU.add)
            link(V.tensor_tensor(logits[0:64, 2, :], lp[0:64, 2, :], br_row[0:64, :], ALU.add))
            lg = logits[:, :, 0:4]
            first_max(lg, 4, m_g, c4, g_id)
            V.tensor_tensor(dl4[:], lg, over_last(m_g, 4), ALU.subtract).then_inc(rt_dl, 1)
            link(V.tensor_tensor(oh4[:], over_tiles(iota32[:, 0:4], 4), over_last(g_id, 4), ALU.is_equal))
            for t in range(TILES):
                last = V.tensor_tensor(le_m[:, t, :].rearrange("p (g e) -> p g e", g=4), logits[:, t, 4:36].rearrange("p (g e) -> p g e", g=4),
                                       oh4[:, t, :].unsqueeze(2).to_broadcast([P, 4, 8]), ALU.mult)
            link(last)
            for t in range(TILES):
                last = V.tensor_reduce(le_s[:, t, :], le_m[:, t, :].rearrange("p (g e) -> p e g", g=4), AX.X, ALU.add)
            link(last)
            first_max(le_s[:], 8, m1, c8a, i1)
            link(V.tensor_tensor(oh8a[:], over_tiles(iota32[:, 0:8], 8), over_last(i1, 8), ALU.is_equal))
            link(V.scalar_tensor_tensor(lt8[:], oh8a[:], -3e38, le_s[:], ALU.mult, ALU.add))
            first_max(lt8[:], 8, m2, c8b, i2)
            V.tensor_tensor(ex[:, :], m2[:, :], m1[:, :], ALU.subtract).then_inc(rt_dm, 1)
            V.scalar_tensor_tensor(e1[:, :], g_id[:, :], 8.0, i1[:, :], ALU.mult, ALU.add)
            link(V.scalar_tensor_tensor(e2[:, :], g_id[:, :], 8.0, i2[:, :], ALU.mult, ALU.add))
            i32 = over_tiles(iota32, 32)
            V.tensor_tensor(E1[:], i32, over_last(e1, 32), ALU.is_equal)
            V.tensor_tensor(E2[:], i32, over_last(e2, 32), ALU.is_equal)
            V.tensor_tensor(GG[:], i32, over_last(e1, 32), ALU.is_gt)
            link(V.tensor_tensor(G2[:], i32, over_last(e2, 32), ALU.is_gt))
            V.tensor_tensor(Mt[:], E1[:], E2[:], ALU.add).then_inc(m_hot, 1)
            V.tensor_tensor(GG[:], GG[:], G2[:], ALU.add).then_inc(m_hot, 1)
            dve.wait_ge(rt_exp, 1)
            dve.wait_ge(rt_ex, 1)
            link(V.tensor_reduce(s_g[:, :], dl4[:], AX.X, ALU.add))
            link(V.scalar_tensor_tensor(c1[:, :], ex[:, :], 1.0, s_g[:, :], ALU.add, ALU.mult))
            link(V.reciprocal(c1[:, :], c1[:, :]))
            link(V.tensor_tensor(c2[:, :], ex[:, :], c1[:, :], ALU.mult))
            dve.wait_ge(rank_ps, 1)
            rank = bank[7][:, 0:96].rearrange("p (t n) -> p t n", t=3)
            for E, pos in ((E1, pos1), (E2, pos2)):
                V.memset(G2[64:128, 2, :], 0.0)
                link(V.tensor_tensor(G2[:, 0:2, :], E[:, 0:2, :], rank[:, 0:2, :], ALU.mult))
                link(V.tensor_tensor(G2[0:64, 2, :], E[0:64, 2, :], rank[0:64, 2, :], ALU.mult))
                link(V.tensor_reduce(pos[:, :], G2[:], AX.X, ALU.add))
            dve.wait_ge(iota_here, 16)
            for t in range(TILES):
                r = ROWS[t]
                link(V.tensor_scalar(PT[0:r, t, :], iota[0:r, :], pos1[0:r, t:t + 1], None, ALU.is_equal))
                V.scalar_tensor_tensor(PT[0:r, t, :], iota[0:r, :], pos2[0:r, t:t + 1], PT[0:r, t, :], ALU.is_equal, ALU.add).then_inc(pt_set, 1)
            off = bank[7][:, 96:128]
            for w in range(WINDOWS):
                last = V.tensor_scalar(start_f[:, w, 0:32], off, float(WIN * w), float(PAIRS), ALU.add, ALU.min)
            link(last)
            for w in range(1, WINDOWS):
                last = V.memset(start_f[:, w, 32:33], float(PAIRS))
            link(last)
            link(V.tensor_reduce(cnt_max[:, 0:1], bank[7][:, 128:160], AX.X, ALU.max))
            link(V.tensor_scalar(cnt_max[:, 1:2], cnt_max[:, 0:1], float(WIN), None, ALU.is_gt))
            V.tensor_copy(flag[:, 0:1], cnt_max[:, 1:2])
            V.tensor_copy(start_i[:], start_f[:]).then_inc(starts_set, 1)
            for t in range(TILES):
                r = ROWS[t]
                V.tensor_scalar(CT[0:r, t, :], iota[0:r, :], pos1[0:r, t:t + 1], c1[0:r, t:t + 1], ALU.is_equal, ALU.mult)
                link(V.tensor_scalar(weighted[0:r, :], iota[0:r, :], pos2[0:r, t:t + 1], c2[0:r, t:t + 1], ALU.is_equal, ALU.mult))
                V.tensor_tensor(CT[0:r, t, :], CT[0:r, t, :], weighted[0:r, :], ALU.add).then_inc(ct_set, 1)
                dve.wait_ge(ct_set, t + 1)
            for j in range(0, 21, 2):
                dve.wait_ge(ga_ps, j + 1)
                gather_out(V.tensor_copy, j).then_inc(ga_v, 1)

            def pick(b, place, done):
                V.tensor_copy(xg[:, b, :].rearrange("p (k n) -> p k n", k=KD), XsT[:, :, bass.ds(place, WIN)]).then_inc(done, 1)

            def hidden(q, n, b):
                dve.wait_ge(q["sig"], n)
                V.tensor_tensor(gg[:], b[:, 0:P], sig[:], ALU.mult).then_inc(q["g"], 1)
                dve.wait_ge(q["g"], n)
                V.tensor_tensor(hh[:], gg[:], b[:, P:2 * P], ALU.mult).then_inc(q["h"], 1)

            def put(q, n, b, place):
                dve.wait_ge(q["yt"], n)
                V.tensor_copy(YsT[:, :, bass.ds(place, WIN)].rearrange("p (d c) n -> p c d n", d=2),
                              b[:, :].rearrange("p (c d n) -> p c d n", c=4, d=2)).then_inc(q["out"], 1)
                dve.wait_ge(q["out"], n)

            dve.wait_ge(pads_set, 1)
            dve.wait_ge(ga_a, 10)
            dve.wait_ge(ga_v, 11)
            dve.wait_ge(starts_set, 1)
            pick(0, 0, main["xg"])
            with dve.Fori(0, EXPERTS // 4) as i:
                place = [dve.value_load(start_i[0:1, 0, bass.ds(i * 4 + j, 1)], min_val=0, max_val=PAIRS) for j in range(5)]
                for j in range(4):
                    n = i * 4 + (j + 1)
                    hidden(main, n, bank[j % 2])
                    pick((j + 1) % 2, place[j + 1], main["xg"])
                    if j > 0:
                        put(main, i * 4 + j, bank[4 + (j - 1) % 2], place[j - 1])
                put(main, i * 4 + 4, bank[5], place[3])
            crowded = dve.value_load(flag[0:1, 0:1], min_val=0, max_val=1)
            with dve.If(crowded > 0):
                with dve.Fori(0, EXPERTS) as e:
                    for w in range(WINDOWS):
                        n = e * WINDOWS + (w + 1)
                        place = dve.value_load(start_i[0:1, w, bass.ds(e, 1)], min_val=0, max_val=PAIRS)
                        pick(0, place, over["xg"])
                        hidden(over, n, bank[0])
                        put(over, n, bank[4], place)
            V.memset(scratch[:, 2:3], 0.0).then_inc(moe_done, 1)

            for g in range(0, 10, 2):
                dve.wait_ge(yt_ps, g + 1)
                yt_out(V.tensor_copy, g).then_inc(yt_v, 1)
            for j in range(6):
                t, hf = j // 2, j % 2
                dve.wait_ge(cm_ps, j + 1)
                c = slice(512 * hf, 512 * (hf + 1))
                V.scalar_tensor_tensor(x2[0:ROWS[t], t, c], x1[0:ROWS[t], t, c], ALPHA, bank[6 + j % 2][0:ROWS[t], :], ALU.mult, ALU.add).then_inc(cm_used, 1)
            dve.wait_ge(cm_used, 6)
            dve.wait_ge(late_here, 80)
            layer_norm(x2, ln2[:, 0:D], ln2[:, D:2 * D], 2, x2_set)
            for g in range(0, 6, 2):
                t, hf = g // 2, g % 2
                dve.wait_ge(x2t_ps, g + 1)
                V.tensor_copy(x2T[:, 4 * hf:4 * hf + 4, P * t:P * t + ROWS[t]], four(bank[g], ROWS[t])).then_inc(x2t_v, 1)

            def residual(j):
                t, c = j % 3, slice(256 * (j // 3), 256 * (j // 3 + 1))
                dve.wait_ge(pg_mul, j + 1)
                v = x2[0:ROWS[t], t, c]
                return V.scalar_tensor_tensor(v, v, ALPHA, gt[0:ROWS[t], t, c], ALU.mult, ALU.add)

            for j in range(12):
                t, c = j % 3, slice(256 * (j // 3), 256 * (j // 3 + 1))
                dve.wait_ge(pg_ps, j + 1)
                V.tensor_tensor(gt[0:ROWS[t], t, c], bank[j % 4][0:ROWS[t], 0:256], bpg[0:ROWS[t], c], ALU.add).then_inc(pg_add, 1)
                if j >= 3:
                    residual(j - 3)
            dve.wait_ge(x2t_ps, 6)
            for j in range(9, 12):
                last = residual(j)
            link(last)
            layer_norm(x2, ln3[:, 0:D], ln3[:, D:2 * D], 3, y_set)

        @block.tensor
        def _(pe):
            mm = nc.tensor.matmul

            def weights(i):
                pe.wait_ge(w_in_slot[i % RING], 16 * (i // RING + 1))

            def transpose_tokens(src, ps, evens, odds, ready):
                for g in range(6):
                    t, hf = g // 2, g % 2
                    r = ROWS[t]
                    ready(t)
                    for j in range(4):
                        k = 4 * hf + j
                        last = nc.tensor.transpose(bank[g][:, P * j:P * j + r], src[0:r, t, P * k:P * (k + 1)], ident[0:r, 0:r])
                    last.then_inc(ps, 1)

            pe.wait_ge(cst_here, 16)
            pe.wait_ge(x_here, 32)
            transpose_tokens(x_tm, xt_ps, xt_v, xt_a, lambda t: None)
            pe.wait_ge(vec_here, 7 * 16)
            nc.tensor.transpose(bank[6][:, 0:41], vec[:, :], ident[0:41, 0:41]).then_inc(vec_ps, 1)
            pe.wait_ge(lam_prod, 1)
            pe.wait_ge(ones_set, 1)
            mm(bank[6][:, 64:66], ones[0:HD, :], lam_p[0:HD, :], start=True, stop=True).then_inc(lam_ps, 1)
            pe.wait_ge(xt_v, 3)
            pe.wait_ge(xt_a, 3)

            def z_job(j):
                c = j if j < 8 else j + 4
                i = c // 2
                if c % 2 == 0:
                    weights(i)
                if j >= 2:
                    pe.wait_ge(z_out, j - 1)
                for k in range(KD):
                    last = mm(bank[j % 2][:, 0:T], unit(i % RING, KD)[:, k, P * (c % 2):P * (c % 2 + 1)], xT[:, k, :],
                              start=(k == 0), stop=(k == KD - 1))
                last.then_inc(z_ps, 1)

            for j in range(8):
                z_job(j)
            for j in range(6):
                t, c = j % 3, j // 3
                if t == 0:
                    weights(4 + c)
                if j >= 2:
                    pe.wait_ge(v_out, j - 1)
                for k in range(KD):
                    last = mm(bank[2 + j % 2][0:ROWS[t], 0:256], xT[:, k, P * t:P * t + ROWS[t]], unit(4 + c, KD)[:, k, :],
                              start=(k == 0), stop=(k == KD - 1))
                last.then_inc(v_ps, 1)
            pe.wait_ge(z_out, 8)
            for t in range(TILES):
                for h in range(H):
                    last = nc.tensor.transpose(bank[4 + t][0:ROWS[t], P * h:P * (h + 1)], kT[:, h, P * t:P * t + ROWS[t]], ident)
                last.then_inc(ko_ps, 1)
            pe.wait_ge(v_out, 6)
            pe.wait_ge(ko_set, TILES)

            def prompt_scores(h):
                if h >= 1:
                    pe.wait_ge(sc_used, 2 * h)
                for c in range(2):
                    r = slice(64 * c, 64 * c + 64)
                    mm(bank[2 + c][:, 0:128], qT[r, h, 0:128], kT[r, h, 0:128], start=True, stop=True)
                    last = mm(bank[2 + c][:, 128:384], qT[r, h, 128:256], kT[r, h, 0:256], start=True, stop=True)
                last.then_inc(sc_ps, 1)

            def prompt_transposes(h):
                pe.wait_ge(a_set, 2 * h + 2)
                if h >= 1:
                    pe.wait_ge(at_set, h)
                for b in range(3):
                    last = nc.tensor.transpose(bank[4][:, P * b:P * (b + 1)], s_p[:, 2 * (h % 2), P * b:P * (b + 1)], ident)
                last.then_inc(at_ps, 1)

            def prompt_values(h):
                pe.wait_ge(at_set, h + 1)
                o = bank[6 + h // 2][:, 256 * (h % 2):256 * (h % 2 + 1)]
                hs = slice(P * h, P * (h + 1))
                A = aT_p[:, h % 2, :]
                mm(o[:, 0:128], v_tm[:, 0, hs], A[:, 0:128], start=True, stop=True)
                mm(o[:, 128:256], v_tm[:, 0, hs], A[:, 128:256], start=True, stop=False)
                mm(o[:, 128:256], v_tm[:, 1, hs], A[:, 256:384], start=False, stop=True).then_inc(pv_ps, 1)

            def keys(s, n):
                if n == 0:
                    pe.wait_ge(k_here[s % 2], 16 * PAGES * (s // 2 + 1))
                    if s >= 1:
                        pe.wait_ge(kt_v, s)
                else:
                    pe.wait_ge(kt_a, s + 1)
                for h in range(H):
                    last = nc.tensor.transpose(bank[5][:, P * h:P * (h + 1)], k_raw[:, s % 2, 512 * n + P * h:512 * n + P * (h + 1)], ident)
                last.then_inc(kt_ps, 1)

            def sample_scores(s):
                pe.wait_ge(kt_a, s + 1)
                pe.wait_ge(kt_v, s + 1)
                if s == 0:
                    pe.wait_ge(qbd_set, 8)
                    pe.wait_ge(sc_used, 8)
                if s >= 2:
                    pe.wait_ge(ssc_max, s - 1)
                for h in range(H):
                    q = qbd[:, s, 32 * h:32 * (h + 1)]
                    o = bank[2 + s % 2][32 * h:32 * (h + 1), :]
                    mm(o[:, 0:PAST], q, k_t[:, h, :], start=True, stop=True, tile_position=(0, 32 * h))
                    last = mm(o[:, PAST:320], q, kT[:, h, PROMPT:T], start=True, stop=True, tile_position=(0, 32 * h))
                last.then_inc(ssc_ps, 1)

            def sample_fold(s):
                pe.wait_ge(ss_set, s + 1)
                if s == 0:
                    pe.wait_ge(at_set, H)
                else:
                    pe.wait_ge(fold_set, s)
                fold = cst[:, C_FOLD:C_FOLD + 32]
                for c in range(2):
                    mm(bank[4][:, 32 * c:32 * (c + 1)], p_s[:, s % 2, P * c:P * (c + 1)], fold, start=True, stop=True)
                mm(bank[4][0:64, 64:96], p_s[:, s % 2, PAST:320], fold, start=True, stop=True).then_inc(fold_ps, 1)

            def sample_values(s):
                pe.wait_ge(fold_set, s + 1)
                pe.wait_ge(v_here[s % 2], 16 * PAGES * (s // 2 + 1))
                if s == 0:
                    pe.wait_ge(op_out, 1)
                for h in range(H):
                    o = bank[6][:, 64 * h + 8 * s:64 * h + 8 * s + 8]
                    for n in range(PAGES):
                        mm(o, v_raw[:, s % 2, 512 * n + P * h:512 * n + P * (h + 1)], a_s[:, s % 2, 32 * n + 8 * h:32 * n + 8 * h + 8],
                           start=(n == 0), stop=False)
                    last = mm(o, v_tm[0:64, 2, P * h:P * (h + 1)], a_s[0:64, s % 2, 64 + 8 * h:72 + 8 * h], start=False, stop=True)
                last.then_inc(spv_ps, 1)

            for i in range(14):
                if i < 4:
                    prompt_scores(i)
                if 2 <= i < 6:
                    prompt_values(i - 2)
                if 1 <= i < 5:
                    prompt_transposes(i - 1)
                if 4 <= i < 12:
                    sample_scores(i - 4)
                if 6 <= i:
                    sample_values(i - 6)
                if 5 <= i < 13:
                    sample_fold(i - 5)
                if 3 <= i < 11:
                    keys(i - 3, 0)
                if i < 12:
                    z_job(8 + i)
                if 3 <= i < 11:
                    keys(i - 3, 1)

            pe.wait_ge(state_here, 16)
            pe.wait_ge(op_out, 2)
            for g in range(GROUPS):
                last = nc.tensor.transpose(bank[7][:, 120 * g:120 * (g + 1)], state[0:120, P * g:P * (g + 1)], ident[0:120, 0:120])
            last.then_inc(st_ps, 1)
            for j in range(20, 24):
                z_job(j)
            pe.wait_ge(sq_set, 1)
            pe.wait_ge(ssc_max, SEQS)
            pe.wait_ge(fold_set, SEQS)
            pe.wait_ge(kt_v, SEQS)
            for h in range(H):
                mm(bank[2 + h][:, 0:T], ones[:, :], sq[:, h, :], start=True, stop=True).then_inc(ms_ps, 1)
            for j in range(24, 28):
                z_job(j)
            pe.wait_ge(std_set, 1)
            pe.wait_ge(unew_set, 1)
            for g in range(GROUPS):
                last = nc.tensor.transpose(bank[2][0:15, P * g:P * (g + 1)], lvP[0][:, g, 256:271], ident)
            last.then_inc(u_ps, 1)
            for g in range(GROUPS):
                last = nc.tensor.transpose(bank[3][0:64, P * g:P * (g + 1)], u_new[:, g, :], ident)
            last.then_inc(u_ps, 1)
            pe.wait_ge(wgrp_here, 16)
            pe.wait_ge(st_set, 1)
            for g in range(GROUPS):
                pe.wait_ge(d_set, g + 1)
                mm(bank[4 + g][:, 0:T], w_grp[:, g, :], dT[:, g, :], start=True, stop=True).then_inc(yp_ps, 1)

            pe.wait_ge(u_set, 2)
            pe.wait_ge(yp_set, GROUPS)
            pe.wait_ge(ya_set, 1)
            pe.wait_ge(z_out, 28)
            for n in range(KD):
                i = U_BRANCH + 2 * (n // 4)
                weights(i)
                weights(i + 1)
                if n >= 2:
                    pe.wait_ge(br_mul, n - 1)
                c = slice(P * (n % 4), P * (n % 4 + 1))
                for k in range(4):
                    mm(bank[n % 2][:, 0:T], unit(i % RING, 4)[:, k, c], ypT[:, k, :], start=(k == 0), stop=(k == 3))
                for k in range(4):
                    last = mm(bank[2 + n % 2][:, 0:T], unit((i + 1) % RING, 4)[:, k, c], yaT[:, k, :], start=(k == 0), stop=(k == 3))
                last.then_inc(br_ps, 1)
            for j in range(12):
                t, c = j % 3, j // 3
                if t == 0:
                    weights(U_WO + c)
                if j >= 4:
                    pe.wait_ge(wo_used, j - 3)
                for k in range(KD):
                    if j == 0:
                        pe.wait_ge(m_set, k + 1)
                    last = mm(bank[4 + j % 4][0:ROWS[t], 0:256], mT[:, k, P * t:P * t + ROWS[t]], unit((U_WO + c) % RING, KD)[:, k, :],
                              start=(k == 0), stop=(k == KD - 1))
                last.then_inc(wo_ps, 1)
            transpose_tokens(x1, x1t_ps, x1t_v, x1t_a, lambda t: (pe.wait_ge(x1_set, t + 1), pe.wait_ge(wo_used, 12)))
            pe.wait_ge(x1t_v, 3)
            pe.wait_ge(x1t_a, 3)
            pe.wait_ge(wr_here, 32)
            for t in range(TILES):
                for k in range(KD):
                    last = mm(bank[6][0:ROWS[t], 36 * t:36 * (t + 1)], x1T[:, k, P * t:P * t + ROWS[t]], w_r[:, k, :],
                              start=(k == 0), stop=(k == KD - 1))
            last.then_inc(rt_ps, 1)
            pe.wait_ge(ple_here, 48)
            for t in range(TILES):
                r = ROWS[t]
                for k in range(2):
                    last = nc.tensor.transpose(bank[t][:, P * k:P * k + r], p_tm[0:r, t, P * k:P * (k + 1)], ident[0:r, 0:r])
                last.then_inc(pt_ps, 1)
            pe.wait_ge(pt_out, TILES)
            for j in range(6):
                t, hf = j // 2, j % 2
                if j >= 3:
                    pe.wait_ge(pe_out, j - 2)
                for k in range(2):
                    last = mm(bank[3 + j % 3][0:ROWS[t], :], pT[:, k, P * t:P * t + ROWS[t]], w_ple[:, k, 512 * hf:512 * (hf + 1)],
                              start=(k == 0), stop=(k == 1))
                last.then_inc(pe_ps, 1)
            pe.wait_ge(m_hot, 2)
            b = bank[7]
            for t in range(TILES):
                r = ROWS[t]
                parts = [(ones[0:ROWS[u], 0:r], GG[0:ROWS[u], u, :]) for u in range(TILES)]
                parts += [(ones[0:ROWS[u], 0:r], Mt[0:ROWS[u], u, :]) for u in range(t)]
                parts += [(tri[0:r, 0:r], Mt[0:r, t, :])]
                for n, (l, x) in enumerate(parts):
                    mm(b[0:r, 32 * t:32 * (t + 1)], l, x, start=(n == 0), stop=(n == len(parts) - 1))
            for o, X in ((96, GG), (128, Mt)):
                for u in range(TILES):
                    last = mm(b[:, o:o + 32], ones[0:ROWS[u], :], X[0:ROWS[u], u, :], start=(u == 0), stop=(u == TILES - 1))
            last.then_inc(rank_ps, 1)
            pe.wait_ge(pt_set, TILES)
            pe.wait_ge(pe_out, 6)
            for j in range(21):
                if j >= 6:
                    m = j - 6
                    pe.wait_ge(ga_v if m % 2 == 0 else ga_a, m // 2 + 1)
                if j < 16:
                    for t in range(TILES):
                        r = ROWS[t]
                        last = mm(bank[j % 6][:, 0:320], x1[0:r, t, P * (j // 2):P * (j // 2 + 1)], PT[0:r, t, 320 * (j % 2):320 * (j % 2 + 1)],
                                  start=(t == 0), stop=(t == TILES - 1))
                else:
                    pe.wait_ge(ct_set, TILES)
                    for t in range(TILES):
                        r = ROWS[t]
                        last = nc.tensor.transpose(bank[j % 6][:, P * t:P * t + r], CT[0:r, t, P * (j - 16):P * (j - 15)], ident[0:r, 0:r])
                last.then_inc(ga_ps, 1)
            pe.wait_ge(ga_v, 11)
            pe.wait_ge(ga_a, 10)

            def gate_up(q, slot, x, b):
                w = ring[:, slot:slot + 2, :].rearrange("p s (k n) -> p s k n", k=KD)
                for k in range(KD):
                    for f in range(2):
                        last = mm(b[WIN * f:WIN * (f + 1), 0:256].rearrange("p (s n) -> p s n", s=2), x[:, WIN * k:WIN * (k + 1)],
                                  w[:, :, k, P * f:P * (f + 1)], start=(k == 0), stop=(k == KD - 1), tile_position=(0, WIN * f))
                last.then_inc(q["gu"], 1)

            def turn_hidden(q, n):
                pe.wait_ge(q["h"], n)
                nc.tensor.transpose(bank[2][:, 0:P], hh[:], ident).then_inc(q["ht"], 1)

            def down(q, n, slot):
                pe.wait_ge(q["hT"], n)
                for f in range(2):
                    for d in range(2):
                        last = mm(bank[3][WIN * d:WIN * (d + 1), :], hT[:, WIN * f:WIN * (f + 1)],
                                  unit(slot, 2)[:, f, 512 * d:512 * (d + 1)], start=(f == 0), stop=(f == 1), tile_position=(0, WIN * d))
                last.then_inc(q["y"], 1)

            def turn_result(q, n, b):
                pe.wait_ge(q["ys"], n)
                for c in range(4):
                    last = nc.tensor.transpose(b[:, P * c:P * (c + 1)], y_s[:, P * c:P * (c + 1)], ident)
                last.then_inc(q["yt"], 1)

            with pe.Fori(0, EXPERTS // 4) as i:
                for j in range(4):
                    n = i * 4 + (j + 1)
                    pe.wait_ge(main["xg"], n)
                    for r in range(2):
                        pe.wait_ge(w_in_slot[3 * j + r], i * 16 + 16 * (U_EXPERT // RING + 1))
                    gate_up(main, 3 * j, xg[:, j % 2, :], bank[j % 2])
                    if j > 0:
                        turn_result(main, i * 4 + j, bank[4 + (j - 1) % 2])
                    turn_hidden(main, n)
                    pe.wait_ge(w_in_slot[3 * j + 2], i * 16 + 16 * (U_EXPERT // RING + 1))
                    down(main, n, 3 * j + 2)
                turn_result(main, i * 4 + 4, bank[5])
            pe.wait_ge(starts_set, 1)
            crowded = pe.value_load(flag[0:1, 0:1], min_val=0, max_val=1)
            with pe.If(crowded > 0):
                pe.wait_ge(main["out"], EXPERTS)
                pe.sem_inc(over["freed"], 1)
                with pe.Fori(0, EXPERTS) as e:
                    pe.wait_ge(over["w"], e * 48 + 48)
                    for w in range(WINDOWS):
                        n = e * WINDOWS + (w + 1)
                        pe.wait_ge(over["xg"], n)
                        gate_up(over, 9, xg[:, 0, :], bank[0])
                        turn_hidden(over, n)
                        down(over, n, 11)
                        turn_result(over, n, bank[4])
                    pe.sem_inc(over["freed"], 1)

            pe.wait_ge(moe_done, 1)
            for g in range(10):
                if g >= 6:
                    m = g - 6
                    pe.wait_ge(yt_v if m % 2 == 0 else yt_a, m // 2 + 1)
                for j in range(4):
                    k = 4 * (g % 2) + j
                    last = nc.tensor.transpose(bank[g % 6][:, P * j:P * (j + 1)], YsT[:, k, P * (g // 2):P * (g // 2 + 1)], ident)
                last.then_inc(yt_ps, 1)
            pe.wait_ge(yt_v, 5)
            pe.wait_ge(yt_a, 5)
            for j in range(6):
                t, hf = j // 2, j % 2
                if j >= 2:
                    pe.wait_ge(cm_used, j - 1)
                for n in range(5):
                    last = mm(bank[6 + j % 2][0:ROWS[t], :], Pj[:, n, P * t:P * t + ROWS[t]], Yj[:, n, 512 * hf:512 * (hf + 1)],
                              start=(n == 0), stop=(n == 4))
                last.then_inc(cm_ps, 1)
            transpose_tokens(x2, x2t_ps, x2t_v, x2t_a, lambda t: pe.wait_ge(x2_set, t + 1))
            pe.wait_ge(x2t_v, 3)
            pe.wait_ge(x2t_a, 3)
            for j in range(12):
                t, c = j % 3, j // 3
                if t == 0:
                    weights(U_PLE + c)
                if j >= 4:
                    pe.wait_ge(pg_add, j - 3)
                for k in range(KD):
                    last = mm(bank[j % 4][0:ROWS[t], 0:256], x2T[:, k, P * t:P * t + ROWS[t]], unit((U_PLE + c) % RING, KD)[:, k, :],
                              start=(k == 0), stop=(k == KD - 1))
                last.then_inc(pg_ps, 1)


_INS = ['x_prompt', 'x_sample', 'p_prompt', 'p_sample', 'cache_k', 'cache_v', 'state_pool', 'page_table', 'w_in', 'b_in',
        'lam_q1', 'lam_k1', 'lam_q2', 'lam_k2', 'g_sub', 'w_pool_grp', 's_pool', 'w_pool_br', 'w_attn_br', 'w_o', 'ln1_g',
        'ln1_b', 'w_rg', 'b_rg', 'w_re', 'b_re', 'w_gate', 'w_up', 'w_down', 'ln2_g', 'ln2_b', 'w_ple_gate', 'b_ple_gate',
        'w_ple', 'ln3_g', 'ln3_b']
_OUTS = [('y_prompt', (1, 256, 1024)), ('y_sample', (8, 8, 1024)), ('new_k_prompt', (1, 1, 256, 4, 128)),
         ('new_v_prompt', (1, 1, 256, 4, 128)), ('new_pool_prompt', (1, 1, 15, 512)), ('new_k_sample', (1, 8, 8, 4, 128)),
         ('new_v_sample', (1, 8, 8, 4, 128)), ('new_pool_sample', (1, 8, 15, 512))]


def kernel(**inputs):
    import numpy as _np
    import concourse.bacc as _bacc
    from concourse import mybir as _mybir
    from concourse.bass_utils import run_bass_kernel_spmd as _run

    nc = _bacc.Bacc("TRN2", target_bir_lowering=False, num_devices=1)
    arrays, args = {}, {}
    cst, iota = constant_tables()
    named = {n: _np.ascontiguousarray(inputs[n]) for n in _INS}
    named["cst"], named["iota"] = cst, iota
    for name, arr in named.items():
        arrays[f"in_{name}_dram"] = arr
        args[name] = nc.dram_tensor(f"in_{name}_dram", arr.shape, _mybir.dt.from_np(arr.dtype), kind="ExternalInput").ap()
    for name, shape in _OUTS:
        args[name] = nc.dram_tensor(f"out_{name}_dram", shape, F32, kind="ExternalOutput").ap()
    hybrid_step(nc, args)
    r = _run(nc, [arrays], core_ids=[0])
    return tuple(r.results[0][f"out_{name}_dram"] for name, _ in _OUTS)
```

```python
from contextlib import ExitStack

import concourse.bass as bass
from concourse import mybir
import math
import numpy as np

F32 = mybir.dt.float32
I32 = mybir.dt.int32
F32R = mybir.dt.float32r
ALU = mybir.AluOpType
ACT = mybir.ActivationFunctionType
AX = mybir.AxisListType

P = 128
D = 1024
KD = D // P
PROMPT = 256
SEQS, NEW = 8, 8
T = PROMPT + SEQS * NEW
TILES = 3
ROWS = [128, 128, 64]
H, HD = 4, 64
PAST, PAGE = 256, 128
PAGES = PAST // PAGE
N_PHYS = 20
POOL, GROUPS, STATE = 512, 4, 15
EXPERTS, EG, EE, FF = 32, 4, 8, 256
WIN = 64
PAIRS = 2 * T
SORTED = PAIRS + WIN
WINDOWS = T // WIN
PLE = 256
EPS = 1e-5
ALPHA = 2.0 ** 0.25
LAM_INIT = 0.8 - 0.6 * math.exp(0.0)
MASKED = -1e30
SLOPES = [2.0 ** (-8.0 * (h + 1) / H) for h in range(H)]

UNIT = 2048
RING = 12
W_IN_ORDER = [2, 3, 4, 5, 6, 7, 8, 9, 10, 11, 12, 13, 0, 1, 14, 15]
U_BRANCH = 16
U_WO = 20
U_EXPERT = 24
EARLY = EXPERTS - 4
U_PLE = U_EXPERT + 3 * EARLY
U_LATE = U_PLE + 1
U_GATE = U_LATE + 12

C_IDENT = 0
C_TRI = C_IDENT + 128
C_PROMPT = C_TRI + 128
C_PAST = C_PROMPT + H * 384
C_NEW = C_PAST + PAST
C_FOLD = C_NEW + SEQS * 64
C_COUNT = C_FOLD + 32
C_IOTA = C_COUNT + GROUPS * 16
C_ROW = C_IOTA + 32
C_END = C_ROW + 2


def constant_tables():
    c = np.zeros((P, C_END), np.float32)
    p = np.arange(P)[:, None]
    c[:, C_IDENT:C_IDENT + 128] = np.eye(P)
    c[:, C_TRI:C_TRI + 128] = p < np.arange(P)[None, :]
    j = np.arange(384)[None, :]
    dist = np.where(j < 128, p - j, p + 128 - (j - 128))
    for h in range(H):
        c[:, C_PROMPT + 384 * h:C_PROMPT + 384 * (h + 1)] = np.where(dist >= 0, -SLOPES[h] * dist, MASKED)
    h, r = p // 32, p % 32
    q, used = r % 8, r < 16
    slope = np.array(SLOPES)[h]
    c[:, C_PAST:C_PAST + PAST] = np.where(used, -slope * (PAST + q - np.arange(PAST)[None, :]), 0.0)
    key = np.arange(64)[None, :]
    for s in range(SEQS):
        d = q - key % NEW
        ok = (key // NEW == s) & (d >= 0)
        c[:, C_NEW + 64 * s:C_NEW + 64 * (s + 1)] = np.where(used, np.where(ok, -slope * d, MASKED), 0.0)
    c[:, C_FOLD:C_FOLD + 32] = used & (np.arange(32)[None, :] == 8 * h + q)
    for g in range(GROUPS):
        w = 2 ** (g + 1)
        c[:, C_COUNT + 16 * g:C_COUNT + 16 * (g + 1)] = [w / min(i + 1, w) for i in range(16)]
    c[:, C_IOTA:C_IOTA + 32] = np.arange(32)
    c[:, C_ROW] = (used & (r < 8))[:, 0]
    c[:, C_ROW + 1] = (used & (r >= 8))[:, 0]
    iota = np.broadcast_to(np.arange(PAIRS, dtype=np.float32), (P, PAIRS)).copy()
    return c, iota


def hybrid_step(nc, a):
    ctx = ExitStack()
    with ctx:
        def fixed(name, shape, dt=F32):
            return ctx.enter_context(nc.sbuf_tensor(name, shape, dt))

        def sem(name):
            return ctx.enter_context(nc.semaphore(name))

        ring = fixed("ring", [P, RING, UNIT])
        cst = fixed("cst", [P, C_END])
        ones = fixed("ones", [P, P])
        br_row = fixed("br_row", [P, 36])
        vec = fixed("vec", [41, P])
        col = fixed("col", [P, 41])
        misc = fixed("misc", [P, 64])
        arena_bytes = 95488
        ARENA = -(-nc.sbuf_base // 32) * 32
        arena = fixed("arena", [P, arena_bytes // 4])

        def rounded(name, off, shape):
            return nc.alloc_sbuf_tensor_at(name, shape, F32R, offset=ARENA + off)


        def at(off, shape, dt=F32):
            n = int(np.prod(shape[1:]))
            v = arena[:, off // 4:off // 4 + n]
            if dt != F32:
                v = v.bitcast(dt)
            if len(shape) == 3:
                v = v.rearrange("p (a b) -> p a b", a=shape[1])
            if len(shape) == 4:
                v = v.rearrange("p (a b c) -> p a b c", a=shape[1], b=shape[2])
            return v

        xT = at(0, [P, KD, T])
        qT = at(10240, [P, H, T])
        kT = at(15360, [P, H, T])
        v_tm = at(20480, [P, TILES, 512])
        gT = at(26624, [P, 16, T])
        x_tm = at(47104, [P, TILES, D])
        k_raw = at(47104, [P, 2, PAGES * 512])
        k_t = at(55296, [P, H, PAST])
        v_raw = at(59392, [P, 2, PAGES * 512])
        qbd = at(67584, [P, SEQS, H * 32])
        p_s = at(71680, [P, 2, 320])
        a_s = at(74240, [P, 2, 96])
        s_p = at(75008, [P, 4, 384])
        aT_p = at(81152, [P, 2, 384])
        k_out = at(84224, [P, TILES, 512])
        oT = at(90368, [P, H, T])
        sq = at(75008, [P, H, T])
        os_raw = at(75008, [P, 2, 512])
        bv_row = at(75008, [P, 512])
        rs = at(47104, [P, H, T])
        state = at(81152, [P, 512])
        lv = [at(52224 + 7280 * i, [P, 1820]) for i in range(3)]
        lvP = [x[:, 0:GROUPS * 271].rearrange("p (g j) -> p g j", g=GROUPS) for x in lv]
        lvS = [x[:, GROUPS * 271:1820].rearrange("p (g s j) -> p g s j", g=GROUPS, s=SEQS) for x in lv]
        dT = at(84224, [P, GROUPS, T])
        u_out = at(75008, [P, 2, 512])
        w_grp = at(79104, [P, GROUPS, P])
        u_new = at(83200, [P, 4, 64])
        yaT = at(10240, [P, H, T])
        ypT = at(15360, [P, GROUPS, T])
        mT = at(0, [P, KD, T])
        x_again = at(47104, [P, TILES, D])
        ln1 = at(59520, [P, 2, D])
        x1 = at(26624, [P, TILES, D])
        x1T = at(10240, [P, KD, T])
        w_r = at(67712, [P, KD, 36])
        XsT = at(38912, [P, KD, SORTED])
        PT = rounded("permutation", 61440, [P, TILES, PAIRS])
        x_parts = rounded("x_parts", 0, [P, 5, D])
        CT = at(69120, [P, TILES, PAIRS])
        YsT = at(61440, [P, KD, SORTED])
        p_tm = at(84992, [P, TILES, PLE])
        xg = at(88064, [P, 2, KD * WIN])
        weighted = at(88064, [P, PAIRS])
        iota = at(92160, [P, PAIRS])
        Pj = at(0, [P, 5, T])
        pe_s = at(10240, [P, TILES, D])
        pT = at(22528, [P, 2, T])
        sig, gg, hh = (at(25088 + 512 * i, [P, P]) for i in range(3))
        hT = at(8448, [P, P])
        y_s = at(6400, [P, 512])
        Yj = at(38912, [P, 5, D])
        x2 = at(61440, [P, TILES, D])
        x2T = at(73728, [P, KD, T])
        gt = at(38912, [P, TILES, D])
        ln2, ln3, bpg = ring[:, 5, :], ring[:, 6, :], ring[:, 7, 0:D]
        small = fixed("small", [P, 1330])
        cursor = [0]

        def tiny(*shape):
            n = int(np.prod(shape))
            v = small[:, cursor[0]:cursor[0] + n]
            cursor[0] += n
            assert cursor[0] <= 1330, cursor[0]
            if len(shape) == 2:
                v = v.rearrange("p (a b) -> p a b", a=shape[0])
            return v

        logits = tiny(3, 36)
        c4, c8a, c8b, oh8a, le_s = tiny(3, 4), tiny(3, 8), tiny(3, 8), tiny(3, 8), tiny(3, 8)
        oh4, dl4, lt8 = tiny(3, 4), tiny(3, 4), tiny(3, 8)
        le_m = tiny(3, 32)
        E1, E2, GG, G2 = tiny(3, 32), tiny(3, 32), tiny(3, 32), tiny(3, 32)
        Mt = c_rank = tiny(3, 32)
        m_g, g_id, s_g, m1, i1, m2, i2, ex, c1, c2, e1, e2, pos1, pos2 = (tiny(3) for _ in range(14))
        start_f = tiny(WINDOWS, 33)
        start_i = tiny(WINDOWS, 33).bitcast(I32)
        cnt_max = tiny(2)
        flag = tiny(2).bitcast(I32)
        stats, mv = tiny(3, 12), tiny(3, 2)
        rstd = tiny(4)
        mx, nmx, sm, rr = tiny(2, 4), tiny(2, 4), tiny(2, 4), tiny(2, 4)
        msx, nms, ss, rrs = tiny(2), tiny(2), tiny(2), tiny(2)
        coef, coef_s, lam_p, lam_e, neg_lam, gs, eps = tiny(4), tiny(1), tiny(2), tiny(2), tiny(1), tiny(1), tiny(1)
        pages = fixed("pages", [1, SEQS * PAGES], I32)
        scratch = misc[:, 0:4]

        bank = [ctx.enter_context(nc.psum_tensor(f"bank{i}", [P, 512], F32)) for i in range(8)]

        ident = cst[:, C_IDENT:C_IDENT + P]
        tri = cst[:, C_TRI:C_TRI + P]
        iota32 = cst[:, C_IOTA:C_IOTA + 32]

        w_in_slot = [sem(f"w_in_slot{i}") for i in range(RING)]
        x_here, ident_here, cst_here, vec_here, rows_here, grp_here = map(sem, ("x_here", "ident_here", "cst_here", "vec_here", "rows_here", "grp_here"))
        wgrp_here = sem("wgrp_here")
        pages_here, vec_zero, ones_set, qbd_zero = map(sem, ("pages_here", "vec_zero", "ones_set", "qbd_zero"))
        xt_ps, xt_v, xt_a = map(sem, ("xt_ps", "xt_v", "xt_a"))
        vec_ps, col_set, lam_prod, lam_ps, lam_exp = map(sem, ("vec_ps", "col_set", "lam_prod", "lam_ps", "lam_exp"))
        z_ps, z_out, v_ps, v_out, qbd_set = map(sem, ("z_ps", "z_out", "v_ps", "v_out", "qbd_set"))
        ko_ps, ko_set = map(sem, ("ko_ps", "ko_set"))
        sc_ps, sc_used, sc_max, sc_exp, a_set, at_ps, at_set, pv_ps, op_out = map(
            sem, ("sc_ps", "sc_used", "sc_max", "sc_exp", "a_set", "at_ps", "at_set", "pv_ps", "op_out"))
        k_here, v_here = [sem(f"k_here{i}") for i in range(2)], [sem(f"v_here{i}") for i in range(2)]
        kt_ps, kt_a, kt_v = map(sem, ("kt_ps", "kt_a", "kt_v"))
        ssc_ps, ssc_max, ssc_exp, ss_set, fold_ps, fold_set, spv_ps, os_out = map(
            sem, ("ssc_ps", "ssc_max", "ssc_exp", "ss_set", "fold_ps", "fold_set", "spv_ps", "os_out"))
        or_set, ot_ps = map(sem, ("or_set", "ot_ps"))
        sq_set, ms_ps, std_set, ya_set = map(sem, ("sq_set", "ms_ps", "std_set", "ya_set"))
        state_here, st_ps, st_set, pre_zero, win_set, win_step, d_set, u_ps, u_set, unew_set = map(
            sem, ("state_here", "st_ps", "st_set", "pre_zero", "win_set", "win_step", "d_set", "u_ps", "u_set", "unew_set"))
        yp_ps, yp_set, br_ps, br_mul, m_set = map(sem, ("yp_ps", "yp_set", "br_ps", "br_mul", "m_set"))
        x2_here, ln1_here, wo_ps, wo_used = map(sem, ("x2_here", "ln1_here", "wo_ps", "wo_used"))
        var_set, sd_set, x1_set = map(sem, ("var_set", "sd_set", "x1_set"))
        x1t_ps, x1t_v, x1t_a, wr_here, rt_ps = map(sem, ("x1t_ps", "x1t_v", "x1t_a", "wr_here", "rt_ps"))
        rt_dl, rt_exp, m_hot, rank_ps, pt_set, ct_set, starts_set = map(
            sem, ("rt_dl", "rt_exp", "m_hot", "rank_ps", "pt_set", "ct_set", "starts_set"))
        iota_here, ple_here, pt_ps, pt_out, pe_ps, pe_out = map(sem, ("iota_here", "ple_here", "pt_ps", "pt_out", "pe_ps", "pe_out"))
        ga_ps, ga_out, pj_set, pads_set, high_set, low_set = map(sem, ("ga_ps", "ga_out", "pj_set", "pads_set", "high_set", "low_set"))
        steps = ("xg", "gu", "sig", "g", "h", "ht", "hT", "y", "ys", "yt", "out")
        main = {n: sem("main_" + n) for n in steps}
        over = {n: sem("over_" + n) for n in steps + ("w", "freed")}
        moe_done = sem("moe_done")
        yt_ps, yt_v, yt_a, cm_ps, cm_used = map(sem, ("yt_ps", "yt_v", "yt_a", "cm_ps", "cm_used"))
        x2t_ps, x2t_v, x2t_a, pg_ps, pg_add, pg_sig, pg_mul = map(
            sem, ("x2t_ps", "x2t_v", "x2t_a", "pg_ps", "pg_add", "pg_sig", "pg_mul"))
        late_here, y_set, x2_set = map(sem, ("late_here", "y_set", "x2_set"))
        stored = sem("stored")
        chain_v = sem("chain_v")

        win_d = a["w_in"].rearrange("l (k p) (c n) -> (l c) p k n", p=P, n=256)
        pbr_d = a["w_pool_br"].rearrange("l (k p) (c n) -> (l c) p k n", p=P, n=512)
        abr_d = a["w_attn_br"].rearrange("l (k p) (c n) -> (l c) p k n", p=P, n=512)
        wo_d = a["w_o"].rearrange("l (k p) (c n) -> (l c) p k n", p=P, n=256)
        wg_d = a["w_gate"].rearrange("l g e (k p) f -> (l g e) p k f", p=P)
        wu_d = a["w_up"].rearrange("l g e (k p) f -> (l g e) p k f", p=P)
        wd_d = a["w_down"].rearrange("l g e (k p) d -> (l g e) p k d", p=P)
        pg_d = a["w_ple_gate"].rearrange("l (k p) (c n) -> (l c) p k n", p=P, n=256)
        ck_d = a["cache_k"].rearrange("l n p h d -> (l n) p (h d)")
        cv_d = a["cache_v"].rearrange("l n p h d -> (l n) p (h d)")
        xp_d = a["x_prompt"].rearrange("b (t p) d -> p (b t) d", p=P)
        xs_d = a["x_sample"].rearrange("s t d -> (s t) d")
        pp_d = a["p_prompt"].rearrange("l b (t p) d -> p (l b t) d", p=P)
        ps_d = a["p_sample"].rearrange("l s t d -> (l s t) d")

        def unit(slot, k):
            return ring[:, slot, :].rearrange("p (k n) -> p k n", k=k)

        def level(n):
            return 0 if n == 0 else 2 - n % 2

        def halves(j):
            t = j // 2
            if t < 2:
                return [(t, slice(0, P), slice(512 * (j % 2), 512 * (j % 2 + 1)))]
            return [(t, slice(64 * hf, 64 * hf + 64), slice(512 * hf, 512 * (hf + 1))) for hf in range(2)]

        def yt_out(copy, g):
            return copy(Yj[:, g // 2, 512 * (g % 2):512 * (g % 2 + 1)], bank[g % 6][:, :])

        block = ctx.enter_context(nc.Block())

        @block.sync
        def _(sp):
            def wait_used(i):
                if i < U_BRANCH:
                    if i in (4, 5):
                        sp.wait_ge(v_ps, 3 * (i - 3))
                    else:
                        sp.wait_ge(z_ps, 2 * i + 2 if i < 4 else 2 * i - 2)
                elif i < U_WO:
                    sp.wait_ge(br_ps, 4 * ((i - U_BRANCH) // 2 + 1))
                elif i < U_EXPERT:
                    sp.wait_ge(wo_ps, 5)
                elif i == U_PLE:
                    sp.wait_ge(pe_ps, 5)
                else:
                    e, r = divmod(i - U_EXPERT - (i > U_PLE), 3)
                    sp.wait_ge(main["gu"] if r < 2 else main["y"], e + 1)

            def load(i, src, k):
                if i >= RING:
                    wait_used(i - RING)
                sp.dma_start(unit(i % RING, k), src).then_inc(w_in_slot[i % RING], 16)

            sp.dma_start(cst[:, 0:P], a["cst"][:, 0:P]).then_inc(ident_here, 16)
            sp.dma_start(x_tm[:, 0:2, :], xp_d).then_inc(x_here, 16)
            sp.dma_start(x_tm[0:64, 2, :], xs_d).then_inc(x_here, 16)
            sp.wait_ge(vec_zero, 1)
            sp.dma_start(vec[0:32, :], a["b_in"].rearrange("l (c p) -> (l c) p", p=P)).then_inc(vec_here, 16)
            sp.dma_start(vec[32:36, :], a["s_pool"].rearrange("l (c p) -> (l c) p", p=P)).then_inc(vec_here, 16)
            sp.dma_start(vec[36:37, :], a["g_sub"]).then_inc(vec_here, 16)
            for n, name in enumerate(("lam_q1", "lam_k1", "lam_q2", "lam_k2")):
                sp.dma_start(vec[37 + n:38 + n, 0:HD], a[name]).then_inc(vec_here, 16)
            for i, c in enumerate(W_IN_ORDER):
                load(i, win_d[c], KD)
                if i == 3:
                    sp.dma_start(bv_row[:], a["b_in"][0, 1536:2048].partition_broadcast(P)).then_inc(rows_here, 16)
                    sp.dma_start(cst[:, P:C_END], a["cst"][:, P:C_END]).then_inc(cst_here, 16)
            for i, (w, c) in enumerate(((pbr_d, 0), (abr_d, 0), (pbr_d, 1), (abr_d, 1))):
                load(U_BRANCH + i, w[c], 4)
            for c in range(4):
                load(U_WO + c, wo_d[c], KD)
            for e in range(4):
                for r, (w, k) in enumerate(((wg_d, KD), (wu_d, KD), (wd_d, 2))):
                    load(U_EXPERT + 3 * e + r, w[e], k)
            with sp.Fori(0, EARLY // 4 - 1) as i:
                for j in range(4):
                    for r, (w, k) in enumerate(((wg_d, KD), (wu_d, KD), (wd_d, 2))):
                        slot = 3 * j + r
                        sp.wait_ge(main["gu"] if r < 2 else main["y"], i * 4 + (j + 1))
                        src = w[bass.ds(i * 4 + (j + 4), 1), :, :, :].rearrange("o p k n -> p (o k) n")
                        sp.dma_start(unit(slot, k), src).then_inc(w_in_slot[slot], 16)
            load(U_PLE, a["w_ple"].rearrange("l (k p) d -> p (l k) d", p=P), 2)
            for e in range(EARLY, EXPERTS):
                for r, (w, k) in enumerate(((wg_d, KD), (wu_d, KD), (wd_d, 2))):
                    load(U_LATE + 3 * (e - EARLY) + r, w[e], k)
            for c in range(4):
                load(U_GATE + c, pg_d[c], KD)
            wait_used(U_GATE + 5 - RING)
            wait_used(U_GATE + 6 - RING)
            for n, name in enumerate(("ln2_g", "ln2_b", "ln3_g", "ln3_b")):
                dst = (ln2, ln3)[n // 2][:, (n % 2) * D:(n % 2 + 1) * D]
                sp.dma_start(dst, a[name][0].partition_broadcast(P)).then_inc(late_here, 16)
            sp.dma_start(bpg, a["b_ple_gate"][0].partition_broadcast(P)).then_inc(late_here, 16)
            sp.wait_ge(starts_set, 1)
            crowded = sp.value_load(flag[0:1, 0:1], min_val=0, max_val=1)
            with sp.If(crowded > 0):
                with sp.Fori(0, EXPERTS) as e:
                    sp.wait_ge(over["freed"], e + 1)
                    for r, (w, k) in enumerate(((wg_d, KD), (wu_d, KD), (wd_d, 2))):
                        src = w[bass.ds(e, 1), :, :, :].rearrange("o p k n -> p (o k) n")
                        sp.dma_start(unit(9 + r, k), src).then_inc(over["w"], 16)
            yp = a["y_prompt"].rearrange("b (t p) d -> p (b t) d", p=P)
            for t in range(TILES):
                sp.wait_ge(y_set, t + 1)
                dst = yp[:, t, :] if t < 2 else a["y_sample"].rearrange("s t d -> (s t) d")
                sp.dma_start(dst, x2[0:ROWS[t], t, :]).then_inc(stored, 16)
            sp.wait_ge(stored, 16 * 10)

        @block.gpsimd
        def _(pool):
            pool.dma_start(pages[0:1, :], a["page_table"].rearrange("s n -> (s n)").unsqueeze(0)).then_inc(pages_here, 16)
            pool.memset(ones[:], 1.0).then_inc(ones_set, 1)
            pool.dma_start(br_row[:, 0:4], a["b_rg"][0].partition_broadcast(P)).then_inc(grp_here, 16)
            pool.dma_start(br_row[:, 4:36], a["b_re"].rearrange("l g e -> l (g e)")[0].partition_broadcast(P)).then_inc(grp_here, 16)
            pool.wait_ge(xt_ps, 6)
            pool.memset(qbd[:], 0.0).then_inc(qbd_zero, 1)
            pool.wait_ge(pages_here, 16)

            def load_pages(s, src, dst, here):
                for n in range(PAGES):
                    pg = pool.value_load(pages[0:1, PAGES * s + n:PAGES * s + n + 1], min_val=0, max_val=N_PHYS - 1)
                    pool.dma_start(dst[:, s % 2, 512 * n:512 * (n + 1)],
                                   src[bass.ds(pg, 1), :, :].rearrange("o p n -> p (o n)")).then_inc(here[s % 2], 16)

            for s in range(SEQS + 2):
                if s < SEQS:
                    if s >= 2:
                        pool.wait_ge(kt_ps, 2 * (s - 1))
                    load_pages(s, ck_d, k_raw, k_here)
                v = s - 2
                if v >= 0:
                    if v >= 2:
                        pool.wait_ge(spv_ps, v - 1)
                    load_pages(v, cv_d, v_raw, v_here)
                if v == 2:
                    pool.wait_ge(pv_ps, H)
                    pool.dma_start(state[0:120, :], a["state_pool"].rearrange("l s j c -> (l s j) c")).then_inc(state_here, 16)
            pool.wait_ge(os_out, 2 * H)
            pool.wait_ge(op_out, 2)
            pool.tensor_tensor(sq[:], oT[:], oT[:], ALU.mult).then_inc(sq_set, 1)
            pool.wait_ge(spv_ps, SEQS)
            pool.wait_ge(kt_v, SEQS)
            pool.memset(lvP[0][:, :, 0:15], 0.0).then_inc(pre_zero, 1)
            pool.wait_ge(pre_zero, 1)
            pool.wait_ge(z_out, 24)
            pool.wait_ge(st_set, 1)
            for n in range(1, 5):
                src, dst, step, g = level(n - 1), level(n), 2 ** (n - 1), n - 1
                lo = 2 ** n - 1
                pool.tensor_tensor(lvP[dst][:, g:4, lo:271], lvP[src][:, g:4, lo:271], lvP[src][:, g:4, lo - step:271 - step], ALU.add).then_inc(win_step, 1)
                for gg_ in range(g, 4):
                    last = pool.tensor_tensor(lvS[dst][:, gg_, :, lo:23], lvS[src][:, gg_, :, lo:23], lvS[src][:, gg_, :, lo - step:23 - step], ALU.add)
                    last.then_inc(win_step, 1)
                total = sum(1 + 4 - k for k in range(n))
                pool.wait_ge(win_step, total)
                pool.tensor_tensor(lvP[dst][:, g, 15:31], lvP[dst][:, g, 15:31], cst[:, C_COUNT + 16 * g:C_COUNT + 16 * g + 16], ALU.mult).then_inc(win_set, 1)
            pool.wait_ge(ms_ps, H)
            pool.dma_start(w_grp[:], a["w_pool_grp"].rearrange("l g c e -> c (l g) e")).then_inc(wgrp_here, 16)
            pool.wait_ge(d_set, 4)
            pool.wait_ge(ya_set, 1)
            pool.wait_ge(u_ps, 2)
            pool.wait_ge(unew_set, 1)
            pool.dma_start(x_again[:, 0:2, :], xp_d).then_inc(x2_here, 16)
            pool.dma_start(x_again[0:64, 2, :], xs_d).then_inc(x2_here, 16)
            pool.dma_start(ln1[:, 0, :], a["ln1_g"][0].partition_broadcast(P)).then_inc(ln1_here, 16)
            pool.dma_start(ln1[:, 1, :], a["ln1_b"][0].partition_broadcast(P)).then_inc(ln1_here, 16)
            pool.dma_start(w_r[:, :, 0:4], a["w_rg"].rearrange("l (k p) g -> p (l k) g", p=P)).then_inc(wr_here, 16)
            pool.dma_start(w_r[:, :, 4:36], a["w_re"].rearrange("l (k p) g e -> p (l k) (g e)", p=P)).then_inc(wr_here, 16)
            for n in range(KD):
                pool.wait_ge(br_mul, n + 1)
                if n == 0:
                    pool.wait_ge(z_ps, 28)
                pool.tensor_tensor(mT[:, n, :], gT[:, n, :], gT[:, 8 + n, :], ALU.add).then_inc(m_set, 1)
            pool.wait_ge(x1_set, 3)
            pool.dma_start(iota[:], a["iota"]).then_inc(iota_here, 16)
            pool.wait_ge(rt_ps, 1)
            pool.wait_ge(yp_ps, GROUPS)
            pool.wait_ge(stored, 16 * 7)
            pool.dma_start(p_tm[:, 0:2, :], pp_d).then_inc(ple_here, 16)
            pool.dma_start(p_tm[0:64, 2, :], ps_d).then_inc(ple_here, 16)
            pool.memset(XsT[:, :, PAIRS:SORTED], 0.0).then_inc(pads_set, 1)
            pool.wait_ge(pe_out, 6)
            for t in range(TILES):
                for hf in range(2):
                    pool.wait_ge(pg_sig, 2 * t + hf + 1)
                    v = gt[0:ROWS[t], t, 512 * hf:512 * (hf + 1)]
                    pool.tensor_tensor(v, v, pe_s[0:ROWS[t], t, 512 * hf:512 * (hf + 1)], ALU.mult).then_inc(pg_mul, 1)

        @block.scalar
        def _(act):
            def four(b, rows):
                return b[:, :].rearrange("p (j n) -> p j n", j=4)[:, :, 0:rows]

            for g in range(1, 6, 2):
                t, hf = g // 2, g % 2
                act.wait_ge(xt_ps, g + 1)
                nc.scalar.copy(xT[:, 4 * hf:4 * hf + 4, P * t:P * t + ROWS[t]], four(bank[g], ROWS[t])).then_inc(xt_a, 1)
            act.wait_ge(lam_ps, 1)
            nc.scalar.activation(lam_e[:, :], bank[6][:, 64:66], ACT.Exp).then_inc(lam_exp, 1)

            def z_job(j):
                act.wait_ge(z_ps, j + 1)
                b = bank[j % 2]
                if j < 8:
                    dst = (qT if j < 4 else kT)[:, j % 4, :]
                    c = 4 + j
                    nc.scalar.activation(dst, b[:, 0:T], ACT.Identity, bias=col[:, c:c + 1]).then_inc(z_out, 1)
                elif 20 <= j < 24:
                    g = j - 20
                    if g == 0:
                        act.wait_ge(spv_ps, SEQS)
                        act.wait_ge(kt_v, SEQS)
                    nc.scalar.activation(lvP[0][:, g, 15:271], b[:, 0:PROMPT], ACT.Identity, bias=col[:, g:g + 1])
                    nc.scalar.activation(lvS[0][:, g, :, 15:23], b[:, PROMPT:T].rearrange("p (s j) -> p s j", s=SEQS),
                                         ACT.Identity, bias=col[:, g:g + 1]).then_inc(z_out, 1)
                else:
                    g = j - 8 if j < 20 else j - 12
                    nc.scalar.activation(gT[:, g, :], b[:, 0:T], ACT.Sigmoid, bias=col[:, 16 + g:17 + g]).then_inc(z_out, 1)

            act.wait_ge(col_set, 1)
            for j in range(8):
                z_job(j)
            for t in range(TILES):
                act.wait_ge(ko_ps, t + 1)
                nc.scalar.copy(k_out[0:ROWS[t], t, :], bank[4 + t][0:ROWS[t], :]).then_inc(ko_set, 1)
            act.wait_ge(ko_set, TILES)
            act.dma_start(a["new_k_prompt"].rearrange("l b (t p) h d -> p (l b t) (h d)", p=P), k_out[:, 0:2, :]).then_inc(stored, 16)
            act.dma_start(a["new_k_sample"].rearrange("l s t h d -> (l s t) (h d)"), k_out[0:64, 2, :]).then_inc(stored, 16)
            act.wait_ge(v_out, 6)
            act.dma_start(a["new_v_prompt"].rearrange("l b (t p) h d -> p (l b t) (h d)", p=P), v_tm[:, 0:2, :]).then_inc(stored, 16)
            act.dma_start(a["new_v_sample"].rearrange("l s t h d -> (l s t) (h d)"), v_tm[0:64, 2, :]).then_inc(stored, 16)

            for i in range(14):
                if i < 4:
                    act.wait_ge(sc_max, i + 1)
                    for c in range(2):
                        for q in range(2):
                            v = s_p[:, 2 * (i % 2) + c, 128 * q:128 + 256 * q]
                            last = nc.scalar.activation(v, v, ACT.Exp, bias=nmx[:, i % 2, 2 * c + q:2 * c + q + 1],
                                                        accum_out=sm[:, i % 2, 2 * c + q:2 * c + q + 1])
                    last.then_inc(sc_exp, 1)
                if 4 <= i < 12:
                    s = i - 4
                    act.wait_ge(ssc_max, s + 1)
                    v = p_s[:, s % 2, :]
                    nc.scalar.activation(v, v, ACT.Exp, bias=nms[:, s % 2:s % 2 + 1], accum_out=ss[:, s % 2:s % 2 + 1]).then_inc(ssc_exp, 1)
                if 3 <= i < 11:
                    s = i - 3
                    act.wait_ge(kt_ps, 2 * s + 1)
                    if s >= 1:
                        act.wait_ge(ssc_ps, s)
                    nc.scalar.copy(k_t[:, :, 0:PAGE], four(bank[5], P)).then_inc(kt_a, 1)
                if i == 10:
                    act.wait_ge(spv_ps, 4)
                    nc.scalar.copy(os_raw[:, 0, :], bank[6][:, :]).then_inc(or_set, 1)
                if i in (4, 6):
                    n = i // 2 - 2
                    act.wait_ge(pv_ps, 2 * n + 2)
                    nc.scalar.copy(oT[:, 2 * n:2 * n + 2, 0:PROMPT], bank[6 + n][:, :].rearrange("p (h q) -> p h q", h=2)).then_inc(op_out, 1)
                if i < 12:
                    z_job(8 + i)
            act.wait_ge(spv_ps, SEQS)
            nc.scalar.copy(os_raw[:, 1, :], bank[7][:, :]).then_inc(or_set, 1)
            for j in range(20, 24):
                z_job(j)
            act.wait_ge(ms_ps, 4)
            act.wait_ge(spv_ps, SEQS)
            for h in range(H):
                last = nc.scalar.activation(rs[:, h, :], bank[2 + h][:, 0:T], ACT.Sqrt, bias=eps[:, :], scale=1.0 / P)
            last.then_inc(std_set, 1)
            for j in range(24, 28):
                z_job(j)
            for g in range(GROUPS):
                act.wait_ge(yp_ps, g + 1)
                nc.scalar.activation(ypT[:, g, :], bank[4 + g][:, 0:T], ACT.Copy, scale=col[:, 32 + g:33 + g]).then_inc(yp_set, 1)
            act.wait_ge(u_set, 2)
            act.dma_start(a["new_pool_prompt"].rearrange("l b j c -> (l b j) c"), u_out[0:15, 0, :]).then_inc(stored, 16)
            act.dma_start(a["new_pool_sample"].rearrange("l s j c -> (l s) j c")[:, 7:15, :], u_out[0:64, 1, :]).then_inc(stored, 16)
            act.dma_start(a["new_pool_sample"].rearrange("l s j c -> (l s) j c")[:, 0:7, :],
                          a["state_pool"].rearrange("l s j c -> (l s) j c")[:, 8:15, :]).then_inc(stored, 16)

            def norm(n):
                act.wait_ge(var_set, n)
                v = rstd[0:ROWS[(n - 1) % TILES], (n - 1) % TILES:(n - 1) % TILES + 1]
                nc.scalar.activation(v, v, ACT.Sqrt).then_inc(sd_set, 1)

            def columns(xT_, t, ps, done):
                act.wait_ge(ps, 2 * t + 2)
                nc.scalar.copy(xT_[:, 4:8, P * t:P * t + ROWS[t]], four(bank[2 * t + 1], ROWS[t])).then_inc(done, 1)

            for t in range(TILES):
                norm(t + 1)
                columns(x1T, t, x1t_ps, x1t_a)
            act.wait_ge(x1_set, 3)
            act.wait_ge(wo_ps, 5)
            for t in range(2):
                nc.scalar.copy(x_parts[:, t, :], x1[:, t, :]).then_inc(high_set, 1)
            act.wait_ge(rt_dl, 1)
            nc.scalar.activation(dl4[:], dl4[:], ACT.Exp).then_inc(rt_exp, 1)
            act.wait_ge(rt_ps, 1)
            nc.scalar.copy(x_parts[0:64, 4, :], x1[0:64, 2, :]).then_inc(high_set, 1)
            act.wait_ge(rt_dl, 2)
            nc.scalar.activation(ex[:, :], ex[:, :], ACT.Exp).then_inc(rt_exp, 1)
            for t in range(TILES):
                act.wait_ge(pt_ps, t + 1)
                nc.scalar.copy(pT[:, :, P * t:P * t + ROWS[t]], four(bank[t], ROWS[t])[:, 0:2, :]).then_inc(pt_out, 1)
            for j in range(16):
                act.wait_ge(ga_ps, j + 1)
                nc.scalar.copy(XsT[:, j // 2, 320 * (j % 2):320 * (j % 2 + 1)], bank[j % 6][:, 0:320]).then_inc(ga_out, 1)

            def gate_sigmoid(q, n, b):
                act.wait_ge(q["gu"], n)
                nc.scalar.activation(sig[:], b[:, 0:P], ACT.Sigmoid).then_inc(q["sig"], 1)

            def hidden_out(q, n):
                act.wait_ge(q["ht"], n)
                nc.scalar.copy(hT[:], bank[2][:, 0:P]).then_inc(q["hT"], 1)

            def result_out(q, n):
                act.wait_ge(q["y"], n)
                nc.scalar.copy(y_s[:], bank[3][:, :]).then_inc(q["ys"], 1)

            def embedding_out(j):
                act.wait_ge(pe_ps, j + 1)
                for t, p, c in halves(j):
                    nc.scalar.copy(pe_s[0:ROWS[t], t, c], bank[6 + j % 2][p, :]).then_inc(pe_out, 1)

            def four_experts(first):
                for j in range(4):
                    hidden_out(main, first + (j - 1))
                    gate_sigmoid(main, first + j, bank[j % 2])
                    result_out(main, first + (j - 1))

            gate_sigmoid(main, 1, bank[0])
            for n in range(1, 4):
                hidden_out(main, n)
                gate_sigmoid(main, n + 1, bank[n % 2])
                result_out(main, n)
            with act.Fori(0, EARLY // 4 - 1) as i:
                four_experts(i * 4 + 5)
            for j in range(5):
                embedding_out(j)
            four_experts(EARLY + 1)
            hidden_out(main, EXPERTS)
            result_out(main, EXPERTS)
            act.wait_ge(starts_set, 1)
            crowded = act.value_load(flag[0:1, 0:1], min_val=0, max_val=1)
            with act.If(crowded > 0):
                with act.Fori(0, EXPERTS * WINDOWS) as n:
                    gate_sigmoid(over, n + 1, bank[0])
                    hidden_out(over, n + 1)
                    result_out(over, n + 1)

            for g in range(1, 10, 2):
                act.wait_ge(yt_ps, g + 1)
                yt_out(nc.scalar.copy, g).then_inc(yt_a, 1)
            def gate_out(n):
                t, hf = n // 2, n % 2
                act.wait_ge(pg_add, n + 1)
                v = gt[0:ROWS[t], t, 512 * hf:512 * (hf + 1)]
                nc.scalar.activation(v, v, ACT.Sigmoid).then_inc(pg_sig, 1)

            norm(4)
            norm(5)
            norm(6)
            columns(x2T, 0, x2t_ps, x2t_a)
            gate_out(0)
            columns(x2T, 1, x2t_ps, x2t_a)
            gate_out(1)
            norm(7)
            gate_out(2)
            columns(x2T, 2, x2t_ps, x2t_a)
            gate_out(3)
            norm(8)
            gate_out(4)
            gate_out(5)
            norm(9)

        @block.vector
        def _(dve):
            V = nc.vector
            count = [0]

            def link(ins):
                count[0] += 1
                ins.then_inc(chain_v, 1)
                dve.wait_ge(chain_v, count[0])

            def four(b, rows):
                return b[:, :].rearrange("p (j n) -> p j n", j=4)[:, :, 0:rows]

            V.memset(vec[:], 0.0).then_inc(vec_zero, 1)
            V.memset(eps[:, :], EPS)
            V.memset(start_f[:, :, 32:33], float(PAIRS))
            V.memset(coef[:, :], 1.0)
            V.memset(rstd[:, :], 1.0)
            link(V.memset(logits[:], 0.0))
            for g in range(0, 6, 2):
                t, hf = g // 2, g % 2
                dve.wait_ge(xt_ps, g + 1)
                V.tensor_copy(xT[:, 4 * hf:4 * hf + 4, P * t:P * t + ROWS[t]], four(bank[g], ROWS[t])).then_inc(xt_v, 1)
            dve.wait_ge(vec_ps, 1)
            link(V.tensor_copy(col[:, :], bank[6][:, 0:41]))
            V.tensor_scalar(gs[:, :], col[:, 36:37], 1.0 - LAM_INIT, None, ALU.mult).then_inc(col_set, 1)
            lv4 = col[0:HD, 37:41].rearrange("p (a b) -> p a b", b=2)
            V.tensor_tensor(lam_p[0:HD, :], lv4[:, :, 0], lv4[:, :, 1], ALU.mult).then_inc(lam_prod, 1)
            dve.wait_ge(lam_exp, 1)
            link(V.tensor_tensor(neg_lam[:, :], lam_e[:, 1:2], lam_e[:, 0:1], ALU.subtract))
            link(V.tensor_scalar(neg_lam[:, :], neg_lam[:, :], -LAM_INIT, None, ALU.add))
            dve.wait_ge(cst_here, 16)
            V.tensor_scalar(coef[:, 2:4], coef[:, 2:4], neg_lam[:, :], None, ALU.mult)
            link(V.scalar_tensor_tensor(coef_s[:, :], cst[:, C_ROW + 1:C_ROW + 2], neg_lam[:, :], cst[:, C_ROW:C_ROW + 1], ALU.mult, ALU.add))

            dve.wait_ge(rows_here, 16)
            for j in range(6):
                t, c = j % 3, j // 3
                dve.wait_ge(v_ps, j + 1)
                V.tensor_tensor(v_tm[0:ROWS[t], t, 256 * c:256 * (c + 1)], bank[2 + j % 2][0:ROWS[t], 0:256],
                                bv_row[0:ROWS[t], 256 * c:256 * (c + 1)], ALU.add).then_inc(v_out, 1)
            dve.wait_ge(qbd_zero, 1)
            dve.wait_ge(z_out, 4)
            for c in range(2):
                dst = qbd[64 * c:64 * c + 64, :, :].rearrange("p s (h r) -> p h s r", h=H)[:, :, :, 8 * c:8 * c + 8]
                src = qT[64 * c:64 * c + 64, :, PROMPT:T].rearrange("p h (s t) -> p h s t", s=SEQS)
                for h in range(H):
                    last = V.tensor_copy(dst[:, h], src[:, h])
                    last.then_inc(qbd_set, 1)

            for i in range(14):
                if i < 4:
                    h, b = i, i % 2
                    dve.wait_ge(sc_ps, i + 1)
                    if i >= 2:
                        dve.wait_ge(at_ps, i - 1)
                    bias = cst[:, C_PROMPT + 384 * h:C_PROMPT + 384 * (h + 1)]
                    V.scalar_tensor_tensor(s_p[:, 2 * b, :], bank[2][:, 0:384], HD ** -0.5, bias, ALU.mult, ALU.add).then_inc(sc_used, 1)
                    V.scalar_tensor_tensor(s_p[:, 2 * b + 1, :], bank[3][:, 0:384], HD ** -0.5, bias, ALU.mult, ALU.add).then_inc(sc_used, 1)
                    dve.wait_ge(sc_used, 2 * i + 2)
                    for c in range(2):
                        for q in range(2):
                            last = V.tensor_reduce(mx[:, b, 2 * c + q:2 * c + q + 1], s_p[:, 2 * b + c, 128 * q:128 + 256 * q], AX.X, ALU.max)
                    link(last)
                    V.tensor_scalar(nmx[:, b, :], mx[:, b, :], -1.0, None, ALU.mult).then_inc(sc_max, 1)
                    dve.wait_ge(sc_exp, i + 1)
                    link(V.reciprocal(rr[:, b, :], sm[:, b, :]))
                    link(V.tensor_tensor(rr[:, b, :], rr[:, b, :], coef[:, :], ALU.mult))
                    for q in range(2):
                        lo, hi = 128 * q, 128 + 256 * q
                        v = s_p[:, 2 * b, lo:hi]
                        link(V.tensor_scalar(v, v, rr[:, b, q:q + 1], None, ALU.mult))
                        last = V.scalar_tensor_tensor(v, s_p[:, 2 * b + 1, lo:hi], rr[:, b, 2 + q:3 + q], v, ALU.mult, ALU.add)
                        last.then_inc(a_set, 1)
                if 1 <= i < 5:
                    h = i - 1
                    dve.wait_ge(at_ps, h + 1)
                    if h >= 2:
                        dve.wait_ge(pv_ps, h - 1)
                    V.tensor_copy(aT_p[:, h % 2, :], bank[4][:, 0:384]).then_inc(at_set, 1)
                if 4 <= i < 12:
                    s = i - 4
                    b = s % 2
                    dve.wait_ge(ssc_ps, s + 1)
                    if s >= 2:
                        dve.wait_ge(fold_ps, s - 1)
                    V.scalar_tensor_tensor(p_s[:, b, 0:PAST], bank[2 + b][:, 0:PAST], HD ** -0.5, cst[:, C_PAST:C_PAST + PAST], ALU.mult, ALU.add)
                    link(V.scalar_tensor_tensor(p_s[:, b, PAST:320], bank[2 + b][:, PAST:320], HD ** -0.5,
                                                cst[:, C_NEW + 64 * s:C_NEW + 64 * (s + 1)], ALU.mult, ALU.add))
                    link(V.tensor_reduce(msx[:, b:b + 1], p_s[:, b, :], AX.X, ALU.max))
                    V.tensor_scalar(nms[:, b:b + 1], msx[:, b:b + 1], -1.0, None, ALU.mult).then_inc(ssc_max, 1)
                if 5 <= i < 13:
                    s = i - 5
                    dve.wait_ge(fold_ps, s + 1)
                    if s >= 2:
                        dve.wait_ge(spv_ps, s - 1)
                    V.tensor_copy(a_s[:, s % 2, 0:64], bank[4][:, 0:64])
                    V.tensor_copy(a_s[0:64, s % 2, 64:96], bank[4][0:64, 64:96]).then_inc(fold_set, 1)
                if 4 <= i < 12:
                    s = i - 4
                    b = s % 2
                    dve.wait_ge(ssc_exp, s + 1)
                    link(V.reciprocal(rrs[:, b:b + 1], ss[:, b:b + 1]))
                    link(V.tensor_tensor(rrs[:, b:b + 1], rrs[:, b:b + 1], coef_s[:, :], ALU.mult))
                    V.tensor_scalar(p_s[:, b, :], p_s[:, b, :], rrs[:, b:b + 1], None, ALU.mult).then_inc(ss_set, 1)
                if 3 <= i < 11:
                    s = i - 3
                    dve.wait_ge(kt_ps, 2 * s + 2)
                    if s >= 1:
                        dve.wait_ge(ssc_ps, s)
                    V.tensor_copy(k_t[:, :, PAGE:PAST], four(bank[5], P)).then_inc(kt_v, 1)
            def sample_outputs(n):
                dve.wait_ge(ot_ps, n + 1)
                for h in range(H):
                    V.tensor_copy(oT[:, h, PROMPT + 32 * n:PROMPT + 32 * (n + 1)].rearrange("p (s q) -> p s q", s=4),
                                  bank[6 + n][:, :].rearrange("p (s r) -> p s r", s=4)[:, :, 40 * h:40 * h + 8]).then_inc(os_out, 1)

            sample_outputs(0)
            dve.wait_ge(st_ps, 1)
            for g in range(GROUPS):
                last = V.tensor_copy(lvS[0][:, g, :, 0:15], bank[5][:, 120 * g:120 * (g + 1)].rearrange("p (s j) -> p s j", s=SEQS))
            last.then_inc(st_set, 1)
            sample_outputs(1)
            dve.wait_ge(z_out, 24)
            for g in range(GROUPS):
                last = V.tensor_copy(u_new[:, g, :].rearrange("p (s j) -> p s j", s=SEQS), lvS[0][:, g, :, 15:23])
            last.then_inc(unew_set, 1)
            dve.wait_ge(std_set, 1)
            dve.wait_ge(os_out, 2 * H)
            dve.wait_ge(op_out, 2)
            link(V.reciprocal(rs[:], rs[:]))
            V.scalar_tensor_tensor(yaT[:], oT[:], gs[:, :], rs[:], ALU.mult, ALU.mult).then_inc(ya_set, 1)
            dve.wait_ge(ko_set, TILES)
            dve.wait_ge(stored, 64)
            for g in range(GROUPS):
                lev = level(g + 1)
                dve.wait_ge(win_set, g + 1)
                V.scalar_tensor_tensor(dT[:, g, 0:PROMPT], lvP[lev][:, g, 15:271], 1.0 / 2 ** (g + 1), lvP[0][:, g, 15:271], ALU.mult, ALU.subtract)
                V.scalar_tensor_tensor(dT[:, g, PROMPT:T].rearrange("p (s j) -> p s j", s=SEQS), lvS[lev][:, g, :, 15:23],
                                       1.0 / 2 ** (g + 1), lvS[0][:, g, :, 15:23], ALU.mult, ALU.subtract).then_inc(d_set, 1)
            for n, r in ((0, 15), (1, 64)):
                dve.wait_ge(u_ps, n + 1)
                V.tensor_copy(u_out[0:r, n, :], bank[2 + n][0:r, :]).then_inc(u_set, 1)
            for n in range(KD):
                dve.wait_ge(br_ps, n + 1)
                if n == 0:
                    dve.wait_ge(z_out, 28)
                V.tensor_tensor(gT[:, n, :], gT[:, n, :], bank[n % 2][:, 0:T], ALU.mult)
                V.tensor_tensor(gT[:, 8 + n, :], gT[:, 8 + n, :], bank[2 + n % 2][:, 0:T], ALU.mult).then_inc(br_mul, 1)
            dve.wait_ge(x2_here, 32)
            def layer_norm(x, t, gamma, beta, n, done):
                r = slice(0, ROWS[t])
                for k in range(2):
                    last = V.bn_stats(stats[r, t, 6 * k:6 * k + 6], x[r, t, 512 * k:512 * (k + 1)])
                link(last)
                link(V.bn_aggr(mv[r, t, :], stats[r, t, 0:12]))
                V.tensor_scalar(rstd[r, t:t + 1], mv[r, t, 1:2], EPS, None, ALU.add).then_inc(var_set, 1)
                v = x[r, t, :]
                link(V.scalar_tensor_tensor(v, v, mv[r, t, 0:1], gamma[r, :], ALU.subtract, ALU.mult))
                dve.wait_ge(sd_set, n)
                link(V.reciprocal(rstd[r, t:t + 1], rstd[r, t:t + 1]))
                V.scalar_tensor_tensor(v, v, rstd[r, t:t + 1], beta[r, :], ALU.mult, ALU.add).then_inc(done, 1)

            def columns(xT_, t, ps, done):
                dve.wait_ge(ps, 2 * t + 1)
                V.tensor_copy(xT_[:, 0:4, P * t:P * t + ROWS[t]], four(bank[2 * t], ROWS[t])).then_inc(done, 1)

            def job_out(j):
                dve.wait_ge(wo_ps, j + 1)
                for t, p, c in halves(j):
                    V.scalar_tensor_tensor(x1[0:ROWS[t], t, c], x_again[0:ROWS[t], t, c], ALPHA, bank[4 + j % 4][p, :], ALU.mult, ALU.add).then_inc(wo_used, 1)

            def norm1(t):
                dve.wait_ge(wo_used, 2 * t + 2)
                layer_norm(x1, t, ln1[:, 0, :], ln1[:, 1, :], t + 1, x1_set)

            job_out(0)
            job_out(1)
            dve.wait_ge(ln1_here, 32)
            norm1(0)
            job_out(2)
            job_out(3)
            columns(x1T, 0, x1t_ps, x1t_v)
            norm1(1)
            job_out(4)
            columns(x1T, 1, x1t_ps, x1t_v)
            norm1(2)
            columns(x1T, 2, x1t_ps, x1t_v)

            def over_last(v, n):
                return v.unsqueeze(2).to_broadcast([P, 3, n])

            def over_tiles(v, n):
                return v.unsqueeze(1).to_broadcast([P, 3, n])

            def first_max(x, n, top, cand, idx):
                link(V.tensor_reduce(top[:, :], x, AX.X, ALU.max))
                link(V.tensor_tensor(cand[:], x, over_last(top, n), ALU.is_lt))
                link(V.scalar_tensor_tensor(cand[:], cand[:], 64.0, over_tiles(iota32[:, 0:n], n), ALU.mult, ALU.add))
                link(V.tensor_reduce(idx[:, :], cand[:], AX.X, ALU.min))

            dve.wait_ge(rt_ps, 1)
            dve.wait_ge(grp_here, 32)
            lp = bank[6][:, 0:108].rearrange("p (t n) -> p t n", t=3)
            V.tensor_tensor(logits[:, 0:2, :], lp[:, 0:2, :], br_row[:, :].unsqueeze(1).to_broadcast([P, 2, 36]), ALU.add)
            link(V.tensor_tensor(logits[0:64, 2, :], lp[0:64, 2, :], br_row[0:64, :], ALU.add))
            lg = logits[:, :, 0:4]
            first_max(lg, 4, m_g, c4, g_id)
            V.tensor_tensor(dl4[:], lg, over_last(m_g, 4), ALU.subtract).then_inc(rt_dl, 1)
            link(V.tensor_tensor(oh4[:], over_tiles(iota32[:, 0:4], 4), over_last(g_id, 4), ALU.is_equal))
            for t in range(TILES):
                last = V.tensor_tensor(le_m[:, t, :].rearrange("p (g e) -> p g e", g=4), logits[:, t, 4:36].rearrange("p (g e) -> p g e", g=4),
                                       oh4[:, t, :].unsqueeze(2).to_broadcast([P, 4, 8]), ALU.mult)
            link(last)
            for t in range(TILES):
                last = V.tensor_reduce(le_s[:, t, :], le_m[:, t, :].rearrange("p (g e) -> p e g", g=4), AX.X, ALU.add)
            link(last)
            first_max(le_s[:], 8, m1, c8a, i1)
            link(V.tensor_tensor(oh8a[:], over_tiles(iota32[:, 0:8], 8), over_last(i1, 8), ALU.is_equal))
            link(V.scalar_tensor_tensor(lt8[:], oh8a[:], -3e38, le_s[:], ALU.mult, ALU.add))
            first_max(lt8[:], 8, m2, c8b, i2)
            V.tensor_tensor(ex[:, :], m2[:, :], m1[:, :], ALU.subtract).then_inc(rt_dl, 1)
            V.scalar_tensor_tensor(e1[:, :], g_id[:, :], 8.0, i1[:, :], ALU.mult, ALU.add)
            link(V.scalar_tensor_tensor(e2[:, :], g_id[:, :], 8.0, i2[:, :], ALU.mult, ALU.add))
            i32 = over_tiles(iota32, 32)
            V.tensor_tensor(E1[:], i32, over_last(e1, 32), ALU.is_equal)
            V.tensor_tensor(E2[:], i32, over_last(e2, 32), ALU.is_equal)
            V.tensor_tensor(GG[:], i32, over_last(e1, 32), ALU.is_gt)
            link(V.tensor_tensor(G2[:], i32, over_last(e2, 32), ALU.is_gt))
            V.tensor_tensor(Mt[:], E1[:], E2[:], ALU.add).then_inc(m_hot, 1)
            V.tensor_tensor(GG[:], GG[:], G2[:], ALU.add).then_inc(m_hot, 1)
            dve.wait_ge(rt_exp, 2)
            link(V.tensor_reduce(s_g[:, :], dl4[:], AX.X, ALU.add))
            link(V.scalar_tensor_tensor(c1[:, :], ex[:, :], 1.0, s_g[:, :], ALU.add, ALU.mult))
            link(V.reciprocal(c1[:, :], c1[:, :]))
            link(V.tensor_tensor(c2[:, :], ex[:, :], c1[:, :], ALU.mult))
            for t in range(TILES):
                dve.wait_ge(high_set, t + 1)
                src, dst = ((slice(0, P), t), (slice(0, P), 2 + t)) if t < 2 else ((slice(0, 64), 4), (slice(64, P), 4))
                V.tensor_tensor(x_parts[dst[0], dst[1], :], x1[0:ROWS[t], t, :], x_parts[src[0], src[1], :].bitcast(F32), ALU.subtract).then_inc(low_set, 1)
            dve.wait_ge(rank_ps, 1)
            rank = bank[7][:, 0:96].rearrange("p (t n) -> p t n", t=3)
            for E, pos in ((E1, pos1), (E2, pos2)):
                V.memset(G2[64:128, 2, :], 0.0)
                link(V.tensor_tensor(G2[:, 0:2, :], E[:, 0:2, :], rank[:, 0:2, :], ALU.mult))
                link(V.tensor_tensor(G2[0:64, 2, :], E[0:64, 2, :], rank[0:64, 2, :], ALU.mult))
                link(V.tensor_reduce(pos[:, :], G2[:], AX.X, ALU.add))
            dve.wait_ge(iota_here, 16)
            for t in range(TILES):
                r = ROWS[t]
                link(V.tensor_scalar(PT[0:r, t, :], iota[0:r, :], pos1[0:r, t:t + 1], None, ALU.is_equal))
                V.scalar_tensor_tensor(PT[0:r, t, :], iota[0:r, :], pos2[0:r, t:t + 1], PT[0:r, t, :].bitcast(F32), ALU.is_equal, ALU.add).then_inc(pt_set, 1)
            dve.wait_ge(pt_set, TILES)
            V.tensor_copy(PT[64:P, 2, :], PT[0:64, 2, :].bitcast(F32)).then_inc(pt_set, 1)
            off = bank[6][:, 128:160]
            for w in range(WINDOWS):
                last = V.tensor_scalar(start_f[:, w, 0:32], off, float(WIN * w), float(PAIRS), ALU.add, ALU.min)
            link(last)
            for w in range(1, WINDOWS):
                last = V.memset(start_f[:, w, 32:33], float(PAIRS))
            link(last)
            link(V.tensor_reduce(cnt_max[:, 0:1], bank[6][:, 160:192], AX.X, ALU.max))
            link(V.tensor_scalar(cnt_max[:, 1:2], cnt_max[:, 0:1], float(WIN), None, ALU.is_gt))
            V.tensor_copy(flag[:, 0:1], cnt_max[:, 1:2])
            V.tensor_copy(start_i[:], start_f[:]).then_inc(starts_set, 1)
            for t in range(TILES):
                r = ROWS[t]
                V.tensor_scalar(CT[0:r, t, :], iota[0:r, :], pos1[0:r, t:t + 1], c1[0:r, t:t + 1], ALU.is_equal, ALU.mult)
                link(V.tensor_scalar(weighted[0:r, :], iota[0:r, :], pos2[0:r, t:t + 1], c2[0:r, t:t + 1], ALU.is_equal, ALU.mult))
                V.tensor_tensor(CT[0:r, t, :], CT[0:r, t, :], weighted[0:r, :], ALU.add).then_inc(ct_set, 1)
                dve.wait_ge(ct_set, t + 1)
            for n in range(5):
                dve.wait_ge(ga_ps, 16 + n + 1)
                V.tensor_copy(Pj[:, n, :], bank[(16 + n) % 6][:, 0:T]).then_inc(pj_set, 1)

            def pick(b, place, done):
                V.tensor_copy(xg[:, b, :].rearrange("p (k n) -> p k n", k=KD), XsT[:, :, bass.ds(place, WIN)]).then_inc(done, 1)

            def hidden(q, n, b):
                dve.wait_ge(q["sig"], n)
                V.tensor_tensor(gg[:], b[:, 0:P], sig[:], ALU.mult).then_inc(q["g"], 1)
                dve.wait_ge(q["g"], n)
                V.tensor_tensor(hh[:], gg[:], b[:, P:2 * P], ALU.mult).then_inc(q["h"], 1)

            def put(q, n, b, place):
                dve.wait_ge(q["yt"], n)
                V.tensor_copy(YsT[:, :, bass.ds(place, WIN)].rearrange("p (d c) n -> p c d n", d=2),
                              b[:, :].rearrange("p (c d n) -> p c d n", c=4, d=2)).then_inc(q["out"], 1)
                dve.wait_ge(q["out"], n)

            dve.wait_ge(pads_set, 1)
            dve.wait_ge(ga_out, 16)
            dve.wait_ge(starts_set, 1)
            pick(0, 0, main["xg"])
            pick(1, dve.value_load(start_i[0:1, 0, 1:2], min_val=0, max_val=PAIRS), main["xg"])
            def four_experts(first, place):
                for j in range(4):
                    hidden(main, first + j, bank[j % 2])
                    if j + 3 < len(place):
                        pick(j % 2, place[j + 3], main["xg"])
                    if place[j] is not None:
                        put(main, first + (j - 1), bank[4 + (j + 1) % 2], place[j])

            def place(e):
                return dve.value_load(start_i[0:1, 0, bass.ds(e, 1)], min_val=0, max_val=PAIRS)

            four_experts(1, [None] + [place(e) for e in range(6)])
            with dve.Fori(0, EARLY // 4 - 1) as i:
                four_experts(i * 4 + 5, [place(i * 4 + (3 + j)) for j in range(7)])
            four_experts(EARLY + 1, [place(e) for e in range(EARLY - 1, EXPERTS)])
            put(main, EXPERTS, bank[4 + 1], place(EXPERTS - 1))
            crowded = dve.value_load(flag[0:1, 0:1], min_val=0, max_val=1)
            with dve.If(crowded > 0):
                with dve.Fori(0, EXPERTS) as e:
                    for w in range(WINDOWS):
                        n = e * WINDOWS + (w + 1)
                        place = dve.value_load(start_i[0:1, w, bass.ds(e, 1)], min_val=0, max_val=PAIRS)
                        pick(0, place, over["xg"])
                        hidden(over, n, bank[0])
                        put(over, n, bank[4], place)
            V.memset(scratch[:, 2:3], 0.0).then_inc(moe_done, 1)

            for g in range(0, 10, 2):
                dve.wait_ge(yt_ps, g + 1)
                yt_out(V.tensor_copy, g).then_inc(yt_v, 1)
            dve.wait_ge(late_here, 80)
            for j in range(5):
                dve.wait_ge(cm_ps, j + 1)
                for t, p, c in halves(j):
                    last = V.scalar_tensor_tensor(x2[0:ROWS[t], t, c], x1[0:ROWS[t], t, c], ALPHA, bank[6 + j % 2][p, :], ALU.mult, ALU.add)
                last.then_inc(cm_used, 1)
                dve.wait_ge(cm_used, j + 1)
                if j in (1, 3, 4):
                    t = j // 2
                    layer_norm(x2, t, ln2[:, 0:D], ln2[:, D:2 * D], TILES + t + 1, x2_set)

            def gates(j):
                dve.wait_ge(pg_ps, j + 1)
                for t, p, c in halves(j):
                    V.tensor_tensor(gt[0:ROWS[t], t, c], bank[6 + j % 2][p, :], bpg[0:ROWS[t], c], ALU.add).then_inc(pg_add, 1)

            def last_norm(t):
                r = ROWS[t]
                for hf in range(2):
                    dve.wait_ge(pg_mul, 2 * t + hf + 1)
                    c = slice(512 * hf, 512 * (hf + 1))
                    last = V.scalar_tensor_tensor(x2[0:r, t, c], x2[0:r, t, c], ALPHA, gt[0:r, t, c], ALU.mult, ALU.add)
                link(last)
                layer_norm(x2, t, ln3[:, 0:D], ln3[:, D:2 * D], 2 * TILES + t + 1, y_set)

            columns(x2T, 0, x2t_ps, x2t_v)
            gates(0)
            columns(x2T, 1, x2t_ps, x2t_v)
            gates(1)
            last_norm(0)
            gates(2)
            columns(x2T, 2, x2t_ps, x2t_v)
            gates(3)
            last_norm(1)
            gates(4)
            last_norm(2)

        @block.tensor
        def _(pe):
            mm = nc.tensor.matmul

            def weights(i):
                pe.wait_ge(w_in_slot[i % RING], 16 * (i // RING + 1))

            def turn_tile(src, t, ps, ready=None):
                if ready:
                    pe.wait_ge(ready, t + 1)
                r = ROWS[t]
                for g in range(2 * t, 2 * t + 2):
                    for j in range(4):
                        k = 4 * (g % 2) + j
                        last = nc.tensor.transpose(bank[g][:, P * j:P * j + r], src[0:r, t, P * k:P * (k + 1)], ident[0:r, 0:r])
                    last.then_inc(ps, 1)

            def by_halves(b, j, xT_, first, ready=None):
                t = j // 2
                for q in range(2):
                    for k in range(KD):
                        if ready and j == 0 and q == 0:
                            pe.wait_ge(ready, k + 1)
                        for hf in ((j % 2,) if t < 2 else (0, 1)):
                            p0 = 64 * hf if t == 2 else 0
                            last = mm(b[p0:p0 + ROWS[t], 256 * q:256 * (q + 1)], xT_[:, k, P * t:P * t + ROWS[t]],
                                      unit((first + 2 * hf + q) % RING, KD)[:, k, :], start=(k == 0), stop=(k == KD - 1),
                                      tile_position=(0, p0))
                return last

            pe.wait_ge(ident_here, 16)
            pe.wait_ge(x_here, 32)
            for t in range(TILES):
                turn_tile(x_tm, t, xt_ps)
            pe.wait_ge(vec_here, 7 * 16)
            nc.tensor.transpose(bank[6][:, 0:41], vec[:, :], ident[0:41, 0:41]).then_inc(vec_ps, 1)
            pe.wait_ge(lam_prod, 1)
            pe.wait_ge(ones_set, 1)
            mm(bank[6][:, 64:66], ones[0:HD, :], lam_p[0:HD, :], start=True, stop=True).then_inc(lam_ps, 1)
            pe.wait_ge(xt_v, 3)
            pe.wait_ge(xt_a, 3)

            def z_job(j, halfway=None):
                c = j if j < 8 else j + 4
                i = c // 2
                if c % 2 == 0:
                    weights(i)
                if j >= 2:
                    pe.wait_ge(z_out, j - 1)
                for k in range(KD):
                    if k == KD // 2 and halfway:
                        halfway()
                    last = mm(bank[j % 2][:, 0:T], unit(i % RING, KD)[:, k, P * (c % 2):P * (c % 2 + 1)], xT[:, k, :],
                              start=(k == 0), stop=(k == KD - 1))
                last.then_inc(z_ps, 1)

            for j in range(8):
                z_job(j)
            for j in range(6):
                t, c = j % 3, j // 3
                if t == 0:
                    weights(4 + c)
                if j >= 2:
                    pe.wait_ge(v_out, j - 1)
                for k in range(KD):
                    last = mm(bank[2 + j % 2][0:ROWS[t], 0:256], xT[:, k, P * t:P * t + ROWS[t]], unit(4 + c, KD)[:, k, :],
                              start=(k == 0), stop=(k == KD - 1))
                last.then_inc(v_ps, 1)
            pe.wait_ge(z_out, 8)
            for t in range(TILES):
                for h in range(H):
                    last = nc.tensor.transpose(bank[4 + t][0:ROWS[t], P * h:P * (h + 1)], kT[:, h, P * t:P * t + ROWS[t]], ident)
                last.then_inc(ko_ps, 1)
            pe.wait_ge(v_out, 6)
            pe.wait_ge(ko_set, TILES)

            def prompt_scores(h):
                if h >= 1:
                    pe.wait_ge(sc_used, 2 * h)
                for c in range(2):
                    r = slice(64 * c, 64 * c + 64)
                    mm(bank[2 + c][:, 0:128], qT[r, h, 0:128], kT[r, h, 0:128], start=True, stop=True)
                    last = mm(bank[2 + c][:, 128:384], qT[r, h, 128:256], kT[r, h, 0:256], start=True, stop=True)
                last.then_inc(sc_ps, 1)

            def prompt_transposes(h):
                pe.wait_ge(a_set, 2 * h + 2)
                if h >= 1:
                    pe.wait_ge(at_set, h)
                for b in range(3):
                    last = nc.tensor.transpose(bank[4][:, P * b:P * (b + 1)], s_p[:, 2 * (h % 2), P * b:P * (b + 1)], ident)
                last.then_inc(at_ps, 1)

            def prompt_values(h):
                pe.wait_ge(at_set, h + 1)
                o = bank[6 + h // 2][:, 256 * (h % 2):256 * (h % 2 + 1)]
                hs = slice(P * h, P * (h + 1))
                A = aT_p[:, h % 2, :]
                mm(o[:, 0:128], v_tm[:, 0, hs], A[:, 0:128], start=True, stop=True)
                mm(o[:, 128:256], v_tm[:, 0, hs], A[:, 128:256], start=True, stop=False)
                mm(o[:, 128:256], v_tm[:, 1, hs], A[:, 256:384], start=False, stop=True).then_inc(pv_ps, 1)

            def keys(s, n):
                if n == 0:
                    pe.wait_ge(k_here[s % 2], 16 * PAGES * (s // 2 + 1))
                    if s >= 1:
                        pe.wait_ge(kt_v, s)
                else:
                    pe.wait_ge(kt_a, s + 1)
                for h in range(H):
                    last = nc.tensor.transpose(bank[5][:, P * h:P * (h + 1)], k_raw[:, s % 2, 512 * n + P * h:512 * n + P * (h + 1)], ident)
                last.then_inc(kt_ps, 1)

            def sample_scores(s):
                pe.wait_ge(kt_a, s + 1)
                pe.wait_ge(kt_v, s + 1)
                if s == 0:
                    pe.wait_ge(qbd_set, 8)
                    pe.wait_ge(sc_used, 8)
                if s >= 2:
                    pe.wait_ge(ssc_max, s - 1)
                for h in range(H):
                    q = qbd[:, s, 32 * h:32 * (h + 1)]
                    o = bank[2 + s % 2][32 * h:32 * (h + 1), :]
                    mm(o[:, 0:PAST], q, k_t[:, h, :], start=True, stop=True, tile_position=(0, 32 * h))
                    last = mm(o[:, PAST:320], q, kT[:, h, PROMPT:T], start=True, stop=True, tile_position=(0, 32 * h))
                last.then_inc(ssc_ps, 1)

            def sample_fold(s):
                pe.wait_ge(ss_set, s + 1)
                if s == 0:
                    pe.wait_ge(at_set, H)
                else:
                    pe.wait_ge(fold_set, s)
                fold = cst[:, C_FOLD:C_FOLD + 32]
                for c in range(2):
                    mm(bank[4][:, 32 * c:32 * (c + 1)], p_s[:, s % 2, P * c:P * (c + 1)], fold, start=True, stop=True)
                mm(bank[4][0:64, 64:96], p_s[:, s % 2, PAST:320], fold, start=True, stop=True).then_inc(fold_ps, 1)

            def sample_values(s):
                pe.wait_ge(fold_set, s + 1)
                pe.wait_ge(v_here[s % 2], 16 * PAGES * (s // 2 + 1))
                if s % 4 == 0:
                    pe.wait_ge(op_out, s // 4 + 1)
                for n in range(PAGES + 1):
                    for h in range(H):
                        o = bank[6 + s // 4][32 * h:32 * (h + 1), P * (s % 4):P * (s % 4 + 1)]
                        if n < PAGES:
                            mm(o, a_s[:, s % 2, 32 * n:32 * (n + 1)], v_raw[:, s % 2, 512 * n + P * h:512 * n + P * (h + 1)],
                               start=(n == 0), stop=False, tile_position=(0, 32 * h))
                        else:
                            last = mm(o, a_s[0:64, s % 2, 64:96], v_tm[0:64, 2, P * h:P * (h + 1)], start=False, stop=True,
                                      tile_position=(0, 32 * h))
                last.then_inc(spv_ps, 1)

            def turn_outputs(n):
                pe.wait_ge(or_set, n + 1)
                for q in range(4):
                    last = nc.tensor.transpose(bank[6 + n][:, P * q:P * (q + 1)], os_raw[:, n, P * q:P * (q + 1)], ident)
                last.then_inc(ot_ps, 1)

            pe.wait_ge(cst_here, 16)
            for i in range(14):
                if i < 4:
                    prompt_scores(i)
                if 2 <= i < 6:
                    prompt_values(i - 2)
                if 1 <= i < 5:
                    prompt_transposes(i - 1)
                if 4 <= i < 12:
                    sample_scores(i - 4)
                if 6 <= i:
                    sample_values(i - 6)
                if 5 <= i < 13:
                    sample_fold(i - 5)
                if 3 <= i < 11:
                    keys(i - 3, 0)
                if i < 12:
                    z_job(8 + i, (lambda: keys(i - 3, 1)) if 3 <= i < 11 else None)

            turn_outputs(0)
            pe.wait_ge(state_here, 16)
            pe.wait_ge(kt_v, SEQS)
            for g in range(GROUPS):
                last = nc.tensor.transpose(bank[5][:, 120 * g:120 * (g + 1)], state[0:120, P * g:P * (g + 1)], ident[0:120, 0:120])
            last.then_inc(st_ps, 1)
            z_job(20)
            turn_outputs(1)
            for j in range(21, 24):
                z_job(j)
            pe.wait_ge(sq_set, 1)
            pe.wait_ge(st_set, 1)
            pe.wait_ge(ssc_max, SEQS)
            pe.wait_ge(fold_set, SEQS)
            pe.wait_ge(kt_v, SEQS)
            for h in range(H):
                mm(bank[2 + h][:, 0:T], ones[:, :], sq[:, h, :], start=True, stop=True).then_inc(ms_ps, 1)
            for j in range(24, 28):
                z_job(j)
            pe.wait_ge(std_set, 1)
            pe.wait_ge(unew_set, 1)
            for g in range(GROUPS):
                last = nc.tensor.transpose(bank[2][0:15, P * g:P * (g + 1)], lvP[0][:, g, 256:271], ident)
            last.then_inc(u_ps, 1)
            for g in range(GROUPS):
                last = nc.tensor.transpose(bank[3][0:64, P * g:P * (g + 1)], u_new[:, g, :], ident)
            last.then_inc(u_ps, 1)
            pe.wait_ge(wgrp_here, 16)
            pe.wait_ge(st_set, 1)
            for g in range(GROUPS):
                pe.wait_ge(d_set, g + 1)
                mm(bank[4 + g][:, 0:T], w_grp[:, g, :], dT[:, g, :], start=True, stop=True).then_inc(yp_ps, 1)

            pe.wait_ge(u_set, 2)
            pe.wait_ge(yp_set, GROUPS)
            pe.wait_ge(ya_set, 1)
            pe.wait_ge(z_out, 28)
            for n in range(KD):
                i = U_BRANCH + 2 * (n // 4)
                weights(i)
                weights(i + 1)
                if n >= 2:
                    pe.wait_ge(br_mul, n - 1)
                c = slice(P * (n % 4), P * (n % 4 + 1))
                for k in range(4):
                    mm(bank[n % 2][:, 0:T], unit(i % RING, 4)[:, k, c], ypT[:, k, :], start=(k == 0), stop=(k == 3))
                for k in range(4):
                    last = mm(bank[2 + n % 2][:, 0:T], unit((i + 1) % RING, 4)[:, k, c], yaT[:, k, :], start=(k == 0), stop=(k == 3))
                last.then_inc(br_ps, 1)
            for j in range(5):
                if j == 4:
                    pe.wait_ge(wo_used, 1)
                    turn_tile(x1, 0, x1t_ps, x1_set)
                for c in range(4):
                    if j == 0 or c >= 2:
                        weights(U_WO + c)
                by_halves(bank[4 + j % 4], j, mT, U_WO, m_set).then_inc(wo_ps, 1)
            pe.wait_ge(wr_here, 32)
            for t in range(TILES):
                if t > 0:
                    turn_tile(x1, t, x1t_ps, x1_set)
                pe.wait_ge(x1t_v, t + 1)
                pe.wait_ge(x1t_a, t + 1)
                for k in range(KD):
                    last = mm(bank[6][0:ROWS[t], 36 * t:36 * (t + 1)], x1T[:, k, P * t:P * t + ROWS[t]], w_r[:, k, :],
                              start=(k == 0), stop=(k == KD - 1))
            last.then_inc(rt_ps, 1)
            pe.wait_ge(ple_here, 32)
            for t in range(TILES):
                r = ROWS[t]
                for k in range(2):
                    last = nc.tensor.transpose(bank[t][:, P * k:P * k + r], p_tm[0:r, t, P * k:P * (k + 1)], ident[0:r, 0:r])
                last.then_inc(pt_ps, 1)
            pe.wait_ge(m_hot, 2)
            b = bank[7]
            def starts(u, start, stop):
                mm(b[:, 0:96].rearrange("p (c n) -> p c n", c=3), ones[0:ROWS[u], :], GG[0:ROWS[u], u, :].unsqueeze(1).to_broadcast([ROWS[u], 3, 32]),
                   start=start, stop=stop)

            starts(0, True, False)
            starts(1, False, False)
            for u in range(TILES - 1):
                mm(b[:, 32 * (u + 1):96].rearrange("p (c n) -> p c n", n=32), ones[0:ROWS[u], :],
                   Mt[0:ROWS[u], u, :].unsqueeze(1).to_broadcast([ROWS[u], 2 - u, 32]), start=False, stop=False)
            for t in range(TILES):
                r = ROWS[t]
                mm(b[0:r, 32 * t:32 * (t + 1)], tri[0:r, 0:r], Mt[0:r, t, :], start=False, stop=False)
            starts(2, False, True)
            for o, X in ((128, GG), (160, Mt)):
                for u in range(TILES):
                    last = mm(bank[6][:, o:o + 32], ones[0:ROWS[u], :], X[0:ROWS[u], u, :], start=(u == 0), stop=(u == TILES - 1))
            last.then_inc(rank_ps, 1)
            pe.wait_ge(pt_out, TILES)
            pe.wait_ge(high_set, TILES)
            pe.wait_ge(low_set, TILES)
            for j in range(21):
                if j >= 6:
                    pe.wait_ge(ga_out, j - 5)
                if j < 16:
                    for n, (part, t) in enumerate(((0, 0), (2, 0), (1, 1), (3, 1), (4, 2))):
                        if j == 0:
                            pe.wait_ge(pt_set, t + 1 if t < 2 else 4)
                        last = mm(bank[j % 6][:, 0:320], x_parts[:, part, P * (j // 2):P * (j // 2 + 1)], PT[:, t, 320 * (j % 2):320 * (j % 2 + 1)],
                                  start=(n == 0), stop=(n == 4))
                else:
                    pe.wait_ge(ct_set, TILES)
                    for t in range(TILES):
                        r = ROWS[t]
                        last = nc.tensor.transpose(bank[j % 6][:, P * t:P * t + r], CT[0:r, t, P * (j - 16):P * (j - 15)], ident[0:r, 0:r])
                last.then_inc(ga_ps, 1)
            pe.wait_ge(pj_set, 5)

            def gate_up(q, slot, x, b, halfway=None):
                w = ring[:, slot:slot + 2, :].rearrange("p s (k n) -> p s k n", k=KD)
                for k in range(KD):
                    if k == KD // 2 and halfway:
                        halfway()
                    for f in range(2):
                        last = mm(b[WIN * f:WIN * (f + 1), 0:256].rearrange("p (s n) -> p s n", s=2), x[:, WIN * k:WIN * (k + 1)],
                                  w[:, :, k, P * f:P * (f + 1)], start=(k == 0), stop=(k == KD - 1), tile_position=(0, WIN * f))
                last.then_inc(q["gu"], 1)

            def turn_hidden(q, n):
                pe.wait_ge(q["h"], n)
                nc.tensor.transpose(bank[2][:, 0:P], hh[:], ident).then_inc(q["ht"], 1)

            def down(q, n, slot):
                pe.wait_ge(q["hT"], n)
                for f in range(2):
                    for d in range(2):
                        last = mm(bank[3][WIN * d:WIN * (d + 1), :], hT[:, WIN * f:WIN * (f + 1)],
                                  unit(slot, 2)[:, f, 512 * d:512 * (d + 1)], start=(f == 0), stop=(f == 1), tile_position=(0, WIN * d))
                last.then_inc(q["y"], 1)

            def turn_result(q, n, b):
                pe.wait_ge(q["ys"], n)
                for c in range(4):
                    last = nc.tensor.transpose(b[:, P * c:P * (c + 1)], y_s[:, P * c:P * (c + 1)], ident)
                last.then_inc(q["yt"], 1)

            def four_experts(first, slots, here, behind=(2, 2, 2, 2)):
                for j in range(4):
                    pe.wait_ge(main["xg"], first + j)
                    here(j, 0)
                    here(j, 1)
                    gate_up(main, slots[3 * j], xg[:, j % 2, :], bank[j % 2],
                            (lambda: turn_hidden(main, first + (j - 1))) if behind[j] > 0 else None)
                    if behind[j] > 1:
                        turn_result(main, first + (j - 2), bank[4 + j % 2])
                    if behind[j] > 0:
                        here(j - 1, 2)
                        down(main, first + (j - 1), slots[3 * j - 1])

            def in_turn(turns):
                def here(j, r):
                    if j < 0:
                        pe.wait_ge(w_in_slot[RING - 1], turns - 16)
                    else:
                        pe.wait_ge(w_in_slot[3 * j + r], turns)
                return here

            def late(j, r):
                weights(U_LATE + 3 * j + r if j >= 0 else U_PLE - 1)

            turns = 16 * (U_EXPERT // RING + 1)
            four_experts(1, list(range(RING)), in_turn(turns), (0, 1, 2, 2))
            with pe.Fori(0, EARLY // 4 - 1) as i:
                four_experts(i * 4 + 5, list(range(RING)), in_turn(i * 16 + (turns + 16)))
            weights(U_PLE)
            pe.wait_ge(starts_set, 1)
            for j in range(5):
                t = j // 2
                if j >= 2:
                    pe.wait_ge(pe_out, j - 1)
                for k in range(2):
                    for hf in ((j % 2,) if t < 2 else (0, 1)):
                        p0 = 64 * hf if t == 2 else 0
                        last = mm(bank[6 + j % 2][p0:p0 + ROWS[t], :], pT[:, k, P * t:P * t + ROWS[t]],
                                  unit(U_PLE % RING, 2)[:, k, 512 * hf:512 * (hf + 1)], start=(k == 0), stop=(k == 1), tile_position=(0, p0))
                last.then_inc(pe_ps, 1)
            four_experts(EARLY + 1, [(U_LATE + n) % RING for n in range(11)] + [(U_PLE - 1) % RING], late)
            turn_hidden(main, EXPERTS)
            turn_result(main, EXPERTS - 1, bank[4])
            weights(U_LATE + 11)
            down(main, EXPERTS, (U_LATE + 11) % RING)
            turn_result(main, EXPERTS, bank[5])
            pe.wait_ge(starts_set, 1)
            crowded = pe.value_load(flag[0:1, 0:1], min_val=0, max_val=1)
            with pe.If(crowded > 0):
                pe.wait_ge(main["out"], EXPERTS)
                pe.sem_inc(over["freed"], 1)
                with pe.Fori(0, EXPERTS) as e:
                    pe.wait_ge(over["w"], e * 48 + 48)
                    for w in range(WINDOWS):
                        n = e * WINDOWS + (w + 1)
                        pe.wait_ge(over["xg"], n)
                        gate_up(over, 9, xg[:, 0, :], bank[0])
                        turn_hidden(over, n)
                        down(over, n, 11)
                        turn_result(over, n, bank[4])
                    pe.sem_inc(over["freed"], 1)

            pe.wait_ge(moe_done, 1)
            for g in range(10):
                if g >= 6:
                    m = g - 6
                    pe.wait_ge(yt_v if m % 2 == 0 else yt_a, m // 2 + 1)
                for j in range(4):
                    k = 4 * (g % 2) + j
                    last = nc.tensor.transpose(bank[g % 6][:, P * j:P * (j + 1)], YsT[:, k, P * (g // 2):P * (g // 2 + 1)], ident)
                last.then_inc(yt_ps, 1)
            pe.wait_ge(yt_v, 5)
            pe.wait_ge(yt_a, 5)
            pe.wait_ge(pe_out, 6)
            for j in range(5):
                t = j // 2
                if j >= 2:
                    pe.wait_ge(cm_used, j - 1)
                for n in range(5):
                    for hf in ((j % 2,) if t < 2 else (0, 1)):
                        p0 = 64 * hf if t == 2 else 0
                        last = mm(bank[6 + j % 2][p0:p0 + ROWS[t], :], Pj[:, n, P * t:P * t + ROWS[t]], Yj[:, n, 512 * hf:512 * (hf + 1)],
                                  start=(n == 0), stop=(n == 4), tile_position=(0, p0))
                last.then_inc(cm_ps, 1)
            for c in range(4):
                weights(U_GATE + c)
            pe.wait_ge(cm_used, 5)
            for j in range(5):
                t = j // 2
                if j in (0, 1, 3):
                    n = (j + 1) // 2
                    turn_tile(x2, n, x2t_ps, x2_set)
                pe.wait_ge(x2t_v, t + 1)
                pe.wait_ge(x2t_a, t + 1)
                if j >= 2:
                    pe.wait_ge(pg_add, j - 1)
                by_halves(bank[6 + j % 2], j, x2T, U_GATE).then_inc(pg_ps, 1)


_INS = ['x_prompt', 'x_sample', 'p_prompt', 'p_sample', 'cache_k', 'cache_v', 'state_pool', 'page_table', 'w_in', 'b_in',
        'lam_q1', 'lam_k1', 'lam_q2', 'lam_k2', 'g_sub', 'w_pool_grp', 's_pool', 'w_pool_br', 'w_attn_br', 'w_o', 'ln1_g',
        'ln1_b', 'w_rg', 'b_rg', 'w_re', 'b_re', 'w_gate', 'w_up', 'w_down', 'ln2_g', 'ln2_b', 'w_ple_gate', 'b_ple_gate',
        'w_ple', 'ln3_g', 'ln3_b']
_OUTS = [('y_prompt', (1, 256, 1024)), ('y_sample', (8, 8, 1024)), ('new_k_prompt', (1, 1, 256, 4, 128)),
         ('new_v_prompt', (1, 1, 256, 4, 128)), ('new_pool_prompt', (1, 1, 15, 512)), ('new_k_sample', (1, 8, 8, 4, 128)),
         ('new_v_sample', (1, 8, 8, 4, 128)), ('new_pool_sample', (1, 8, 15, 512))]


def kernel(**inputs):
    import numpy as _np
    import concourse.bacc as _bacc
    from concourse import mybir as _mybir
    from concourse.bass_utils import run_bass_kernel_spmd as _run

    nc = _bacc.Bacc("TRN2", target_bir_lowering=False, num_devices=1)
    arrays, args = {}, {}
    cst, iota = constant_tables()
    named = {n: _np.ascontiguousarray(inputs[n]) for n in _INS}
    named["cst"], named["iota"] = cst, iota
    for name, arr in named.items():
        arrays[f"in_{name}_dram"] = arr
        args[name] = nc.dram_tensor(f"in_{name}_dram", arr.shape, _mybir.dt.from_np(arr.dtype), kind="ExternalInput").ap()
    for name, shape in _OUTS:
        args[name] = nc.dram_tensor(f"out_{name}_dram", shape, F32, kind="ExternalOutput").ap()
    hybrid_step(nc, args)
    r = _run(nc, [arrays], core_ids=[0])
    return tuple(r.results[0][f"out_{name}_dram"] for name, _ in _OUTS)
```

```python
from contextlib import ExitStack

import concourse.bass as bass
from concourse import mybir
import math
import numpy as np

F32 = mybir.dt.float32
I32 = mybir.dt.int32
F32R = mybir.dt.float32r
ALU = mybir.AluOpType
ACT = mybir.ActivationFunctionType
AX = mybir.AxisListType

P = 128
D = 1024
KD = D // P
PROMPT = 256
SEQS, NEW = 8, 8
T = PROMPT + SEQS * NEW
TILES = 3
ROWS = [128, 128, 64]
H, HD = 4, 64
PAST, PAGE = 256, 128
PAGES = PAST // PAGE
N_PHYS = 20
POOL, GROUPS, STATE = 512, 4, 15
EXPERTS, EG, EE, FF = 32, 4, 8, 256
WIN = 64
PAIRS = 2 * T
SORTED = PAIRS + WIN
WINDOWS = T // WIN
PLE = 256
EPS = 1e-5
ALPHA = 2.0 ** 0.25
LAM_INIT = 0.8 - 0.6 * math.exp(0.0)
MASKED = -1e30
SLOPES = [2.0 ** (-8.0 * (h + 1) / H) for h in range(H)]

UNIT = 2048
RING = 12
FRONT = 6
W_IN_ORDER = [2, 3, 4, 5, 6, 7, 8, 9, 10, 11, 12, 13, 0, 1, 14, 15]
U_BRANCH = 16
U_WO = 20
U_EXPERT = 24
EARLY = EXPERTS - 4
U_PLE = U_EXPERT + 3 * EARLY
U_LATE = U_PLE + 1
U_GATE = U_LATE + 12

Z_JOBS = 32


def slot_of(i):
    if i < U_BRANCH:
        return i % FRONT
    if i < U_EXPERT:
        return (4, 5, 0, 1, 2, 3, 4, 5)[i - U_BRANCH]
    return i % RING


def turn_of(i):
    return sum(slot_of(m) == slot_of(i) for m in range(i + 1))


C_IDENT = 0
C_TRI = C_IDENT + 128
C_PROMPT = C_TRI + 128
C_PAST = C_PROMPT + H * 384
C_NEW = C_PAST + PAST
C_FOLD = C_NEW + SEQS * 64
C_COUNT = C_FOLD + 32
C_IOTA = C_COUNT + GROUPS * 16
C_ROW = C_IOTA + 32
C_END = C_ROW + 2


def constant_tables():
    c = np.zeros((P, C_END), np.float32)
    p = np.arange(P)[:, None]
    c[:, C_IDENT:C_IDENT + 128] = np.eye(P)
    c[:, C_TRI:C_TRI + 128] = p < np.arange(P)[None, :]
    j = np.arange(384)[None, :]
    dist = np.where(j < 128, p - j, p + 128 - (j - 128))
    for h in range(H):
        c[:, C_PROMPT + 384 * h:C_PROMPT + 384 * (h + 1)] = np.where(dist >= 0, -SLOPES[h] * dist, MASKED)
    h, r = p // 32, p % 32
    q, used = r % 8, r < 16
    slope = np.array(SLOPES)[h]
    c[:, C_PAST:C_PAST + PAST] = np.where(used, -slope * (PAST + q - np.arange(PAST)[None, :]), 0.0)
    key = np.arange(64)[None, :]
    for s in range(SEQS):
        d = q - key % NEW
        ok = (key // NEW == s) & (d >= 0)
        c[:, C_NEW + 64 * s:C_NEW + 64 * (s + 1)] = np.where(used, np.where(ok, -slope * d, MASKED), 0.0)
    c[:, C_FOLD:C_FOLD + 32] = used & (np.arange(32)[None, :] == 8 * h + q)
    for g in range(GROUPS):
        w = 2 ** (g + 1)
        c[:, C_COUNT + 16 * g:C_COUNT + 16 * (g + 1)] = [w / min(i + 1, w) for i in range(16)]
    c[:, C_IOTA:C_IOTA + 32] = np.arange(32)
    c[:, C_ROW] = (used & (r < 8))[:, 0]
    c[:, C_ROW + 1] = (used & (r >= 8))[:, 0]
    iota = np.broadcast_to(np.arange(PAIRS, dtype=np.float32), (P, PAIRS)).copy()
    return c, iota


def hybrid_step(nc, a):
    ctx = ExitStack()
    with ctx:
        def fixed(name, shape, dt=F32):
            return ctx.enter_context(nc.sbuf_tensor(name, shape, dt))

        def sem(name):
            return ctx.enter_context(nc.semaphore(name))

        RING_AT = -(-nc.sbuf_base // 32) * 32
        ring = fixed("ring", [P, RING, UNIT])
        cst = fixed("cst", [P, C_END])
        ones = fixed("ones", [P, P])
        br_row = fixed("br_row", [P, 36])
        vec = fixed("vec", [41, P])
        col = fixed("col", [P, 41])
        misc = fixed("misc", [P, 64])
        arena_bytes = 95488
        ARENA = -(-nc.sbuf_base // 32) * 32
        arena = fixed("arena", [P, arena_bytes // 4])

        def rounded(name, off, shape):
            return nc.alloc_sbuf_tensor_at(name, shape, F32R, offset=ARENA + off)

        def rounded_in_ring(name, slot, shape):
            return nc.alloc_sbuf_tensor_at(name, shape, F32R, offset=RING_AT + 4 * UNIT * slot)


        def at(off, shape, dt=F32):
            n = int(np.prod(shape[1:]))
            v = arena[:, off // 4:off // 4 + n]
            if dt != F32:
                v = v.bitcast(dt)
            if len(shape) == 3:
                v = v.rearrange("p (a b) -> p a b", a=shape[1])
            if len(shape) == 4:
                v = v.rearrange("p (a b c) -> p a b c", a=shape[1], b=shape[2])
            return v

        x_high = rounded("x_high", 0, [P, KD, T])
        x_low = rounded_in_ring("x_low", 6, [P, KD, T])
        w_high = rounded_in_ring("w_high", 8, [P, 4, KD, P])
        w_low = rounded_in_ring("w_low", 10, [P, 4, KD, P])
        qT = at(10240, [P, H, T])
        kT = at(15360, [P, H, T])
        v_tm = at(20480, [P, TILES, 512])
        gT = at(26624, [P, 16, T])
        x_tm = at(47104, [P, TILES, D])
        k_raw = at(47104, [P, 2, PAGES * 512])
        k_t = at(55296, [P, H, PAST])
        v_raw = at(59392, [P, 2, PAGES * 512])
        qbd = at(67584, [P, SEQS, H * 32])
        p_s = at(71680, [P, 2, 320])
        a_s = at(74240, [P, 2, 96])
        s_p = at(75008, [P, 4, 384])
        aT_p = at(81152, [P, 2, 384])
        k_out = at(84224, [P, TILES, 512])
        oT = at(90368, [P, H, T])
        sq = at(75008, [P, H, T])
        os_raw = at(75008, [P, 2, 512])
        vT = at(90368, [P, H, T])
        rs = at(47104, [P, H, T])
        state = at(81152, [P, 512])
        lv = [at(52224 + 7280 * i, [P, 1820]) for i in range(3)]
        lvP = [x[:, 0:GROUPS * 271].rearrange("p (g j) -> p g j", g=GROUPS) for x in lv]
        lvS = [x[:, GROUPS * 271:1820].rearrange("p (g s j) -> p g s j", g=GROUPS, s=SEQS) for x in lv]
        dT = at(84224, [P, GROUPS, T])
        u_out = at(75008, [P, 2, 512])
        w_grp = at(79104, [P, GROUPS, P])
        u_new = at(83200, [P, 4, 64])
        yaT = at(10240, [P, H, T])
        ya_high = rounded("ya_high", 15360, [P, H, T])
        ya_low = rounded_in_ring("ya_low", 6, [P, H, T])
        yp_high = nc.alloc_sbuf_tensor_at("yp_high", [P, GROUPS, T], F32R, offset=RING_AT + 4 * (UNIT * 6 + H * T))
        yp_low = nc.alloc_sbuf_tensor_at("yp_low", [P, GROUPS, T], F32R, offset=RING_AT + 4 * (UNIT * 6 + 2 * H * T))
        mT = at(0, [P, KD, T])
        m_high = [rounded(f"m_high{n}", off, [P, 4, T + ROWS[2]]) for n, off in enumerate((68864, 20480))]
        m_low = rounded("m_low", 0, [P, KD, T])
        wo_high = rounded_in_ring("wo_high", 8, [P, 4, KD, 256])
        wo_low = rounded_in_ring("wo_low", slot_of(U_WO), [P, 4, KD, 256])
        x_again = at(47104, [P, TILES, D])
        ln1 = at(59520, [P, 2, D])
        x1 = at(26624, [P, TILES, D])
        x1T = at(10240, [P, KD, T])
        w_r = at(67712, [P, KD, 36])
        XsT = at(38912, [P, KD, SORTED])
        PT = rounded("permutation", 61440, [P, TILES, PAIRS])
        x_parts = rounded("x_parts", 0, [P, 5, D])
        CT = at(69120, [P, TILES, PAIRS])
        YsT = at(61440, [P, KD, SORTED])
        p_tm = at(84992, [P, TILES, PLE])
        xg = at(88064, [P, 2, KD * WIN])
        weighted = at(88064, [P, PAIRS])
        iota = at(92160, [P, PAIRS])
        Pj = at(0, [P, 5, T])
        pe_s = at(10240, [P, TILES, D])
        pT = at(22528, [P, 2, T])
        sig, gg, hh = (at(25088 + 512 * i, [P, P]) for i in range(3))
        hT = at(8448, [P, P])
        y_s = at(6400, [P, 512])
        Yj = at(38912, [P, 5, D])
        x2 = at(61440, [P, TILES, D])
        x2_high = rounded("x2_high", 73728, [P, KD, T + ROWS[2]])
        x2_low = rounded("x2_low", 86016, [P, KD, PROMPT])
        gw_high = rounded_in_ring("gw_high", 8, [P, 4, KD, 256])
        gw_low = rounded_in_ring("gw_low", U_GATE % RING, [P, 4, KD, 256])
        gt = at(38912, [P, TILES, D])
        ln2, ln3, bpg = ring[:, 5, :], ring[:, 6, :], ring[:, 7, 0:D]
        small = fixed("small", [P, 1330])
        cursor = [0]

        def tiny(*shape):
            n = int(np.prod(shape))
            v = small[:, cursor[0]:cursor[0] + n]
            cursor[0] += n
            assert cursor[0] <= 1330, cursor[0]
            if len(shape) == 2:
                v = v.rearrange("p (a b) -> p a b", a=shape[0])
            return v

        logits = tiny(3, 36)
        c4, c8a, c8b, oh8a, le_s = tiny(3, 4), tiny(3, 8), tiny(3, 8), tiny(3, 8), tiny(3, 8)
        oh4, dl4, lt8 = tiny(3, 4), tiny(3, 4), tiny(3, 8)
        le_m = tiny(3, 32)
        E1, E2, GG, G2 = tiny(3, 32), tiny(3, 32), tiny(3, 32), tiny(3, 32)
        Mt = c_rank = tiny(3, 32)
        m_g, g_id, s_g, m1, i1, m2, i2, ex, c1, c2, e1, e2, pos1, pos2 = (tiny(3) for _ in range(14))
        start_f = tiny(WINDOWS, 33)
        start_i = tiny(WINDOWS, 33).bitcast(I32)
        cnt_max = tiny(2)
        flag = tiny(2).bitcast(I32)
        stats, mv = tiny(3, 12), tiny(3, 2)
        rstd = tiny(4)
        mx, nmx, sm, rr = tiny(2, 4), tiny(2, 4), tiny(2, 4), tiny(2, 4)
        msx, nms, ss, rrs = tiny(2), tiny(2), tiny(2), tiny(2)
        coef, coef_s, lam_p, lam_e, neg_lam, gs, eps = tiny(4), tiny(1), tiny(2), tiny(2), tiny(1), tiny(1), tiny(1)
        pages = fixed("pages", [1, SEQS * PAGES], I32)
        scratch = misc[:, 0:4]

        bank = [ctx.enter_context(nc.psum_tensor(f"bank{i}", [P, 512], F32)) for i in range(8)]

        ident = cst[:, C_IDENT:C_IDENT + P]
        tri = cst[:, C_TRI:C_TRI + P]
        iota32 = cst[:, C_IOTA:C_IOTA + 32]

        w_in_slot = [sem(f"w_in_slot{i}") for i in range(RING)]
        x_here, ident_here, cst_here, vec_here, grp_here = map(sem, ("x_here", "ident_here", "cst_here", "vec_here", "grp_here"))
        wgrp_here = sem("wgrp_here")
        pages_here, vec_zero, ones_set, qbd_zero = map(sem, ("pages_here", "vec_zero", "ones_set", "qbd_zero"))
        xt_ps, xh_set, xl_set, wh_set, wl_set = map(sem, ("xt_ps", "xh_set", "xl_set", "wh_set", "wl_set"))
        vec_ps, col_set, lam_ps, lam_exp = map(sem, ("vec_ps", "col_set", "lam_ps", "lam_exp"))
        z_ps, z_out, v_ps, v_out, qbd_set = map(sem, ("z_ps", "z_out", "v_ps", "v_out", "qbd_set"))
        ko_ps, ko_set = map(sem, ("ko_ps", "ko_set"))
        sc_ps, sc_used, sc_max, sc_exp, a_set, at_ps, at_set, pv_ps, op_out = map(
            sem, ("sc_ps", "sc_used", "sc_max", "sc_exp", "a_set", "at_ps", "at_set", "pv_ps", "op_out"))
        k_here, v_here = [sem(f"k_here{i}") for i in range(2)], [sem(f"v_here{i}") for i in range(2)]
        kt_ps, kt_a, kt_v = map(sem, ("kt_ps", "kt_a", "kt_v"))
        ssc_ps, ssc_max, ssc_exp, ss_set, fold_ps, fold_set, spv_ps, os_out = map(
            sem, ("ssc_ps", "ssc_max", "ssc_exp", "ss_set", "fold_ps", "fold_set", "spv_ps", "os_out"))
        or_set, ot_ps = map(sem, ("or_set", "ot_ps"))
        sq_set, ms_ps, std_set, ya_set = map(sem, ("sq_set", "ms_ps", "std_set", "ya_set"))
        state_here, st_ps, st_set, pre_zero, win_set, win_step, d_set, u_ps, u_set, unew_set = map(
            sem, ("state_here", "st_ps", "st_set", "pre_zero", "win_set", "win_step", "d_set", "u_ps", "u_set", "unew_set"))
        yp_ps, y_high, y_low, br_ps, br_mul, m_set = map(sem, ("yp_ps", "y_high", "y_low", "br_ps", "br_mul", "m_set"))
        x2_here, ln1_here, wo_ps, wo_used = map(sem, ("x2_here", "ln1_here", "wo_ps", "wo_used"))
        var_set, sd_set, x1_set = map(sem, ("var_set", "sd_set", "x1_set"))
        x1t_ps, x1t_v, x1t_a, wr_here, rt_ps = map(sem, ("x1t_ps", "x1t_v", "x1t_a", "wr_here", "rt_ps"))
        rt_dl, rt_exp, m_hot, rank_ps, pt_set, ct_set, starts_set = map(
            sem, ("rt_dl", "rt_exp", "m_hot", "rank_ps", "pt_set", "ct_set", "starts_set"))
        iota_here, ple_here, pt_ps, pt_out, pe_ps, pe_out = map(sem, ("iota_here", "ple_here", "pt_ps", "pt_out", "pe_ps", "pe_out"))
        ga_ps, ga_out, pj_set, pads_set, high_set, low_set = map(sem, ("ga_ps", "ga_out", "pj_set", "pads_set", "high_set", "low_set"))
        steps = ("xg", "gu", "sig", "g", "h", "ht", "hT", "y", "ys", "yt", "out")
        main = {n: sem("main_" + n) for n in steps}
        over = {n: sem("over_" + n) for n in steps + ("w", "freed")}
        moe_done = sem("moe_done")
        yt_ps, yt_v, yt_a, cm_ps, cm_used = map(sem, ("yt_ps", "yt_v", "yt_a", "cm_ps", "cm_used"))
        x2t_ps, x2t_v, x2t_a, pg_ps, pg_add, pg_sig, pg_mul = map(
            sem, ("x2t_ps", "x2t_v", "x2t_a", "pg_ps", "pg_add", "pg_sig", "pg_mul"))
        late_here, y_set, x2_set = map(sem, ("late_here", "y_set", "x2_set"))
        stored = sem("stored")
        chain_v = sem("chain_v")

        win_d = a["w_in"].rearrange("l (k p) (c n) -> (l c) p k n", p=P, n=256)
        pbr_d = a["w_pool_br"].rearrange("l (k p) (c n) -> (l c) p k n", p=P, n=512)
        abr_d = a["w_attn_br"].rearrange("l (k p) (c n) -> (l c) p k n", p=P, n=512)
        wo_d = a["w_o"].rearrange("l (k p) (c n) -> (l c) p k n", p=P, n=256)
        wg_d = a["w_gate"].rearrange("l g e (k p) f -> (l g e) p k f", p=P)
        wu_d = a["w_up"].rearrange("l g e (k p) f -> (l g e) p k f", p=P)
        wd_d = a["w_down"].rearrange("l g e (k p) d -> (l g e) p k d", p=P)
        pg_d = a["w_ple_gate"].rearrange("l (k p) (c n) -> (l c) p k n", p=P, n=256)
        ck_d = a["cache_k"].rearrange("l n p h d -> (l n) p (h d)")
        cv_d = a["cache_v"].rearrange("l n p h d -> (l n) p (h d)")
        xp_d = a["x_prompt"].rearrange("b (t p) d -> p (b t) d", p=P)
        xs_d = a["x_sample"].rearrange("s t d -> (s t) d")
        pp_d = a["p_prompt"].rearrange("l b (t p) d -> p (l b t) d", p=P)
        ps_d = a["p_sample"].rearrange("l s t d -> (l s t) d")

        def unit(slot, k):
            return ring[:, slot, :].rearrange("p (k n) -> p k n", k=k)

        def level(n):
            return 0 if n == 0 else 2 - n % 2

        def halves(j):
            t = j // 2
            if t < 2:
                return [(t, slice(0, P), slice(512 * (j % 2), 512 * (j % 2 + 1)))]
            return [(t, slice(64 * hf, 64 * hf + 64), slice(512 * hf, 512 * (hf + 1))) for hf in range(2)]

        PAIR_BANKS = (4, 5, 6, 2, 3)

        def yt_out(copy, g):
            return copy(Yj[:, g // 2, 512 * (g % 2):512 * (g % 2 + 1)], bank[g % 6][:, :])

        block = ctx.enter_context(nc.Block())

        @block.sync
        def _(sp):
            def wait_used(i):
                if i < U_BRANCH:
                    sp.wait_ge(wl_set, 2 * i + 2)
                elif i < U_WO:
                    sp.wait_ge(wl_set, Z_JOBS + 4 * ((i - U_BRANCH) // 2 + 1))
                elif i < U_EXPERT:
                    sp.wait_ge(wo_ps, 6)
                elif i == U_PLE:
                    sp.wait_ge(pe_ps, 5)
                else:
                    e, r = divmod(i - U_EXPERT - (i > U_PLE), 3)
                    sp.wait_ge(main["gu"] if r < 2 else main["y"], e + 1)

            def load(i, src, k):
                before = [m for m in range(i) if slot_of(m) == slot_of(i)]
                if before:
                    wait_used(before[-1])
                elif i >= U_BRANCH:
                    sp.wait_ge(br_ps, KD)
                sp.dma_start(unit(slot_of(i), k), src).then_inc(w_in_slot[slot_of(i)], 16)

            sp.dma_start(cst[:, 0:P], a["cst"][:, 0:P]).then_inc(ident_here, 16)
            sp.dma_start(x_tm[:, 0:2, :], xp_d).then_inc(x_here, 16)
            sp.dma_start(x_tm[0:64, 2, :], xs_d).then_inc(x_here, 16)
            sp.wait_ge(vec_zero, 1)
            sp.dma_start(vec[0:32, :], a["b_in"].rearrange("l (c p) -> (l c) p", p=P)).then_inc(vec_here, 16)
            sp.dma_start(vec[32:36, :], a["s_pool"].rearrange("l (c p) -> (l c) p", p=P)).then_inc(vec_here, 16)
            sp.dma_start(vec[36:37, :], a["g_sub"]).then_inc(vec_here, 16)
            for n, name in enumerate(("lam_q1", "lam_k1", "lam_q2", "lam_k2")):
                sp.dma_start(vec[37 + n:38 + n, 0:HD], a[name]).then_inc(vec_here, 16)
            for i, c in enumerate(W_IN_ORDER):
                load(i, win_d[c], KD)
                if i == 1:
                    sp.dma_start(cst[:, P:C_END], a["cst"][:, P:C_END]).then_inc(cst_here, 16)
            for i, (w, c) in enumerate(((pbr_d, 0), (abr_d, 0), (pbr_d, 1), (abr_d, 1))):
                load(U_BRANCH + i, w[c], 4)
            for c in range(4):
                load(U_WO + c, wo_d[c], KD)
            for e in range(4):
                for r, (w, k) in enumerate(((wg_d, KD), (wu_d, KD), (wd_d, 2))):
                    load(U_EXPERT + 3 * e + r, w[e], k)
            with sp.Fori(0, EARLY // 4 - 1) as i:
                for j in range(4):
                    for r, (w, k) in enumerate(((wg_d, KD), (wu_d, KD), (wd_d, 2))):
                        slot = 3 * j + r
                        sp.wait_ge(main["gu"] if r < 2 else main["y"], i * 4 + (j + 1))
                        src = w[bass.ds(i * 4 + (j + 4), 1), :, :, :].rearrange("o p k n -> p (o k) n")
                        sp.dma_start(unit(slot, k), src).then_inc(w_in_slot[slot], 16)
            load(U_PLE, a["w_ple"].rearrange("l (k p) d -> p (l k) d", p=P), 2)
            for e in range(EARLY, EXPERTS):
                for r, (w, k) in enumerate(((wg_d, KD), (wu_d, KD), (wd_d, 2))):
                    load(U_LATE + 3 * (e - EARLY) + r, w[e], k)
            for c in range(4):
                load(U_GATE + c, pg_d[c], KD)
            wait_used(U_GATE + 5 - RING)
            wait_used(U_GATE + 6 - RING)
            for n, name in enumerate(("ln2_g", "ln2_b", "ln3_g", "ln3_b")):
                dst = (ln2, ln3)[n // 2][:, (n % 2) * D:(n % 2 + 1) * D]
                sp.dma_start(dst, a[name][0].partition_broadcast(P)).then_inc(late_here, 16)
            sp.dma_start(bpg, a["b_ple_gate"][0].partition_broadcast(P)).then_inc(late_here, 16)
            sp.wait_ge(starts_set, 1)
            crowded = sp.value_load(flag[0:1, 0:1], min_val=0, max_val=1)
            with sp.If(crowded > 0):
                with sp.Fori(0, EXPERTS) as e:
                    sp.wait_ge(over["freed"], e + 1)
                    for r, (w, k) in enumerate(((wg_d, KD), (wu_d, KD), (wd_d, 2))):
                        src = w[bass.ds(e, 1), :, :, :].rearrange("o p k n -> p (o k) n")
                        sp.dma_start(unit(9 + r, k), src).then_inc(over["w"], 16)
            yp = a["y_prompt"].rearrange("b (t p) d -> p (b t) d", p=P)
            for t in range(TILES):
                sp.wait_ge(y_set, t + 1)
                dst = yp[:, t, :] if t < 2 else a["y_sample"].rearrange("s t d -> (s t) d")
                sp.dma_start(dst, x2[0:ROWS[t], t, :]).then_inc(stored, 16)
            sp.wait_ge(stored, 16 * 10)

        @block.gpsimd
        def _(pool):
            pool.dma_start(pages[0:1, :], a["page_table"].rearrange("s n -> (s n)").unsqueeze(0)).then_inc(pages_here, 16)
            pool.memset(ones[:], 1.0).then_inc(ones_set, 1)
            pool.dma_start(br_row[:, 0:4], a["b_rg"][0].partition_broadcast(P)).then_inc(grp_here, 16)
            pool.dma_start(br_row[:, 4:36], a["b_re"].rearrange("l g e -> l (g e)")[0].partition_broadcast(P)).then_inc(grp_here, 16)
            pool.wait_ge(xt_ps, 6)
            pool.memset(qbd[:], 0.0).then_inc(qbd_zero, 1)
            pool.wait_ge(pages_here, 16)

            def load_pages(s, src, dst, here):
                for n in range(PAGES):
                    pg = pool.value_load(pages[0:1, PAGES * s + n:PAGES * s + n + 1], min_val=0, max_val=N_PHYS - 1)
                    pool.dma_start(dst[:, s % 2, 512 * n:512 * (n + 1)],
                                   src[bass.ds(pg, 1), :, :].rearrange("o p n -> p (o n)")).then_inc(here[s % 2], 16)

            for s in range(SEQS + 2):
                if s < SEQS:
                    if s >= 2:
                        pool.wait_ge(kt_ps, 2 * (s - 1))
                    load_pages(s, ck_d, k_raw, k_here)
                v = s - 2
                if v >= 0:
                    if v >= 2:
                        pool.wait_ge(spv_ps, v - 1)
                    load_pages(v, cv_d, v_raw, v_here)
                if v == 2:
                    pool.wait_ge(pv_ps, H)
                    pool.dma_start(state[0:120, :], a["state_pool"].rearrange("l s j c -> (l s j) c")).then_inc(state_here, 16)
            pool.wait_ge(os_out, 2 * H)
            pool.wait_ge(op_out, 2)
            pool.tensor_tensor(sq[:], oT[:], oT[:], ALU.mult).then_inc(sq_set, 1)
            pool.wait_ge(spv_ps, SEQS)
            pool.wait_ge(kt_v, SEQS)
            pool.memset(lvP[0][:, :, 0:15], 0.0).then_inc(pre_zero, 1)
            pool.wait_ge(pre_zero, 1)
            pool.wait_ge(ms_ps, H)
            pool.dma_start(w_grp[:], a["w_pool_grp"].rearrange("l g c e -> c (l g) e")).then_inc(wgrp_here, 16)
            pool.wait_ge(z_out, 28)
            pool.wait_ge(st_set, 1)
            for n in range(1, 5):
                src, dst, step, g = level(n - 1), level(n), 2 ** (n - 1), n - 1
                lo = 2 ** n - 1
                pool.tensor_tensor(lvP[dst][:, g:4, lo:271], lvP[src][:, g:4, lo:271], lvP[src][:, g:4, lo - step:271 - step], ALU.add).then_inc(win_step, 1)
                for gg_ in range(g, 4):
                    last = pool.tensor_tensor(lvS[dst][:, gg_, :, lo:23], lvS[src][:, gg_, :, lo:23], lvS[src][:, gg_, :, lo - step:23 - step], ALU.add)
                    last.then_inc(win_step, 1)
                total = sum(1 + 4 - k for k in range(n))
                pool.wait_ge(win_step, total)
                pool.tensor_tensor(lvP[dst][:, g, 15:31], lvP[dst][:, g, 15:31], cst[:, C_COUNT + 16 * g:C_COUNT + 16 * g + 16], ALU.mult).then_inc(win_set, 1)
            pool.wait_ge(d_set, 4)
            pool.wait_ge(ya_set, 1)
            pool.wait_ge(u_ps, 2)
            pool.wait_ge(unew_set, 1)
            pool.dma_start(x_again[:, 0:2, :], xp_d).then_inc(x2_here, 16)
            pool.dma_start(x_again[0:64, 2, :], xs_d).then_inc(x2_here, 16)
            pool.dma_start(ln1[:, 0, :], a["ln1_g"][0].partition_broadcast(P)).then_inc(ln1_here, 16)
            pool.dma_start(ln1[:, 1, :], a["ln1_b"][0].partition_broadcast(P)).then_inc(ln1_here, 16)
            pool.dma_start(w_r[:, :, 0:4], a["w_rg"].rearrange("l (k p) g -> p (l k) g", p=P)).then_inc(wr_here, 16)
            pool.dma_start(w_r[:, :, 4:36], a["w_re"].rearrange("l (k p) g e -> p (l k) (g e)", p=P)).then_inc(wr_here, 16)
            pool.dma_start(iota[:], a["iota"]).then_inc(iota_here, 16)
            pool.wait_ge(yp_ps, GROUPS)
            pool.dma_start(p_tm[:, 0:2, :], pp_d).then_inc(ple_here, 16)
            pool.dma_start(p_tm[0:64, 2, :], ps_d).then_inc(ple_here, 16)
            for n in range(KD):
                pool.wait_ge(br_mul, n + 1)
                if n == 0:
                    pool.wait_ge(z_ps, Z_JOBS)
                pool.tensor_tensor(mT[:, n, :], gT[:, n, :], gT[:, 8 + n, :], ALU.add).then_inc(m_set, 1)
            pool.wait_ge(rt_ps, 1)
            pool.wait_ge(stored, 16 * 7)
            for t in range(2):
                pool.wait_ge(high_set, t + 1)
                pool.tensor_tensor(x_parts[:, 2 + t, :], x1[:, t, :], x_parts[:, t, :].bitcast(F32), ALU.subtract).then_inc(low_set, 1)
            pool.memset(XsT[:, :, PAIRS:SORTED], 0.0).then_inc(pads_set, 1)
            pool.wait_ge(pe_out, 6)
            for t in range(TILES):
                for hf in range(2):
                    pool.wait_ge(pg_sig, 2 * t + hf + 1)
                    v = gt[0:ROWS[t], t, 512 * hf:512 * (hf + 1)]
                    pool.tensor_tensor(v, v, pe_s[0:ROWS[t], t, 512 * hf:512 * (hf + 1)], ALU.mult).then_inc(pg_mul, 1)

        @block.scalar
        def _(act):
            def four(b, rows):
                return b[:, :].rearrange("p (j n) -> p j n", j=4)[:, :, 0:rows]

            for g in range(6):
                t, hf = g // 2, g % 2
                act.wait_ge(xt_ps, g + 1)
                nc.scalar.copy(x_high[:, 4 * hf:4 * hf + 4, P * t:P * t + ROWS[t]], four(bank[g], ROWS[t])).then_inc(xh_set, 1)

            def high(j):
                if j < Z_JOBS:
                    act.wait_ge(w_in_slot[slot_of(j // 2)], 16 * turn_of(j // 2))
                    if j >= 4:
                        act.wait_ge(z_ps, j - 3)
                    nc.scalar.copy(w_high[:, j % 4], unit(slot_of(j // 2), KD)[:, :, P * (j % 2):P * (j % 2 + 1)]).then_inc(wh_set, 1)
                    return
                n = j - Z_JOBS
                if n < 4:
                    act.wait_ge(z_ps, j - 3)
                else:
                    act.wait_ge(br_ps, n - 3)
                for w in range(2):
                    i = U_BRANCH + 2 * (n // 4) + w
                    act.wait_ge(w_in_slot[slot_of(i)], 16 * turn_of(i))
                    nc.scalar.copy(w_high[:, j % 4, 4 * w:4 * w + 4], unit(slot_of(i), 4)[:, :, P * (n % 4):P * (n % 4 + 1)]).then_inc(wh_set, 1)

            def z_job(j):
                act.wait_ge(z_ps, j + 1)
                b = bank[j % 2]
                if j < 12:
                    dst = (qT, kT, vT)[j // 4][:, j % 4, :]
                    nc.scalar.activation(dst, b[:, 0:T], ACT.Identity, bias=col[:, 4 + j:5 + j]).then_inc(z_out, 1)
                elif 24 <= j < 28:
                    g = j - 24
                    if g == 0:
                        act.wait_ge(spv_ps, SEQS)
                        act.wait_ge(kt_v, SEQS)
                    nc.scalar.activation(lvP[0][:, g, 15:271], b[:, 0:PROMPT], ACT.Identity, bias=col[:, g:g + 1])
                    nc.scalar.activation(lvS[0][:, g, :, 15:23], b[:, PROMPT:T].rearrange("p (s j) -> p s j", s=SEQS),
                                         ACT.Identity, bias=col[:, g:g + 1]).then_inc(z_out, 1)
                else:
                    g = j - 12 if j < 24 else j - 16
                    nc.scalar.activation(gT[:, g, :], b[:, 0:T], ACT.Sigmoid, bias=col[:, 16 + g:17 + g]).then_inc(z_out, 1)
                high(j + 4)

            for j in range(4):
                high(j)
            act.wait_ge(col_set, 1)
            z_job(0)
            act.wait_ge(lam_ps, 1)
            nc.scalar.activation(lam_e[:, :], bank[6][:, 64:66], ACT.Exp).then_inc(lam_exp, 1)
            for j in range(1, 9):
                z_job(j)
            for t in range(TILES):
                act.wait_ge(ko_ps, t + 1)
                nc.scalar.copy(k_out[0:ROWS[t], t, :], bank[4 + t][0:ROWS[t], :]).then_inc(ko_set, 1)
            act.wait_ge(ko_set, TILES)
            act.dma_start(a["new_k_prompt"].rearrange("l b (t p) h d -> p (l b t) (h d)", p=P), k_out[:, 0:2, :]).then_inc(stored, 16)
            act.dma_start(a["new_k_sample"].rearrange("l s t h d -> (l s t) (h d)"), k_out[0:64, 2, :]).then_inc(stored, 16)
            for j in range(9, 12):
                z_job(j)

            for i in range(14):
                if i < 4:
                    act.wait_ge(sc_max, i + 1)
                    for c in range(2):
                        for q in range(2):
                            v = s_p[:, 2 * (i % 2) + c, 128 * q:128 + 256 * q]
                            last = nc.scalar.activation(v, v, ACT.Exp, bias=nmx[:, i % 2, 2 * c + q:2 * c + q + 1],
                                                        accum_out=sm[:, i % 2, 2 * c + q:2 * c + q + 1])
                    last.then_inc(sc_exp, 1)
                if 4 <= i < 12:
                    s = i - 4
                    act.wait_ge(ssc_max, s + 1)
                    v = p_s[:, s % 2, :]
                    nc.scalar.activation(v, v, ACT.Exp, bias=nms[:, s % 2:s % 2 + 1], accum_out=ss[:, s % 2:s % 2 + 1]).then_inc(ssc_exp, 1)
                if 3 <= i < 11:
                    s = i - 3
                    act.wait_ge(kt_ps, 2 * s + 1)
                    if s >= 1:
                        act.wait_ge(ssc_ps, s)
                    nc.scalar.copy(k_t[:, :, 0:PAGE], four(bank[5], P)).then_inc(kt_a, 1)
                if i == 10:
                    act.wait_ge(spv_ps, 4)
                    nc.scalar.copy(os_raw[:, 0, :], bank[6][:, :]).then_inc(or_set, 1)
                if i == 2:
                    act.wait_ge(v_out, 3)
                    act.dma_start(a["new_v_prompt"].rearrange("l b (t p) h d -> p (l b t) (h d)", p=P), v_tm[:, 0:2, :]).then_inc(stored, 16)
                    act.dma_start(a["new_v_sample"].rearrange("l s t h d -> (l s t) (h d)"), v_tm[0:64, 2, :]).then_inc(stored, 16)
                if i in (4, 6):
                    n = i // 2 - 2
                    act.wait_ge(pv_ps, 2 * n + 2)
                    nc.scalar.copy(oT[:, 2 * n:2 * n + 2, 0:PROMPT], bank[6 + n][:, :].rearrange("p (h q) -> p h q", h=2)).then_inc(op_out, 1)
                if i < 12:
                    z_job(12 + i)
            act.wait_ge(spv_ps, SEQS)
            nc.scalar.copy(os_raw[:, 1, :], bank[7][:, :]).then_inc(or_set, 1)
            for j in range(24, 28):
                z_job(j)
            act.wait_ge(ms_ps, 4)
            act.wait_ge(spv_ps, SEQS)
            for h in range(H):
                nc.scalar.activation(rs[:, h, :], bank[2 + h][:, 0:T], ACT.Sqrt, bias=eps[:, :], scale=1.0 / P).then_inc(std_set, 1)
            for j in range(28, 32):
                z_job(j)
            act.wait_ge(ya_set, 1)
            nc.scalar.copy(ya_high[:], yaT[:]).then_inc(y_high, 1)
            for g in range(GROUPS):
                act.wait_ge(yp_ps, g + 1)
                nc.scalar.activation(yp_high[:, g, :], bank[4 + g][:, 0:T], ACT.Copy, scale=col[:, 32 + g:33 + g]).then_inc(y_high, 1)
            act.wait_ge(u_set, 2)
            act.dma_start(a["new_pool_prompt"].rearrange("l b j c -> (l b j) c"), u_out[0:15, 0, :]).then_inc(stored, 16)
            act.dma_start(a["new_pool_sample"].rearrange("l s j c -> (l s) j c")[:, 7:15, :], u_out[0:64, 1, :]).then_inc(stored, 16)
            act.dma_start(a["new_pool_sample"].rearrange("l s j c -> (l s) j c")[:, 0:7, :],
                          a["state_pool"].rearrange("l s j c -> (l s) j c")[:, 8:15, :]).then_inc(stored, 16)

            def m_out(n):
                act.wait_ge(m_set, n + 1)
                nc.scalar.copy(m_high[n // 4][:, n % 4, 0:T], mT[:, n, :]).then_inc(y_high, 1)

            def high_piece(w_high_, c, first):
                act.wait_ge(w_in_slot[slot_of(first + c)], 16 * turn_of(first + c))
                nc.scalar.copy(w_high_[:, c], unit(slot_of(first + c), KD)).then_inc(wh_set, 1)

            for n in range(4):
                high(Z_JOBS + 4 + n)
                m_out(n)
            for n in range(4, KD - 1):
                m_out(n)
            act.wait_ge(br_ps, KD)
            high_piece(wo_high, 0, U_WO)
            m_out(KD - 1)
            for c in range(1, 4):
                high_piece(wo_high, c, U_WO)

            def norm(n):
                act.wait_ge(var_set, n)
                v = rstd[0:ROWS[(n - 1) % TILES], (n - 1) % TILES:(n - 1) % TILES + 1]
                nc.scalar.activation(v, v, ACT.Sqrt).then_inc(sd_set, 1)

            def columns(xT_, t, ps, done):
                act.wait_ge(ps, 2 * t + 2)
                nc.scalar.copy(xT_[:, 4:8, P * t:P * t + ROWS[t]], four(bank[2 * t + 1], ROWS[t])).then_inc(done, 1)

            for t in range(TILES):
                norm(t + 1)
                columns(x1T, t, x1t_ps, x1t_a)
                if t == 0:
                    continue
                act.wait_ge(x1_set, t)
                act.wait_ge(wo_ps, 6)
                nc.scalar.copy(x_parts[:, t - 1, :], x1[:, t - 1, :]).then_inc(high_set, 1)
            act.wait_ge(rt_dl, 1)
            nc.scalar.activation(dl4[:], dl4[:], ACT.Exp).then_inc(rt_exp, 1)
            act.wait_ge(rt_ps, 1)
            nc.scalar.copy(x_parts[0:64, 4, :], x1[0:64, 2, :]).then_inc(high_set, 1)
            act.wait_ge(rt_dl, 2)
            nc.scalar.activation(ex[:, :], ex[:, :], ACT.Exp).then_inc(rt_exp, 1)
            for t in range(TILES):
                act.wait_ge(pt_ps, t + 1)
                nc.scalar.copy(pT[:, :, P * t:P * t + ROWS[t]], four(bank[t], ROWS[t])[:, 0:2, :]).then_inc(pt_out, 1)
            for j in range(16):
                act.wait_ge(ga_ps, j + 1)
                nc.scalar.copy(XsT[:, j // 2, 320 * (j % 2):320 * (j % 2 + 1)], bank[j % 6][:, 0:320]).then_inc(ga_out, 1)

            def gate_sigmoid(q, n, b):
                act.wait_ge(q["gu"], n)
                nc.scalar.activation(sig[:], b[:, 0:P], ACT.Sigmoid).then_inc(q["sig"], 1)

            def hidden_out(q, n):
                act.wait_ge(q["ht"], n)
                nc.scalar.copy(hT[:], bank[2][:, 0:P]).then_inc(q["hT"], 1)

            def result_out(q, n):
                act.wait_ge(q["y"], n)
                nc.scalar.copy(y_s[:], bank[3][:, :]).then_inc(q["ys"], 1)

            def embedding_out(j):
                act.wait_ge(pe_ps, j + 1)
                for t, p, c in halves(j):
                    nc.scalar.copy(pe_s[0:ROWS[t], t, c], bank[6 + j % 2][p, :]).then_inc(pe_out, 1)

            def four_experts(first):
                for j in range(4):
                    hidden_out(main, first + (j - 1))
                    gate_sigmoid(main, first + j, bank[j % 2])
                    result_out(main, first + (j - 1))

            gate_sigmoid(main, 1, bank[0])
            for n in range(1, 4):
                hidden_out(main, n)
                gate_sigmoid(main, n + 1, bank[n % 2])
                result_out(main, n)
            with act.Fori(0, EARLY // 4 - 1) as i:
                four_experts(i * 4 + 5)
            for j in range(5):
                embedding_out(j)
            four_experts(EARLY + 1)
            hidden_out(main, EXPERTS)
            result_out(main, EXPERTS)
            act.wait_ge(starts_set, 1)
            crowded = act.value_load(flag[0:1, 0:1], min_val=0, max_val=1)
            with act.If(crowded > 0):
                with act.Fori(0, EXPERTS * WINDOWS) as n:
                    gate_sigmoid(over, n + 1, bank[0])
                    hidden_out(over, n + 1)
                    result_out(over, n + 1)

            for g in range(1, 10, 2):
                act.wait_ge(yt_ps, g + 1)
                yt_out(nc.scalar.copy, g).then_inc(yt_a, 1)
            for c in range(4):
                high_piece(gw_high, c, U_GATE)

            def high_columns(t):
                for g in range(2):
                    act.wait_ge(x2t_ps, 2 * t + g + 1)
                    nc.scalar.copy(x2_high[:, 4 * g:4 * g + 4, P * t:P * t + ROWS[t]], four(bank[2 * t + g], ROWS[t])).then_inc(x2t_a, 1)

            def gate_out(n):
                t, hf = n // 2, n % 2
                act.wait_ge(pg_add, n + 1)
                v = gt[0:ROWS[t], t, 512 * hf:512 * (hf + 1)]
                nc.scalar.activation(v, v, ACT.Sigmoid).then_inc(pg_sig, 1)

            norm(4)
            high_columns(0)
            norm(5)
            high_columns(1)
            gate_out(0)
            norm(6)
            gate_out(1)
            norm(7)
            high_columns(2)
            gate_out(2)
            gate_out(3)
            gate_out(4)
            norm(8)
            gate_out(5)
            norm(9)

        @block.vector
        def _(dve):
            V = nc.vector
            count = [0]

            def link(ins):
                count[0] += 1
                ins.then_inc(chain_v, 1)
                dve.wait_ge(chain_v, count[0])

            def four(b, rows):
                return b[:, :].rearrange("p (j n) -> p j n", j=4)[:, :, 0:rows]

            V.memset(vec[:], 0.0).then_inc(vec_zero, 1)
            V.memset(eps[:, :], EPS)
            V.memset(start_f[:, :, 32:33], float(PAIRS))
            V.memset(coef[:, :], 1.0)
            V.memset(rstd[:, :], 1.0)
            link(V.memset(logits[:], 0.0))
            for g in range(6):
                t, hf = g // 2, g % 2
                dve.wait_ge(xh_set, g + 1)
                c = (slice(None), slice(4 * hf, 4 * hf + 4), slice(P * t, P * t + ROWS[t]))
                V.tensor_tensor(x_low[c], four(bank[g], ROWS[t]), x_high[c].bitcast(F32), ALU.subtract).then_inc(xl_set, 1)

            def low(j):
                if j < Z_JOBS:
                    dve.wait_ge(wh_set, j + 1)
                    V.tensor_tensor(w_low[:, j % 4], unit(slot_of(j // 2), KD)[:, :, P * (j % 2):P * (j % 2 + 1)],
                                    w_high[:, j % 4].bitcast(F32), ALU.subtract).then_inc(wl_set, 1)
                    return
                n = j - Z_JOBS
                for w in range(2):
                    i = U_BRANCH + 2 * (n // 4) + w
                    dve.wait_ge(wh_set, Z_JOBS + 2 * n + w + 1)
                    last = V.tensor_tensor(w_low[:, j % 4, 4 * w:4 * w + 4], unit(slot_of(i), 4)[:, :, P * (n % 4):P * (n % 4 + 1)],
                                           w_high[:, j % 4, 4 * w:4 * w + 4].bitcast(F32), ALU.subtract)
                last.then_inc(wl_set, 1)

            low(0)
            dve.wait_ge(vec_ps, 1)
            link(V.tensor_copy(col[:, :], bank[6][:, 0:41]))
            V.tensor_scalar(gs[:, :], col[:, 36:37], 1.0 - LAM_INIT, None, ALU.mult).then_inc(col_set, 1)
            lv4 = col[0:HD, 37:41].rearrange("p (a b) -> p a b", b=2)
            V.tensor_tensor(lam_p[0:HD, :], lv4[:, :, 0], lv4[:, :, 1], ALU.mult).then_inc(col_set, 1)
            for j in range(1, 4):
                low(j)
            dve.wait_ge(lam_exp, 1)
            link(V.tensor_tensor(neg_lam[:, :], lam_e[:, 1:2], lam_e[:, 0:1], ALU.subtract))
            link(V.tensor_scalar(neg_lam[:, :], neg_lam[:, :], -LAM_INIT, None, ALU.add))
            dve.wait_ge(cst_here, 16)
            V.tensor_scalar(coef[:, 2:4], coef[:, 2:4], neg_lam[:, :], None, ALU.mult)
            link(V.scalar_tensor_tensor(coef_s[:, :], cst[:, C_ROW + 1:C_ROW + 2], neg_lam[:, :], cst[:, C_ROW:C_ROW + 1], ALU.mult, ALU.add))
            for j in range(4, 9):
                low(j)

            dve.wait_ge(qbd_zero, 1)
            dve.wait_ge(z_out, 4)
            for c in range(2):
                dst = qbd[64 * c:64 * c + 64, :, :].rearrange("p s (h r) -> p h s r", h=H)[:, :, :, 8 * c:8 * c + 8]
                src = qT[64 * c:64 * c + 64, :, PROMPT:T].rearrange("p h (s t) -> p h s t", s=SEQS)
                for h in range(H):
                    last = V.tensor_copy(dst[:, h], src[:, h])
                    last.then_inc(qbd_set, 1)
            for j in range(9, 15):
                low(j)

            for i in range(14):
                if i < 4:
                    h, b = i, i % 2
                    dve.wait_ge(sc_ps, i + 1)
                    if i >= 2:
                        dve.wait_ge(at_ps, i - 1)
                    bias = cst[:, C_PROMPT + 384 * h:C_PROMPT + 384 * (h + 1)]
                    V.scalar_tensor_tensor(s_p[:, 2 * b, :], bank[2][:, 0:384], HD ** -0.5, bias, ALU.mult, ALU.add).then_inc(sc_used, 1)
                    V.scalar_tensor_tensor(s_p[:, 2 * b + 1, :], bank[3][:, 0:384], HD ** -0.5, bias, ALU.mult, ALU.add).then_inc(sc_used, 1)
                    dve.wait_ge(sc_used, 2 * i + 2)
                    for c in range(2):
                        for q in range(2):
                            last = V.tensor_reduce(mx[:, b, 2 * c + q:2 * c + q + 1], s_p[:, 2 * b + c, 128 * q:128 + 256 * q], AX.X, ALU.max)
                    link(last)
                    V.tensor_scalar(nmx[:, b, :], mx[:, b, :], -1.0, None, ALU.mult).then_inc(sc_max, 1)
                    low(15 + i)
                    dve.wait_ge(sc_exp, i + 1)
                    link(V.reciprocal(rr[:, b, :], sm[:, b, :]))
                    link(V.tensor_tensor(rr[:, b, :], rr[:, b, :], coef[:, :], ALU.mult))
                    for q in range(2):
                        lo, hi = 128 * q, 128 + 256 * q
                        v = s_p[:, 2 * b, lo:hi]
                        link(V.tensor_scalar(v, v, rr[:, b, q:q + 1], None, ALU.mult))
                        last = V.scalar_tensor_tensor(v, s_p[:, 2 * b + 1, lo:hi], rr[:, b, 2 + q:3 + q], v, ALU.mult, ALU.add)
                        last.then_inc(a_set, 1)
                if 1 <= i < 5:
                    h = i - 1
                    dve.wait_ge(at_ps, h + 1)
                    if h >= 2:
                        dve.wait_ge(pv_ps, h - 1)
                    V.tensor_copy(aT_p[:, h % 2, :], bank[4][:, 0:384]).then_inc(at_set, 1)
                if 4 <= i < 12:
                    s = i - 4
                    b = s % 2
                    dve.wait_ge(ssc_ps, s + 1)
                    if s >= 2:
                        dve.wait_ge(fold_ps, s - 1)
                    V.scalar_tensor_tensor(p_s[:, b, 0:PAST], bank[2 + b][:, 0:PAST], HD ** -0.5, cst[:, C_PAST:C_PAST + PAST], ALU.mult, ALU.add)
                    link(V.scalar_tensor_tensor(p_s[:, b, PAST:320], bank[2 + b][:, PAST:320], HD ** -0.5,
                                                cst[:, C_NEW + 64 * s:C_NEW + 64 * (s + 1)], ALU.mult, ALU.add))
                    link(V.tensor_reduce(msx[:, b:b + 1], p_s[:, b, :], AX.X, ALU.max))
                    V.tensor_scalar(nms[:, b:b + 1], msx[:, b:b + 1], -1.0, None, ALU.mult).then_inc(ssc_max, 1)
                if 5 <= i < 13:
                    s = i - 5
                    dve.wait_ge(fold_ps, s + 1)
                    if s >= 2:
                        dve.wait_ge(spv_ps, s - 1)
                    V.tensor_copy(a_s[:, s % 2, 0:64], bank[4][:, 0:64])
                    V.tensor_copy(a_s[0:64, s % 2, 64:96], bank[4][0:64, 64:96]).then_inc(fold_set, 1)
                if 4 <= i < 12:
                    s = i - 4
                    b = s % 2
                    dve.wait_ge(ssc_exp, s + 1)
                    link(V.reciprocal(rrs[:, b:b + 1], ss[:, b:b + 1]))
                    link(V.tensor_tensor(rrs[:, b:b + 1], rrs[:, b:b + 1], coef_s[:, :], ALU.mult))
                    V.tensor_scalar(p_s[:, b, :], p_s[:, b, :], rrs[:, b:b + 1], None, ALU.mult).then_inc(ss_set, 1)
                if 3 <= i < 11:
                    s = i - 3
                    dve.wait_ge(kt_ps, 2 * s + 2)
                    if s >= 1:
                        dve.wait_ge(ssc_ps, s)
                    V.tensor_copy(k_t[:, :, PAGE:PAST], four(bank[5], P)).then_inc(kt_v, 1)
                if i == 0:
                    for t in range(TILES):
                        dve.wait_ge(v_ps, t + 1)
                        V.tensor_copy(v_tm[0:ROWS[t], t, :], bank[5 + t][0:ROWS[t], :]).then_inc(v_out, 1)
                if i >= 4:
                    low(15 + i)
            def sample_outputs(n):
                dve.wait_ge(ot_ps, n + 1)
                for h in range(H):
                    V.tensor_copy(oT[:, h, PROMPT + 32 * n:PROMPT + 32 * (n + 1)].rearrange("p (s q) -> p s q", s=4),
                                  bank[6 + n][:, :].rearrange("p (s r) -> p s r", s=4)[:, :, 40 * h:40 * h + 8]).then_inc(os_out, 1)

            sample_outputs(0)
            dve.wait_ge(st_ps, 1)
            for g in range(GROUPS):
                last = V.tensor_copy(lvS[0][:, g, :, 0:15], bank[5][:, 120 * g:120 * (g + 1)].rearrange("p (s j) -> p s j", s=SEQS))
            last.then_inc(st_set, 1)
            sample_outputs(1)
            for j in range(29, Z_JOBS):
                low(j)
            dve.wait_ge(z_out, 28)
            for g in range(GROUPS):
                last = V.tensor_copy(u_new[:, g, :].rearrange("p (s j) -> p s j", s=SEQS), lvS[0][:, g, :, 15:23])
            last.then_inc(unew_set, 1)
            for h in range(H):
                dve.wait_ge(std_set, h + 1)
                last = V.reciprocal(rs[:, h, :], rs[:, h, :])
            link(last)
            dve.wait_ge(os_out, 2 * H)
            dve.wait_ge(op_out, 2)
            V.scalar_tensor_tensor(yaT[:], oT[:], gs[:, :], rs[:], ALU.mult, ALU.mult).then_inc(ya_set, 1)
            low(Z_JOBS)
            dve.wait_ge(ko_set, TILES)
            dve.wait_ge(stored, 64)
            for g in range(GROUPS):
                lev = level(g + 1)
                dve.wait_ge(win_set, g + 1)
                V.scalar_tensor_tensor(dT[:, g, 0:PROMPT], lvP[lev][:, g, 15:271], 1.0 / 2 ** (g + 1), lvP[0][:, g, 15:271], ALU.mult, ALU.subtract)
                V.scalar_tensor_tensor(dT[:, g, PROMPT:T].rearrange("p (s j) -> p s j", s=SEQS), lvS[lev][:, g, :, 15:23],
                                       1.0 / 2 ** (g + 1), lvS[0][:, g, :, 15:23], ALU.mult, ALU.subtract).then_inc(d_set, 1)
            for n, r in ((0, 15), (1, 64)):
                dve.wait_ge(u_ps, n + 1)
                V.tensor_copy(u_out[0:r, n, :], bank[2 + n][0:r, :]).then_inc(u_set, 1)
            dve.wait_ge(y_high, 1)
            V.tensor_tensor(ya_low[:], yaT[:], ya_high[:].bitcast(F32), ALU.subtract).then_inc(y_low, 1)
            for g in range(GROUPS):
                dve.wait_ge(y_high, g + 2)
                V.scalar_tensor_tensor(yp_low[:, g, :], bank[4 + g][:, 0:T], col[:, 32 + g:33 + g], yp_high[:, g, :].bitcast(F32),
                                       ALU.mult, ALU.subtract).then_inc(y_low, 1)
            low(Z_JOBS + 1)
            def merged_low(n):
                dve.wait_ge(y_high, 1 + GROUPS + n + 1)
                h = m_high[n // 4]
                V.tensor_tensor(h[:, n % 4, T:T + ROWS[2]], mT[:, n, PROMPT:T], h[:, n % 4, PROMPT:T].bitcast(F32), ALU.subtract)
                V.tensor_tensor(m_low[:, n, 0:PROMPT], mT[:, n, 0:PROMPT], h[:, n % 4, 0:PROMPT].bitcast(F32), ALU.subtract).then_inc(y_low, 1)

            def low_piece(w_low_, w_high_, c, first, before):
                dve.wait_ge(wh_set, before + c + 1)
                V.tensor_tensor(w_low_[:, c], unit(slot_of(first + c), KD), w_high_[:, c].bitcast(F32), ALU.subtract).then_inc(wl_set, 1)

            for n in range(KD):
                if n + 2 < KD:
                    low(Z_JOBS + n + 2)
                dve.wait_ge(br_ps, n + 1)
                if n == 0:
                    dve.wait_ge(z_out, Z_JOBS)
                V.tensor_tensor(gT[:, n, :], gT[:, n, :], bank[n % 2][:, 0:T], ALU.mult)
                V.tensor_tensor(gT[:, 8 + n, :], gT[:, 8 + n, :], bank[2 + n % 2][:, 0:T], ALU.mult).then_inc(br_mul, 1)
                if n > 0:
                    merged_low(n - 1)
            merged_low(KD - 1)
            for c in range(4):
                low_piece(wo_low, wo_high, c, U_WO, Z_JOBS + 2 * KD)
            dve.wait_ge(x2_here, 32)
            def layer_norm(x, t, gamma, beta, n, done):
                r = slice(0, ROWS[t])
                for k in range(2):
                    last = V.bn_stats(stats[r, t, 6 * k:6 * k + 6], x[r, t, 512 * k:512 * (k + 1)])
                link(last)
                link(V.bn_aggr(mv[r, t, :], stats[r, t, 0:12]))
                V.tensor_scalar(rstd[r, t:t + 1], mv[r, t, 1:2], EPS, None, ALU.add).then_inc(var_set, 1)
                v = x[r, t, :]
                link(V.scalar_tensor_tensor(v, v, mv[r, t, 0:1], gamma[r, :], ALU.subtract, ALU.mult))
                dve.wait_ge(sd_set, n)
                link(V.reciprocal(rstd[r, t:t + 1], rstd[r, t:t + 1]))
                V.scalar_tensor_tensor(v, v, rstd[r, t:t + 1], beta[r, :], ALU.mult, ALU.add).then_inc(done, 1)

            def columns(xT_, t, ps, done):
                dve.wait_ge(ps, 2 * t + 1)
                V.tensor_copy(xT_[:, 0:4, P * t:P * t + ROWS[t]], four(bank[2 * t], ROWS[t])).then_inc(done, 1)

            def job_out(j):
                dve.wait_ge(wo_ps, j + 1)
                t, c, b = j // 2, slice(512 * (j % 2), 512 * (j % 2 + 1)), bank[4 + j % 4]
                v = x1[0:ROWS[t], t, c]
                last = V.scalar_tensor_tensor(v, x_again[0:ROWS[t], t, c], ALPHA, b[0:ROWS[t], :], ALU.mult, ALU.add)
                if t == 2:
                    link(last)
                    last = V.tensor_tensor(v, v, b[64:P, :], ALU.add)
                last.then_inc(wo_used, 1)

            def norm1(t):
                dve.wait_ge(wo_used, 2 * t + 2)
                layer_norm(x1, t, ln1[:, 0, :], ln1[:, 1, :], t + 1, x1_set)

            job_out(0)
            job_out(1)
            dve.wait_ge(ln1_here, 32)
            norm1(0)
            job_out(2)
            job_out(3)
            columns(x1T, 0, x1t_ps, x1t_v)
            norm1(1)
            job_out(4)
            job_out(5)
            columns(x1T, 1, x1t_ps, x1t_v)
            norm1(2)
            columns(x1T, 2, x1t_ps, x1t_v)

            def over_last(v, n):
                return v.unsqueeze(2).to_broadcast([P, 3, n])

            def over_tiles(v, n):
                return v.unsqueeze(1).to_broadcast([P, 3, n])

            def first_max(x, n, top, cand, idx):
                link(V.tensor_reduce(top[:, :], x, AX.X, ALU.max))
                link(V.tensor_tensor(cand[:], x, over_last(top, n), ALU.is_lt))
                link(V.scalar_tensor_tensor(cand[:], cand[:], 64.0, over_tiles(iota32[:, 0:n], n), ALU.mult, ALU.add))
                link(V.tensor_reduce(idx[:, :], cand[:], AX.X, ALU.min))

            dve.wait_ge(rt_ps, 1)
            dve.wait_ge(grp_here, 32)
            lp = bank[6][:, 0:108].rearrange("p (t n) -> p t n", t=3)
            V.tensor_tensor(logits[:, 0:2, :], lp[:, 0:2, :], br_row[:, :].unsqueeze(1).to_broadcast([P, 2, 36]), ALU.add)
            link(V.tensor_tensor(logits[0:64, 2, :], lp[0:64, 2, :], br_row[0:64, :], ALU.add))
            lg = logits[:, :, 0:4]
            first_max(lg, 4, m_g, c4, g_id)
            V.tensor_tensor(dl4[:], lg, over_last(m_g, 4), ALU.subtract).then_inc(rt_dl, 1)
            link(V.tensor_tensor(oh4[:], over_tiles(iota32[:, 0:4], 4), over_last(g_id, 4), ALU.is_equal))
            for t in range(TILES):
                last = V.tensor_tensor(le_m[:, t, :].rearrange("p (g e) -> p g e", g=4), logits[:, t, 4:36].rearrange("p (g e) -> p g e", g=4),
                                       oh4[:, t, :].unsqueeze(2).to_broadcast([P, 4, 8]), ALU.mult)
            link(last)
            for t in range(TILES):
                last = V.tensor_reduce(le_s[:, t, :], le_m[:, t, :].rearrange("p (g e) -> p e g", g=4), AX.X, ALU.add)
            link(last)
            first_max(le_s[:], 8, m1, c8a, i1)
            link(V.tensor_tensor(oh8a[:], over_tiles(iota32[:, 0:8], 8), over_last(i1, 8), ALU.is_equal))
            link(V.scalar_tensor_tensor(lt8[:], oh8a[:], -3e38, le_s[:], ALU.mult, ALU.add))
            first_max(lt8[:], 8, m2, c8b, i2)
            V.tensor_tensor(ex[:, :], m2[:, :], m1[:, :], ALU.subtract).then_inc(rt_dl, 1)
            V.scalar_tensor_tensor(e1[:, :], g_id[:, :], 8.0, i1[:, :], ALU.mult, ALU.add)
            link(V.scalar_tensor_tensor(e2[:, :], g_id[:, :], 8.0, i2[:, :], ALU.mult, ALU.add))
            i32 = over_tiles(iota32, 32)
            V.tensor_tensor(E1[:], i32, over_last(e1, 32), ALU.is_equal)
            V.tensor_tensor(E2[:], i32, over_last(e2, 32), ALU.is_equal)
            V.tensor_tensor(GG[:], i32, over_last(e1, 32), ALU.is_gt)
            link(V.tensor_tensor(G2[:], i32, over_last(e2, 32), ALU.is_gt))
            V.tensor_tensor(Mt[:], E1[:], E2[:], ALU.add).then_inc(m_hot, 1)
            V.tensor_tensor(GG[:], GG[:], G2[:], ALU.add).then_inc(m_hot, 1)
            dve.wait_ge(rt_exp, 2)
            link(V.tensor_reduce(s_g[:, :], dl4[:], AX.X, ALU.add))
            link(V.scalar_tensor_tensor(c1[:, :], ex[:, :], 1.0, s_g[:, :], ALU.add, ALU.mult))
            link(V.reciprocal(c1[:, :], c1[:, :]))
            link(V.tensor_tensor(c2[:, :], ex[:, :], c1[:, :], ALU.mult))
            dve.wait_ge(high_set, TILES)
            V.tensor_tensor(x_parts[64:P, 4, :], x1[0:64, 2, :], x_parts[0:64, 4, :].bitcast(F32), ALU.subtract).then_inc(low_set, 1)
            dve.wait_ge(rank_ps, 1)
            rank = bank[7][:, 0:96].rearrange("p (t n) -> p t n", t=3)
            for E, pos in ((E1, pos1), (E2, pos2)):
                V.memset(G2[64:128, 2, :], 0.0)
                link(V.tensor_tensor(G2[:, 0:2, :], E[:, 0:2, :], rank[:, 0:2, :], ALU.mult))
                link(V.tensor_tensor(G2[0:64, 2, :], E[0:64, 2, :], rank[0:64, 2, :], ALU.mult))
                link(V.tensor_reduce(pos[:, :], G2[:], AX.X, ALU.add))
            dve.wait_ge(stored, 16 * 7)
            dve.wait_ge(iota_here, 16)
            for t in range(TILES):
                r = ROWS[t]
                link(V.tensor_scalar(PT[0:r, t, :], iota[0:r, :], pos1[0:r, t:t + 1], None, ALU.is_equal))
                V.scalar_tensor_tensor(PT[0:r, t, :], iota[0:r, :], pos2[0:r, t:t + 1], PT[0:r, t, :].bitcast(F32), ALU.is_equal, ALU.add).then_inc(pt_set, 1)
            dve.wait_ge(pt_set, TILES)
            V.tensor_copy(PT[64:P, 2, :], PT[0:64, 2, :].bitcast(F32)).then_inc(pt_set, 1)
            dve.wait_ge(rank_ps, 2)
            off = bank[6][:, 128:160]
            for w in range(WINDOWS):
                last = V.tensor_scalar(start_f[:, w, 0:32], off, float(WIN * w), float(PAIRS), ALU.add, ALU.min)
            link(last)
            for w in range(1, WINDOWS):
                last = V.memset(start_f[:, w, 32:33], float(PAIRS))
            link(last)
            link(V.tensor_reduce(cnt_max[:, 0:1], bank[6][:, 160:192], AX.X, ALU.max))
            link(V.tensor_scalar(cnt_max[:, 1:2], cnt_max[:, 0:1], float(WIN), None, ALU.is_gt))
            V.tensor_copy(flag[:, 0:1], cnt_max[:, 1:2])
            V.tensor_copy(start_i[:], start_f[:]).then_inc(starts_set, 1)
            for t in range(TILES):
                r = ROWS[t]
                V.tensor_scalar(CT[0:r, t, :], iota[0:r, :], pos1[0:r, t:t + 1], c1[0:r, t:t + 1], ALU.is_equal, ALU.mult)
                link(V.tensor_scalar(weighted[0:r, :], iota[0:r, :], pos2[0:r, t:t + 1], c2[0:r, t:t + 1], ALU.is_equal, ALU.mult))
                V.tensor_tensor(CT[0:r, t, :], CT[0:r, t, :], weighted[0:r, :], ALU.add).then_inc(ct_set, 1)
                dve.wait_ge(ct_set, t + 1)

            def pick(b, place, done):
                V.tensor_copy(xg[:, b, :].rearrange("p (k n) -> p k n", k=KD), XsT[:, :, bass.ds(place, WIN)]).then_inc(done, 1)

            def hidden(q, n, b):
                dve.wait_ge(q["sig"], n)
                V.tensor_tensor(gg[:], b[:, 0:P], sig[:], ALU.mult).then_inc(q["g"], 1)
                dve.wait_ge(q["g"], n)
                V.tensor_tensor(hh[:], gg[:], b[:, P:2 * P], ALU.mult).then_inc(q["h"], 1)

            def put(q, n, b, place):
                dve.wait_ge(q["yt"], n)
                V.tensor_copy(YsT[:, :, bass.ds(place, WIN)].rearrange("p (d c) n -> p c d n", d=2),
                              b[:, :].rearrange("p (c d n) -> p c d n", c=4, d=2)).then_inc(q["out"], 1)
                dve.wait_ge(q["out"], n)

            dve.wait_ge(pads_set, 1)
            dve.wait_ge(ga_out, 16)
            dve.wait_ge(starts_set, 1)
            pick(0, 0, main["xg"])
            for n in range(5):
                dve.wait_ge(ga_ps, 16 + n + 1)
                V.tensor_copy(Pj[:, n, :], bank[PAIR_BANKS[n]][:, 0:T]).then_inc(pj_set, 1)
            pick(1, dve.value_load(start_i[0:1, 0, 1:2], min_val=0, max_val=PAIRS), main["xg"])
            def four_experts(first, place):
                for j in range(4):
                    hidden(main, first + j, bank[j % 2])
                    if j + 3 < len(place):
                        pick(j % 2, place[j + 3], main["xg"])
                    if place[j] is not None:
                        put(main, first + (j - 1), bank[4 + (j + 1) % 2], place[j])

            def place(e):
                return dve.value_load(start_i[0:1, 0, bass.ds(e, 1)], min_val=0, max_val=PAIRS)

            four_experts(1, [None] + [place(e) for e in range(6)])
            with dve.Fori(0, EARLY // 4 - 1) as i:
                four_experts(i * 4 + 5, [place(i * 4 + (3 + j)) for j in range(7)])
            four_experts(EARLY + 1, [place(e) for e in range(EARLY - 1, EXPERTS)])
            put(main, EXPERTS, bank[4 + 1], place(EXPERTS - 1))
            crowded = dve.value_load(flag[0:1, 0:1], min_val=0, max_val=1)
            with dve.If(crowded > 0):
                with dve.Fori(0, EXPERTS) as e:
                    for w in range(WINDOWS):
                        n = e * WINDOWS + (w + 1)
                        place = dve.value_load(start_i[0:1, w, bass.ds(e, 1)], min_val=0, max_val=PAIRS)
                        pick(0, place, over["xg"])
                        hidden(over, n, bank[0])
                        put(over, n, bank[4], place)
            V.memset(scratch[:, 2:3], 0.0).then_inc(moe_done, 1)

            for g in range(0, 10, 2):
                dve.wait_ge(yt_ps, g + 1)
                yt_out(V.tensor_copy, g).then_inc(yt_v, 1)
            dve.wait_ge(late_here, 80)
            def combined(j):
                dve.wait_ge(cm_ps, j + 1)
                for t, p, c in halves(j):
                    last = V.scalar_tensor_tensor(x2[0:ROWS[t], t, c], x1[0:ROWS[t], t, c], ALPHA, bank[6 + j % 2][p, :], ALU.mult, ALU.add)
                last.then_inc(cm_used, 1)

            def low_gate(c):
                low_piece(gw_low, gw_high, c, U_GATE, Z_JOBS + 2 * KD + 4)

            def low_columns(t):
                for g in range(2):
                    dve.wait_ge(x2t_a, 2 * t + g + 1)
                    c = slice(4 * g, 4 * g + 4)
                    dst = x2_low[:, c, P * t:P * (t + 1)] if t < 2 else x2_high[:, c, T:T + ROWS[2]]
                    V.tensor_tensor(dst, four(bank[2 * t + g], ROWS[t]), x2_high[:, c, P * t:P * t + ROWS[t]].bitcast(F32), ALU.subtract).then_inc(x2t_v, 1)

            def norm2(t):
                dve.wait_ge(cm_used, min(2 * t + 2, 5))
                layer_norm(x2, t, ln2[:, 0:D], ln2[:, D:2 * D], TILES + t + 1, x2_set)

            low_gate(0)
            low_gate(1)
            combined(0)
            low_gate(2)
            combined(1)
            norm2(0)
            combined(2)
            low_gate(3)
            combined(3)
            low_columns(0)
            combined(4)
            norm2(1)

            def gates(j):
                dve.wait_ge(pg_ps, j + 1)
                t, c, b = j // 2, slice(512 * (j % 2), 512 * (j % 2 + 1)), bank[7 - j % 2]
                v = gt[0:ROWS[t], t, c]
                last = V.tensor_tensor(v, b[0:ROWS[t], :], bpg[0:ROWS[t], c], ALU.add)
                if t == 2:
                    link(last)
                    last = V.tensor_tensor(v, v, b[64:P, :], ALU.add)
                last.then_inc(pg_add, 1)

            def residual(t):
                for hf in range(2):
                    dve.wait_ge(pg_mul, 2 * t + hf + 1)
                    v = x2[0:ROWS[t], t, 512 * hf:512 * (hf + 1)]
                    last = V.scalar_tensor_tensor(v, v, ALPHA, gt[0:ROWS[t], t, 512 * hf:512 * (hf + 1)], ALU.mult, ALU.add)
                link(last)

            def norm3(t):
                layer_norm(x2, t, ln3[:, 0:D], ln3[:, D:2 * D], 2 * TILES + t + 1, y_set)

            gates(0)
            low_columns(1)
            norm2(2)
            gates(1)
            residual(0)
            norm3(0)
            gates(2)
            low_columns(2)
            gates(3)
            residual(1)
            gates(4)
            norm3(1)
            gates(5)
            residual(2)
            norm3(2)

        @block.tensor
        def _(pe):
            mm = nc.tensor.matmul

            def weights(i):
                pe.wait_ge(w_in_slot[slot_of(i)], 16 * turn_of(i))

            def turn_tile(src, t, ps, ready=None):
                if ready:
                    pe.wait_ge(ready, t + 1)
                r = ROWS[t]
                for g in range(2 * t, 2 * t + 2):
                    for j in range(4):
                        k = 4 * (g % 2) + j
                        last = nc.tensor.transpose(bank[g][:, P * j:P * j + r], src[0:r, t, P * k:P * (k + 1)], ident[0:r, 0:r])
                    last.then_inc(ps, 1)

            def by_parts(b, j, high_, low_, w_high_, w_low_, first):
                t, hf = j // 2, j % 2
                rows = (P * t, P * t + ROWS[t])
                for q0, q1 in ((0, 1), (1, 2)) if j == 0 and first == 0 else ((0, 2),):
                    if t == 0:
                        pe.wait_ge(wh_set, Z_JOBS + 2 * KD + first + 2 * hf + q1)
                    if t < 2:
                        products = [(x, w_high_, k) for k in range(KD) for x in (high_(k, *rows), low_(k, *rows))]
                    else:
                        products = [(high_(k, P * t, T + ROWS[2]), w_high_, k) for k in range(KD)]
                    by_low = [(high_(k, *rows), w_low_, k) for k in range(KD)]
                    products = products[:-1] + by_low + products[-1:]
                    for n, (x, w, k) in enumerate(products):
                        if t == 0 and w is w_low_ and k == 0:
                            pe.wait_ge(wl_set, Z_JOBS + KD + first + 2 * hf + q1)
                        last = mm(b[0:x.shape[1], 256 * q0:256 * q1].rearrange("p (s n) -> p s n", n=256), x,
                                  w[:, 2 * hf + q0:2 * hf + q1, k, :], start=(n == 0), stop=(n == len(products) - 1))
                return last

            pe.wait_ge(ident_here, 16)
            pe.wait_ge(x_here, 32)
            for t in range(TILES):
                turn_tile(x_tm, t, xt_ps)
            pe.wait_ge(vec_here, 7 * 16)
            nc.tensor.transpose(bank[6][:, 0:41], vec[:, :], ident[0:41, 0:41]).then_inc(vec_ps, 1)
            pe.wait_ge(xl_set, 6)

            def z_job(j, halfway=None):
                pe.wait_ge(wl_set, j + 1)
                if j >= 2:
                    pe.wait_ge(z_out, j - 1)
                for k in range(KD):
                    if k == KD // 2 and halfway:
                        halfway()
                    for n, (w, x) in enumerate(((w_high, x_high), (w_high, x_low), (w_low, x_high))):
                        last = mm(bank[j % 2][:, 0:T], w[:, j % 4, k, :], x[:, k, :], start=(k == n == 0), stop=(k == KD - 1 and n == 2))
                last.then_inc(z_ps, 1)

            z_job(0)
            pe.wait_ge(col_set, 2)
            pe.wait_ge(ones_set, 1)
            mm(bank[6][:, 64:66], ones[0:HD, :], lam_p[0:HD, :], start=True, stop=True).then_inc(lam_ps, 1)
            for j in range(1, 9):
                z_job(j)
            pe.wait_ge(z_out, 8)
            for t in range(TILES):
                for h in range(H):
                    last = nc.tensor.transpose(bank[4 + t][0:ROWS[t], P * h:P * (h + 1)], kT[:, h, P * t:P * t + ROWS[t]], ident)
                last.then_inc(ko_ps, 1)
            for j in range(9, 12):
                z_job(j)
            pe.wait_ge(ko_set, TILES)

            def prompt_scores(h):
                if h >= 1:
                    pe.wait_ge(sc_used, 2 * h)
                for c in range(2):
                    r = slice(64 * c, 64 * c + 64)
                    mm(bank[2 + c][:, 0:128], qT[r, h, 0:128], kT[r, h, 0:128], start=True, stop=True)
                    last = mm(bank[2 + c][:, 128:384], qT[r, h, 128:256], kT[r, h, 0:256], start=True, stop=True)
                last.then_inc(sc_ps, 1)

            def prompt_transposes(h):
                pe.wait_ge(a_set, 2 * h + 2)
                if h >= 1:
                    pe.wait_ge(at_set, h)
                for b in range(3):
                    last = nc.tensor.transpose(bank[4][:, P * b:P * (b + 1)], s_p[:, 2 * (h % 2), P * b:P * (b + 1)], ident)
                last.then_inc(at_ps, 1)

            def prompt_values(h):
                pe.wait_ge(at_set, h + 1)
                o = bank[6 + h // 2][:, 256 * (h % 2):256 * (h % 2 + 1)]
                hs = slice(P * h, P * (h + 1))
                A = aT_p[:, h % 2, :]
                mm(o[:, 0:128], v_tm[:, 0, hs], A[:, 0:128], start=True, stop=True)
                mm(o[:, 128:256], v_tm[:, 0, hs], A[:, 128:256], start=True, stop=False)
                mm(o[:, 128:256], v_tm[:, 1, hs], A[:, 256:384], start=False, stop=True).then_inc(pv_ps, 1)

            def keys(s, n):
                if n == 0:
                    pe.wait_ge(k_here[s % 2], 16 * PAGES * (s // 2 + 1))
                    if s >= 1:
                        pe.wait_ge(kt_v, s)
                else:
                    pe.wait_ge(kt_a, s + 1)
                for h in range(H):
                    last = nc.tensor.transpose(bank[5][:, P * h:P * (h + 1)], k_raw[:, s % 2, 512 * n + P * h:512 * n + P * (h + 1)], ident)
                last.then_inc(kt_ps, 1)

            def sample_scores(s):
                pe.wait_ge(kt_a, s + 1)
                pe.wait_ge(kt_v, s + 1)
                if s == 0:
                    pe.wait_ge(qbd_set, 8)
                    pe.wait_ge(sc_used, 8)
                if s >= 2:
                    pe.wait_ge(ssc_max, s - 1)
                for h in range(H):
                    q = qbd[:, s, 32 * h:32 * (h + 1)]
                    o = bank[2 + s % 2][32 * h:32 * (h + 1), :]
                    mm(o[:, 0:PAST], q, k_t[:, h, :], start=True, stop=True, tile_position=(0, 32 * h))
                    last = mm(o[:, PAST:320], q, kT[:, h, PROMPT:T], start=True, stop=True, tile_position=(0, 32 * h))
                last.then_inc(ssc_ps, 1)

            def sample_fold(s):
                pe.wait_ge(ss_set, s + 1)
                if s == 0:
                    pe.wait_ge(at_set, H)
                else:
                    pe.wait_ge(fold_set, s)
                fold = cst[:, C_FOLD:C_FOLD + 32]
                for c in range(2):
                    mm(bank[4][:, 32 * c:32 * (c + 1)], p_s[:, s % 2, P * c:P * (c + 1)], fold, start=True, stop=True)
                mm(bank[4][0:64, 64:96], p_s[:, s % 2, PAST:320], fold, start=True, stop=True).then_inc(fold_ps, 1)

            def sample_values(s):
                pe.wait_ge(fold_set, s + 1)
                pe.wait_ge(v_here[s % 2], 16 * PAGES * (s // 2 + 1))
                if s % 4 == 0:
                    pe.wait_ge(op_out, s // 4 + 1)
                for n in range(PAGES + 1):
                    for h in range(H):
                        o = bank[6 + s // 4][32 * h:32 * (h + 1), P * (s % 4):P * (s % 4 + 1)]
                        if n < PAGES:
                            mm(o, a_s[:, s % 2, 32 * n:32 * (n + 1)], v_raw[:, s % 2, 512 * n + P * h:512 * n + P * (h + 1)],
                               start=(n == 0), stop=False, tile_position=(0, 32 * h))
                        else:
                            last = mm(o, a_s[0:64, s % 2, 64:96], v_tm[0:64, 2, P * h:P * (h + 1)], start=False, stop=True,
                                      tile_position=(0, 32 * h))
                last.then_inc(spv_ps, 1)

            def turn_outputs(n):
                pe.wait_ge(or_set, n + 1)
                for q in range(4):
                    last = nc.tensor.transpose(bank[6 + n][:, P * q:P * (q + 1)], os_raw[:, n, P * q:P * (q + 1)], ident)
                last.then_inc(ot_ps, 1)

            pe.wait_ge(cst_here, 16)
            for i in range(14):
                if i < 4:
                    prompt_scores(i)
                if 2 <= i < 6:
                    prompt_values(i - 2)
                if 1 <= i < 5:
                    prompt_transposes(i - 1)
                if 4 <= i < 12:
                    sample_scores(i - 4)
                if 6 <= i:
                    sample_values(i - 6)
                if 5 <= i < 13:
                    sample_fold(i - 5)
                if 3 <= i < 11:
                    keys(i - 3, 0)
                if i < 12:
                    z_job(12 + i, (lambda: keys(i - 3, 1)) if 3 <= i < 11 else None)
                if i == 0:
                    pe.wait_ge(z_out, 12)
                    for t in range(TILES):
                        for h in range(H):
                            last = nc.tensor.transpose(bank[5 + t][0:ROWS[t], P * h:P * (h + 1)], vT[:, h, P * t:P * t + ROWS[t]], ident)
                        last.then_inc(v_ps, 1)
                if i == 1:
                    pe.wait_ge(v_out, TILES)

            turn_outputs(0)
            pe.wait_ge(state_here, 16)
            pe.wait_ge(kt_v, SEQS)
            for g in range(GROUPS):
                last = nc.tensor.transpose(bank[5][:, 120 * g:120 * (g + 1)], state[0:120, P * g:P * (g + 1)], ident[0:120, 0:120])
            last.then_inc(st_ps, 1)
            z_job(24)
            turn_outputs(1)
            for j in range(25, 28):
                z_job(j)
            pe.wait_ge(sq_set, 1)
            pe.wait_ge(st_set, 1)
            pe.wait_ge(ssc_max, SEQS)
            pe.wait_ge(fold_set, SEQS)
            pe.wait_ge(kt_v, SEQS)
            for h in range(H):
                mm(bank[2 + h][:, 0:T], ones[:, :], sq[:, h, :], start=True, stop=True).then_inc(ms_ps, 1)
            for j in range(28, Z_JOBS):
                z_job(j)
            pe.wait_ge(std_set, H)
            pe.wait_ge(unew_set, 1)
            for g in range(GROUPS):
                last = nc.tensor.transpose(bank[2][0:15, P * g:P * (g + 1)], lvP[0][:, g, 256:271], ident)
            last.then_inc(u_ps, 1)
            for g in range(GROUPS):
                last = nc.tensor.transpose(bank[3][0:64, P * g:P * (g + 1)], u_new[:, g, :], ident)
            last.then_inc(u_ps, 1)
            pe.wait_ge(wgrp_here, 16)
            pe.wait_ge(st_set, 1)
            for g in range(GROUPS):
                pe.wait_ge(d_set, g + 1)
                mm(bank[4 + g][:, 0:T], w_grp[:, g, :], dT[:, g, :], start=True, stop=True).then_inc(yp_ps, 1)

            pe.wait_ge(u_set, 2)
            pe.wait_ge(y_low, GROUPS + 1)
            pe.wait_ge(z_out, Z_JOBS)
            for n in range(KD):
                j = Z_JOBS + n
                pe.wait_ge(wl_set, j + 1)
                if n >= 2:
                    pe.wait_ge(br_mul, n - 1)
                for w, (y_h, y_l) in enumerate(((yp_high, yp_low), (ya_high, ya_low))):
                    for k in range(4):
                        for m, (wp, yp_) in enumerate(((w_high, y_h), (w_high, y_l), (w_low, y_h))):
                            last = mm(bank[2 * w + n % 2][:, 0:T], wp[:, j % 4, 4 * w + k, :], yp_[:, k, :],
                                      start=(k == m == 0), stop=(k == 3 and m == 2))
                last.then_inc(br_ps, 1)
            pe.wait_ge(y_high, 1 + GROUPS + KD)
            pe.wait_ge(y_low, 1 + GROUPS + KD)
            for j in range(6):
                if j >= 4:
                    pe.wait_ge(wo_used, j - 3)
                if j == 4:
                    turn_tile(x1, 0, x1t_ps, x1_set)
                by_parts(bank[4 + j % 4], j, lambda k, c0, c1: m_high[k // 4][:, k % 4, c0:c1], lambda k, c0, c1: m_low[:, k, c0:c1],
                         wo_high, wo_low, 0).then_inc(wo_ps, 1)
            pe.wait_ge(wr_here, 32)
            for t in range(TILES):
                if t > 0:
                    turn_tile(x1, t, x1t_ps, x1_set)
                pe.wait_ge(x1t_v, t + 1)
                pe.wait_ge(x1t_a, t + 1)
                for k in range(KD):
                    last = mm(bank[6][0:ROWS[t], 36 * t:36 * (t + 1)], x1T[:, k, P * t:P * t + ROWS[t]], w_r[:, k, :],
                              start=(k == 0), stop=(k == KD - 1))
            last.then_inc(rt_ps, 1)
            pe.wait_ge(ple_here, 32)
            for t in range(TILES):
                r = ROWS[t]
                for k in range(2):
                    last = nc.tensor.transpose(bank[t][:, P * k:P * k + r], p_tm[0:r, t, P * k:P * (k + 1)], ident[0:r, 0:r])
                last.then_inc(pt_ps, 1)
            pe.wait_ge(m_hot, 2)
            b = bank[7]
            def starts(u, start, stop):
                return mm(b[:, 0:96].rearrange("p (c n) -> p c n", c=3), ones[0:ROWS[u], :], GG[0:ROWS[u], u, :].unsqueeze(1).to_broadcast([ROWS[u], 3, 32]),
                          start=start, stop=stop)

            starts(0, True, False)
            starts(1, False, False)
            for u in range(TILES - 1):
                mm(b[:, 32 * (u + 1):96].rearrange("p (c n) -> p c n", n=32), ones[0:ROWS[u], :],
                   Mt[0:ROWS[u], u, :].unsqueeze(1).to_broadcast([ROWS[u], 2 - u, 32]), start=False, stop=False)
            for t in range(TILES):
                r = ROWS[t]
                mm(b[0:r, 32 * t:32 * (t + 1)], tri[0:r, 0:r], Mt[0:r, t, :], start=False, stop=False)
            starts(2, False, True).then_inc(rank_ps, 1)
            for o, X in ((128, GG), (160, Mt)):
                for u in range(TILES):
                    last = mm(bank[6][:, o:o + 32], ones[0:ROWS[u], :], X[0:ROWS[u], u, :], start=(u == 0), stop=(u == TILES - 1))
            last.then_inc(rank_ps, 1)
            pe.wait_ge(pt_out, TILES)
            pe.wait_ge(high_set, TILES)
            pe.wait_ge(low_set, TILES)
            def gather(j, parts, t):
                for part in parts:
                    last = mm(bank[j % 6][:, 0:320], x_parts[:, part, P * (j // 2):P * (j // 2 + 1)], PT[:, t, 320 * (j % 2):320 * (j % 2 + 1)],
                              start=(part == 0), stop=(part == 4))
                return last

            for parts, t, permutation in (((0, 2), 0, 1), ((1, 3), 1, 2), ((4,), 2, 4)):
                pe.wait_ge(pt_set, permutation)
                for j in range(6):
                    last = gather(j, parts, t)
                    if t == 2:
                        last.then_inc(ga_ps, 1)
            for j in range(6, 16):
                pe.wait_ge(ga_out, j - 5)
                gather(j, (0, 2), 0)
                gather(j, (1, 3), 1)
                gather(j, (4,), 2).then_inc(ga_ps, 1)
            pe.wait_ge(starts_set, 1)
            pe.wait_ge(ct_set, TILES)
            pe.wait_ge(ga_out, 12)
            for n in range(5):
                if n == 3:
                    pe.wait_ge(ga_out, 16)
                for t in range(TILES):
                    r = ROWS[t]
                    last = nc.tensor.transpose(bank[PAIR_BANKS[n]][:, P * t:P * t + r], CT[0:r, t, P * n:P * (n + 1)], ident[0:r, 0:r])
                last.then_inc(ga_ps, 1)

            def gate_up(q, slot, x, b, halfway=None):
                w = ring[:, slot:slot + 2, :].rearrange("p s (k n) -> p s k n", k=KD)
                for k in range(KD):
                    if k == KD // 2 and halfway:
                        halfway()
                    for f in range(2):
                        last = mm(b[WIN * f:WIN * (f + 1), 0:256].rearrange("p (s n) -> p s n", s=2), x[:, WIN * k:WIN * (k + 1)],
                                  w[:, :, k, P * f:P * (f + 1)], start=(k == 0), stop=(k == KD - 1), tile_position=(0, WIN * f))
                last.then_inc(q["gu"], 1)

            def turn_hidden(q, n):
                if isinstance(n, int) and n == 1:
                    pe.wait_ge(pj_set, 5)
                pe.wait_ge(q["h"], n)
                nc.tensor.transpose(bank[2][:, 0:P], hh[:], ident).then_inc(q["ht"], 1)

            def down(q, n, slot):
                pe.wait_ge(q["hT"], n)
                for f in range(2):
                    for d in range(2):
                        last = mm(bank[3][WIN * d:WIN * (d + 1), :], hT[:, WIN * f:WIN * (f + 1)],
                                  unit(slot, 2)[:, f, 512 * d:512 * (d + 1)], start=(f == 0), stop=(f == 1), tile_position=(0, WIN * d))
                last.then_inc(q["y"], 1)

            def turn_result(q, n, b):
                pe.wait_ge(q["ys"], n)
                for c in range(4):
                    last = nc.tensor.transpose(b[:, P * c:P * (c + 1)], y_s[:, P * c:P * (c + 1)], ident)
                last.then_inc(q["yt"], 1)

            def four_experts(first, slots, here, behind=(2, 2, 2, 2)):
                for j in range(4):
                    pe.wait_ge(main["xg"], first + j)
                    here(j, 0)
                    here(j, 1)
                    gate_up(main, slots[3 * j], xg[:, j % 2, :], bank[j % 2],
                            (lambda: turn_hidden(main, first + (j - 1))) if behind[j] > 0 else None)
                    if behind[j] > 1:
                        turn_result(main, first + (j - 2), bank[4 + j % 2])
                    if behind[j] > 0:
                        here(j - 1, 2)
                        down(main, first + (j - 1), slots[3 * j - 1])

            def in_turn(more):
                def here(j, r):
                    slot = 3 * j + r if j >= 0 else RING - 1
                    pe.wait_ge(w_in_slot[slot], more + 16 * (turn_of(U_EXPERT + slot) - (j < 0)))
                return here

            def late(j, r):
                weights(U_LATE + 3 * j + r if j >= 0 else U_PLE - 1)

            four_experts(1, list(range(RING)), in_turn(0), (0, 1, 2, 2))
            with pe.Fori(0, EARLY // 4 - 1) as i:
                four_experts(i * 4 + 5, list(range(RING)), in_turn(i * 16 + 16))
            weights(U_PLE)
            pe.wait_ge(starts_set, 1)
            for j in range(5):
                t = j // 2
                if j >= 2:
                    pe.wait_ge(pe_out, j - 1)
                for k in range(2):
                    for hf in ((j % 2,) if t < 2 else (0, 1)):
                        p0 = 64 * hf if t == 2 else 0
                        last = mm(bank[6 + j % 2][p0:p0 + ROWS[t], :], pT[:, k, P * t:P * t + ROWS[t]],
                                  unit(U_PLE % RING, 2)[:, k, 512 * hf:512 * (hf + 1)], start=(k == 0), stop=(k == 1), tile_position=(0, p0))
                last.then_inc(pe_ps, 1)
            four_experts(EARLY + 1, [(U_LATE + n) % RING for n in range(11)] + [(U_PLE - 1) % RING], late)
            turn_hidden(main, EXPERTS)
            turn_result(main, EXPERTS - 1, bank[4])
            weights(U_LATE + 11)
            down(main, EXPERTS, (U_LATE + 11) % RING)
            turn_result(main, EXPERTS, bank[5])
            pe.wait_ge(starts_set, 1)
            crowded = pe.value_load(flag[0:1, 0:1], min_val=0, max_val=1)
            with pe.If(crowded > 0):
                pe.wait_ge(main["out"], EXPERTS)
                pe.sem_inc(over["freed"], 1)
                with pe.Fori(0, EXPERTS) as e:
                    pe.wait_ge(over["w"], e * 48 + 48)
                    for w in range(WINDOWS):
                        n = e * WINDOWS + (w + 1)
                        pe.wait_ge(over["xg"], n)
                        gate_up(over, 9, xg[:, 0, :], bank[0])
                        turn_hidden(over, n)
                        down(over, n, 11)
                        turn_result(over, n, bank[4])
                    pe.sem_inc(over["freed"], 1)

            pe.wait_ge(moe_done, 1)
            for g in range(10):
                if g >= 6:
                    m = g - 6
                    pe.wait_ge(yt_v if m % 2 == 0 else yt_a, m // 2 + 1)
                for j in range(4):
                    k = 4 * (g % 2) + j
                    last = nc.tensor.transpose(bank[g % 6][:, P * j:P * (j + 1)], YsT[:, k, P * (g // 2):P * (g // 2 + 1)], ident)
                last.then_inc(yt_ps, 1)
            pe.wait_ge(yt_v, 5)
            pe.wait_ge(yt_a, 5)
            pe.wait_ge(pe_out, 6)
            for j in range(5):
                t = j // 2
                if j >= 2:
                    pe.wait_ge(cm_used, j - 1)
                for n in range(5):
                    for hf in ((j % 2,) if t < 2 else (0, 1)):
                        p0 = 64 * hf if t == 2 else 0
                        last = mm(bank[6 + j % 2][p0:p0 + ROWS[t], :], Pj[:, n, P * t:P * t + ROWS[t]], Yj[:, n, 512 * hf:512 * (hf + 1)],
                                  start=(n == 0), stop=(n == 4), tile_position=(0, p0))
                last.then_inc(cm_ps, 1)
                if j == 3:
                    turn_tile(x2, 0, x2t_ps, x2_set)
            for j in range(6):
                t = j // 2
                if j in (1, 3):
                    turn_tile(x2, (j + 1) // 2, x2t_ps, x2_set)
                pe.wait_ge(x2t_a, 2 * t + 2)
                pe.wait_ge(x2t_v, 2 * t + 2)
                if j < 2:
                    pe.wait_ge(cm_used, 4 + j)
                else:
                    pe.wait_ge(pg_add, j - 1)
                by_parts(bank[7 - j % 2], j, lambda k, c0, c1: x2_high[:, k, c0:c1], lambda k, c0, c1: x2_low[:, k, c0:c1],
                         gw_high, gw_low, 4).then_inc(pg_ps, 1)


_INS = ['x_prompt', 'x_sample', 'p_prompt', 'p_sample', 'cache_k', 'cache_v', 'state_pool', 'page_table', 'w_in', 'b_in',
        'lam_q1', 'lam_k1', 'lam_q2', 'lam_k2', 'g_sub', 'w_pool_grp', 's_pool', 'w_pool_br', 'w_attn_br', 'w_o', 'ln1_g',
        'ln1_b', 'w_rg', 'b_rg', 'w_re', 'b_re', 'w_gate', 'w_up', 'w_down', 'ln2_g', 'ln2_b', 'w_ple_gate', 'b_ple_gate',
        'w_ple', 'ln3_g', 'ln3_b']
_OUTS = [('y_prompt', (1, 256, 1024)), ('y_sample', (8, 8, 1024)), ('new_k_prompt', (1, 1, 256, 4, 128)),
         ('new_v_prompt', (1, 1, 256, 4, 128)), ('new_pool_prompt', (1, 1, 15, 512)), ('new_k_sample', (1, 8, 8, 4, 128)),
         ('new_v_sample', (1, 8, 8, 4, 128)), ('new_pool_sample', (1, 8, 15, 512))]


def kernel(**inputs):
    import numpy as _np
    import concourse.bacc as _bacc
    from concourse import mybir as _mybir
    from concourse.bass_utils import run_bass_kernel_spmd as _run

    nc = _bacc.Bacc("TRN2", target_bir_lowering=False, num_devices=1)
    arrays, args = {}, {}
    cst, iota = constant_tables()
    named = {n: _np.ascontiguousarray(inputs[n]) for n in _INS}
    named["cst"], named["iota"] = cst, iota
    for name, arr in named.items():
        arrays[f"in_{name}_dram"] = arr
        args[name] = nc.dram_tensor(f"in_{name}_dram", arr.shape, _mybir.dt.from_np(arr.dtype), kind="ExternalInput").ap()
    for name, shape in _OUTS:
        args[name] = nc.dram_tensor(f"out_{name}_dram", shape, F32, kind="ExternalOutput").ap()
    hybrid_step(nc, args)
    r = _run(nc, [arrays], core_ids=[0])
    return tuple(r.results[0][f"out_{name}_dram"] for name, _ in _OUTS)
```
